# Optimizing a Trainium2 kernel written in Bass

```python
import math
import jax, jax.numpy as jnp
from jax import lax
import numpy as np

D_MODEL = 1024
BATCH = 1
SEQ = 256
DEPTH = 2

CONV_WIDTH = 512
CONV_K = 3
SSM_WIDTH = 512
SSM_GROUP = 16
SSM_GROUPS = SSM_WIDTH // SSM_GROUP
SSM_STATE = 64
DT_MIN = 0.001
DT_MAX = 0.1
ATTN_HEADS = 8
HEAD_DIM = 64
ATTN_WIDTH = ATTN_HEADS * HEAD_DIM
IDX_HEADS = 4
IDX_DIM = 64
TOPK_MAX = 256
Q_BLOCK = 128
ROPE_THETA = 10000.0
N_BRANCH = 3
D_FF_DENSE = 2816
N_EXPERTS = 8
TOP_K_EXPERTS = 2
D_FF_EXPERT = 3584
N_DENSE_LAYERS = (DEPTH + 1) // 2
N_MOE_LAYERS = DEPTH // 2
EPS = 1e-6

IN_SIZES = (CONV_WIDTH, CONV_WIDTH, CONV_WIDTH, SSM_WIDTH, ATTN_WIDTH, HEAD_DIM, HEAD_DIM,
            IDX_HEADS * IDX_DIM, IDX_DIM, IDX_HEADS, N_BRANCH * D_MODEL)
IN_COLS = sum(IN_SIZES)

kernel_name = "hybrid_conv_s5_dsa_moe_block"

def rmsnorm(x, g):
    xf = x.astype(jnp.float32)
    y = xf * lax.rsqrt(jnp.mean(xf * xf, axis=-1, keepdims=True) + EPS)
    return (y * g.astype(jnp.float32)).astype(x.dtype)

def split_columns(p):
    bounds = []
    acc = 0
    for s in IN_SIZES[:-1]:
        acc += s
        bounds.append(acc)
    return jnp.split(p, bounds, axis=-1)

def rope_tables(L, dim):
    pos = jnp.arange(L, dtype=jnp.float32)
    inv = ROPE_THETA ** (-jnp.arange(dim // 2, dtype=jnp.float32) / (dim // 2))
    ang = pos[:, None] * inv[None, :]
    return jnp.cos(ang)[:, None, :], jnp.sin(ang)[:, None, :]

def rope(x, cos, sin):
    xf = x.astype(jnp.float32)
    x1, x2 = jnp.split(xf, 2, axis=-1)
    return jnp.concatenate([x1 * cos - x2 * sin, x2 * cos + x1 * sin], axis=-1).astype(x.dtype)

def short_conv_mixer(u, b_gate, c_gate, conv_w):
    v = c_gate * u
    y = lax.conv_general_dilated(v, conv_w[:, None, :].astype(v.dtype), window_strides=(1,),
                                 padding=[(CONV_K - 1, 0)],
                                 dimension_numbers=("NWC", "WIO", "NWC"),
                                 feature_group_count=CONV_WIDTH)
    return b_gate * y

def s5_mixer(u, lam_re, lam_im, log_dt, b_re, b_im, c_re, c_im, d_skip, w_glu):
    f32 = jnp.float32
    Bsz, L, _ = u.shape
    uf = u.astype(f32)
    ug = uf.reshape(Bsz, L, SSM_GROUPS, SSM_GROUP)
    lr = jnp.minimum(lam_re.astype(f32), -1e-4)
    li = lam_im.astype(f32)
    dt = jnp.exp(log_dt.astype(f32))[:, None]
    mag = jnp.exp(lr * dt)
    ang = li * dt
    ab_re = mag * jnp.cos(ang)
    ab_im = mag * jnp.sin(ang)
    nr = ab_re - 1.0
    ni = ab_im
    den = lr * lr + li * li
    coef_re = (nr * lr + ni * li) / den
    coef_im = (ni * lr - nr * li) / den
    bu_re = jnp.einsum('blgh,gph->blgp', ug, b_re.astype(f32))
    bu_im = jnp.einsum('blgh,gph->blgp', ug, b_im.astype(f32))
    x_re = coef_re * bu_re - coef_im * bu_im
    x_im = coef_re * bu_im + coef_im * bu_re
    a_re = jnp.broadcast_to(ab_re[None, None], (1, L, SSM_GROUPS, SSM_STATE))
    a_im = jnp.broadcast_to(ab_im[None, None], (1, L, SSM_GROUPS, SSM_STATE))

    def combine(e1, e2):
        a1r, a1i, b1r, b1i = e1
        a2r, a2i, b2r, b2i = e2
        return (a2r * a1r - a2i * a1i,
                a2r * a1i + a2i * a1r,
                a2r * b1r - a2i * b1i + b2r,
                a2r * b1i + a2i * b1r + b2i)

    _, _, h_re, h_im = lax.associative_scan(combine, (a_re, a_im, x_re, x_im), axis=1)
    y = (jnp.einsum('blgp,ghp->blgh', h_re, c_re.astype(f32))
         - jnp.einsum('blgp,ghp->blgh', h_im, c_im.astype(f32)))
    y = y.reshape(Bsz, L, SSM_WIDTH) + d_skip.astype(f32) * uf
    y = jax.nn.gelu(y)
    y = y * jax.nn.sigmoid(y @ w_glu.astype(f32))
    return y.astype(u.dtype)

def dsa_mixer(q, k, v, q_idx, k_idx, w_idx, q_gain, k_gain, cos, sin):
    f32 = jnp.float32
    Bsz, L = q.shape[0], q.shape[1]
    topk = min(TOPK_MAX, L // 4)
    q = rope(rmsnorm(q, q_gain), cos, sin).astype(f32)
    k = rope(rmsnorm(k[:, :, None, :], k_gain), cos, sin)[:, :, 0].astype(f32)
    vf = v.astype(f32)
    qi = rope(q_idx, cos, sin).astype(f32)
    ki = rope(k_idx[:, :, None, :], cos, sin)[:, :, 0].astype(f32)
    wi = w_idx.astype(f32) * (IDX_HEADS ** -0.5)
    scale = HEAD_DIM ** -0.5
    key_pos = jnp.arange(L)
    gather = jax.vmap(lambda arr, idx: arr[idx])

    def block(i):
        s0 = i * Q_BLOCK
        qb = lax.dynamic_slice_in_dim(q, s0, Q_BLOCK, axis=1)
        qib = lax.dynamic_slice_in_dim(qi, s0, Q_BLOCK, axis=1)
        wib = lax.dynamic_slice_in_dim(wi, s0, Q_BLOCK, axis=1)
        t = s0 + jnp.arange(Q_BLOCK)
        rel = jax.nn.relu(jnp.einsum('bthd,bsd->bths', qib, ki))
        score = jnp.einsum('bths,bth->bts', rel, wib)
        causal = key_pos[None, :] <= t[:, None]
        score = jnp.where(causal[None], score, -jnp.inf)
        _, sel = lax.top_k(score, topk)
        valid = sel <= t[None, :, None]
        kg = gather(k, sel)
        vg = gather(vf, sel)
        logits = jnp.einsum('bthd,btkd->bthk', qb, kg) * scale
        logits = jnp.where(valid[:, :, None, :], logits, -jnp.inf)
        p = jax.nn.softmax(logits, axis=-1)
        return jnp.einsum('bthk,btkd->bthd', p, vg)

    out = lax.map(block, jnp.arange(L // Q_BLOCK))
    out = jnp.transpose(out, (1, 0, 2, 3, 4)).reshape(Bsz, L, ATTN_WIDTH)
    return out.astype(v.dtype)

def swiglu(h, w1, w3, w2):
    return (jax.nn.silu(h @ w1) * (h @ w3)) @ w2

def moe_ffn(h, router_w, w1, w3, w2):
    logits = (h @ router_w).astype(jnp.float32)
    vals, idx = lax.top_k(logits, TOP_K_EXPERTS)
    probs = jax.nn.softmax(vals, axis=-1)
    gate = jnp.sum(jax.nn.one_hot(idx, N_EXPERTS, dtype=jnp.float32) * probs[..., None], axis=-2)
    gate = gate.astype(h.dtype)
    out = jnp.zeros_like(h)
    for e in range(N_EXPERTS):
        out = out + gate[..., e:e + 1] * swiglu(h, w1[e], w3[e], w2[e])
    return out

def setup_inputs(seed: int = 0) -> dict:
    key = jax.random.key(seed)
    ks = jax.random.split(key, 32)
    nrm = jax.random.normal
    f32 = jnp.float32
    D = D_MODEL
    G, P, H16 = SSM_GROUPS, SSM_STATE, SSM_GROUP
    n_idx = jnp.arange(P, dtype=f32)
    inp = {}
    inp["x"] = nrm(ks[0], (BATCH, SEQ, D), f32)
    inp["ln1_g"] = 1.0 + 0.02 * nrm(ks[1], (DEPTH, D), f32)
    inp["w_in"] = nrm(ks[2], (DEPTH, D, IN_COLS), f32) * D ** -0.5
    inp["conv_w"] = nrm(ks[3], (DEPTH, CONV_K, CONV_WIDTH), f32) * CONV_K ** -0.5
    inp["ssm_lam_re"] = -0.5 + 0.01 * nrm(ks[4], (DEPTH, G, P), f32)
    inp["ssm_lam_im"] = math.pi * n_idx[None, None, :] + 0.01 * nrm(ks[5], (DEPTH, G, P), f32)
    inp["ssm_log_dt"] = jax.random.uniform(ks[6], (DEPTH, G), f32, math.log(DT_MIN), math.log(DT_MAX))
    inp["ssm_b_re"] = nrm(ks[7], (DEPTH, G, P, H16), f32) * (2.0 * H16) ** -0.5
    inp["ssm_b_im"] = nrm(ks[8], (DEPTH, G, P, H16), f32) * (2.0 * H16) ** -0.5
    inp["ssm_c_re"] = nrm(ks[9], (DEPTH, G, H16, P), f32) * (2.0 * P) ** -0.5
    inp["ssm_c_im"] = nrm(ks[10], (DEPTH, G, H16, P), f32) * (2.0 * P) ** -0.5
    inp["ssm_d"] = nrm(ks[11], (DEPTH, SSM_WIDTH), f32)
    inp["ssm_w_glu"] = nrm(ks[12], (DEPTH, SSM_WIDTH, SSM_WIDTH), f32) * SSM_WIDTH ** -0.5
    inp["q_norm_g"] = 1.0 + 0.02 * nrm(ks[13], (DEPTH, HEAD_DIM), f32)
    inp["k_norm_g"] = 1.0 + 0.02 * nrm(ks[14], (DEPTH, HEAD_DIM), f32)
    inp["w_out_a"] = nrm(ks[15], (DEPTH, CONV_WIDTH, D), f32) * CONV_WIDTH ** -0.5
    inp["w_out_b"] = nrm(ks[16], (DEPTH, SSM_WIDTH, D), f32) * SSM_WIDTH ** -0.5
    inp["w_out_c"] = nrm(ks[17], (DEPTH, ATTN_WIDTH, D), f32) * ATTN_WIDTH ** -0.5
    inp["w_o"] = nrm(ks[18], (DEPTH, D, D), f32) * D ** -0.5
    inp["ln2_g"] = 1.0 + 0.02 * nrm(ks[19], (DEPTH, D), f32)
    inp["ffn_w1"] = nrm(ks[20], (N_DENSE_LAYERS, D, D_FF_DENSE), f32) * D ** -0.5
    inp["ffn_w3"] = nrm(ks[21], (N_DENSE_LAYERS, D, D_FF_DENSE), f32) * D ** -0.5
    inp["ffn_w2"] = nrm(ks[22], (N_DENSE_LAYERS, D_FF_DENSE, D), f32) * D_FF_DENSE ** -0.5
    inp["router_w"] = nrm(ks[23], (N_MOE_LAYERS, D, N_EXPERTS), f32) * D ** -0.5
    inp["moe_w1"] = nrm(ks[24], (N_MOE_LAYERS, N_EXPERTS, D, D_FF_EXPERT), f32) * D ** -0.5
    inp["moe_w3"] = nrm(ks[25], (N_MOE_LAYERS, N_EXPERTS, D, D_FF_EXPERT), f32) * D ** -0.5
    inp["moe_w2"] = nrm(ks[26], (N_MOE_LAYERS, N_EXPERTS, D_FF_EXPERT, D), f32) * D_FF_EXPERT ** -0.5
    return inp

def reference(x, ln1_g, w_in, conv_w, ssm_lam_re, ssm_lam_im, ssm_log_dt, ssm_b_re, ssm_b_im,
              ssm_c_re, ssm_c_im, ssm_d, ssm_w_glu, q_norm_g, k_norm_g, w_out_a, w_out_b, w_out_c,
              w_o, ln2_g, ffn_w1, ffn_w3, ffn_w2, router_w, moe_w1, moe_w3, moe_w2):
    Bsz, L, _ = x.shape
    cos, sin = rope_tables(L, HEAD_DIM)
    for layer in range(DEPTH):
        h = rmsnorm(x, ln1_g[layer])
        proj = h @ w_in[layer]
        a_u, a_b, a_c, s_u, q, k, v, qi, ki, wi, gates = split_columns(proj)
        y_a = short_conv_mixer(a_u, a_b, a_c, conv_w[layer]) @ w_out_a[layer]
        y_b = s5_mixer(s_u, ssm_lam_re[layer], ssm_lam_im[layer], ssm_log_dt[layer],
                       ssm_b_re[layer], ssm_b_im[layer], ssm_c_re[layer], ssm_c_im[layer],
                       ssm_d[layer], ssm_w_glu[layer]) @ w_out_b[layer]
        y_c = dsa_mixer(q.reshape(Bsz, L, ATTN_HEADS, HEAD_DIM), k, v,
                        qi.reshape(Bsz, L, IDX_HEADS, IDX_DIM), ki, wi,
                        q_norm_g[layer], k_norm_g[layer], cos, sin) @ w_out_c[layer]
        g = jax.nn.sigmoid(gates.reshape(Bsz, L, N_BRANCH, D_MODEL))
        mixed = g[:, :, 0] * y_a + g[:, :, 1] * y_b + g[:, :, 2] * y_c
        x = x + mixed @ w_o[layer]
        h2 = rmsnorm(x, ln2_g[layer])
        if layer % 2 == 0:
            j = layer // 2
            x = x + swiglu(h2, ffn_w1[j], ffn_w3[j], ffn_w2[j])
        else:
            j = layer // 2
            x = x + moe_ffn(h2, router_w[j], moe_w1[j], moe_w3[j], moe_w2[j])
    return x


_drawn_inputs = setup_inputs


def setup_inputs(seed=0):
    import zlib

    import numpy as np

    out = dict(_drawn_inputs(seed))
    spreads = {}
    factors = {'ssm_lam_re': 8.0, 'ssm_c_re': 2.989, 'q_norm_g': 3.751, 'k_norm_g': 5.092}
    for name, (base, spread) in spreads.items():
        noise = np.random.default_rng([zlib.crc32(name.encode()), seed]).standard_normal(out[name].shape)
        drawn = base * np.exp(spread * noise) if base else spread * noise
        out[name] = __import__('jax').numpy.asarray(drawn.astype(out[name].dtype))
    for name, factor in factors.items():
        out[name] = (out[name] * factor).astype(out[name].dtype)
    return out
```

```python
from contextlib import ExitStack

import numpy as np
import concourse.bass as bass
from concourse import mybir

ALU = mybir.AluOpType
ACT = mybir.ActivationFunctionType
F32 = mybir.dt.float32
F32R = mybir.dt.float32r
I32 = mybir.dt.int32
AX_X = mybir.AxisListType.X

P = 128
D = 1024
SEQ = 256
BLOCKS = SEQ // P
DEPTH = 2
KD = D // P
CONV = 512
SSM = 512
CT = CONV // P
GROUP = 16
STATE = 64
SCHUNKS = (SSM // GROUP) * STATE // P
HEADS = 8
HD = 64
IDX_HEADS = 4
TOPK = min(256, SEQ // 4)
FF_DENSE = 2816
EXPERTS = 8
FF_EXPERT = 3584
EPS = 1e-6
SLOTS = P
NEG = -1e30
DEAD = -3e38
HALF = 512

CHUNK = 2048
RAW = 6
SPLIT = 3
DENSE_W = 256
DENSE_STRIPES = FF_DENSE // DENSE_W
MOE_STRIPES = FF_EXPERT // HALF
MIX_CHUNKS = 35
DENSE_CHUNKS = 3 * DENSE_STRIPES
MOE_CHUNKS = 6 * MOE_STRIPES
MIX0 = [0, MIX_CHUNKS + DENSE_CHUNKS]
DENSE0 = MIX_CHUNKS
MOE0 = 2 * MIX_CHUNKS + DENSE_CHUNKS
C_SU, C_Q, C_KV, C_AU, C_AC, C_AB, C_GA, C_OA, C_GC, C_OC, C_GB, C_GLU, C_OB, C_WO = (
    0, 2, 4, 6, 8, 10, 12, 16, 18, 22, 24, 28, 29, 31)
COL_AU, COL_AB, COL_AC, COL_SU, COL_Q, COL_KV = 0, 512, 1024, 1536, 2048, 2560
KV_W = 2 * HD + IDX_HEADS * HD + HD + IDX_HEADS
COL_G = COL_KV + KV_W
BU_AFTER = [2, 3, 4, 5, 7, 8, 10, 11, 13, 14, 16, 17, 19, 20, 22, 23]

PAR_LRE, PAR_LIM, PAR_LDT = 0, SCHUNKS, 2 * SCHUNKS
PAR_CW = 3 * SCHUNKS
PAR_D = PAR_CW + 3 * CT
PAR_GAIN = PAR_D + CT
PAR_CRE = PAR_GAIN + 10 * HD
PAR_CIM = PAR_CRE + SCHUNKS * 32
PAR_B = PAR_CIM + SCHUNKS * 32
PAR_W = PAR_B + CT * 2 * P

MAGIC = 12582912.0
PIO2 = (1.5703125, 4.837512969970703e-4, 7.54978995489188216e-8)


def mixer_stream(w_in, w_out_a, w_out_b, w_out_c, w_glu, w_o, layer):
    wi = w_in[layer].rearrange("(k p) n -> p k n", p=P)
    stripe = lambda col, width: [(wi[:, 4 * h:4 * h + 4, col:col + width], (4, width)) for h in range(2)]
    rows = lambda w: [(w.rearrange("(k p) n -> p k n", p=P)[:, 2 * h:2 * h + 2, :], (2, D))
                      for h in range(w.shape[0] // (2 * P))]
    gates = lambda branch: stripe(COL_G + branch * D, HALF) + stripe(COL_G + branch * D + HALF, HALF)
    chunks = stripe(COL_SU, SSM) + stripe(COL_Q, HALF) + stripe(COL_KV, KV_W)
    chunks += stripe(COL_AU, CONV) + stripe(COL_AC, CONV) + stripe(COL_AB, CONV)
    chunks += gates(0) + rows(w_out_a[layer]) + gates(2) + rows(w_out_c[layer]) + gates(1)
    chunks += [(w_glu[layer].rearrange("(k p) n -> p k n", p=P), (4, SSM))]
    chunks += rows(w_out_b[layer]) + rows(w_o[layer])
    assert len(chunks) == MIX_CHUNKS
    return chunks


class Chain:

    def __init__(self, eng, sem):
        self.eng, self.sem, self.n = eng, sem, 0

    def step(self, ins):
        ins.then_inc(self.sem, 1)
        self.n += 1

    def join(self):
        self.eng.wait_ge(self.sem, self.n)

    def then(self, ins):
        self.step(ins)
        self.join()


def trunk(nc, x, gains, w_in, par, w_glu, w_out_a, w_out_b, w_out_c, w_o, rope, slot_ids, ffn_w1, ffn_w3, ffn_w2,
          router_w, moe_w1, moe_w3, moe_w2, out):
    with ExitStack() as ctx:
        def sb(name, shape, dt=F32, scope=ctx):
            return scope.enter_context(nc.sbuf_tensor(name, shape, dt))

        def sem(name):
            return ctx.enter_context(nc.semaphore(name))

        ps = ctx.enter_context(nc.psum_tensor("ps", [P, 8, HALF], F32))

        raw = sb("raw", [P, RAW, CHUNK])
        w_hi = sb("w_hi", [P, SPLIT, CHUNK], F32R)
        w_lo = sb("w_lo", [P, SPLIT, CHUNK], F32R)
        x_tok = sb("x_tok", [P, BLOCKS, D])
        h_tok = sb("h_tok", [P, BLOCKS, D])
        hT_hi = sb("hT_hi", [P, KD, SEQ], F32R)
        hT_lo = sb("hT_lo", [P, KD, SEQ], F32R)
        ident = sb("ident", [P, P])
        upper = sb("upper", [P, P])
        ones = sb("ones", [P, P])
        causal = sb("causal", [P, P])
        rope_sb = sb("rope_sb", [P, BLOCKS, 3, 32])
        zero_r = sb("zero_r", [P, P], F32R)
        norm_ss = sb("norm_ss", [P, 4, BLOCKS])

        mix = ExitStack()
        gate = sb("gate", [P, BLOCKS, D], F32, mix)
        yac_hi = sb("yac_hi", [P, CT, SEQ], F32R, mix)
        yac_lo = sb("yac_lo", [P, CT, SEQ], F32R, mix)
        su = sb("su", [P, CT, SEQ], F32, mix)
        u_t = sb("u_t", [P, CT, SEQ], F32, mix)
        v_t = sb("v_t", [P, CT, SEQ + 2], F32, mix)
        par_sb = sb("par_sb", [P, PAR_W], F32, mix)
        qkT = sb("qkT", [P, 8, SEQ], F32, mix)
        v_sb = sb("v_sb", [P, BLOCKS, HD], F32, mix)
        wi_sb = sb("wi_sb", [P, BLOCKS, IDX_HEADS], F32, mix)
        probs = sb("probs", [P, 4, SEQ], F32, mix)
        keybias = sb("keybias", [P, BLOCKS, SEQ], F32, mix)
        top8 = sb("top8", [P, 8], F32, mix)
        smalls = sb("smalls", [P, 8], F32, mix)
        qk_ss = sb("qk_ss", [P, 3, BLOCKS, 10], F32, mix)
        rowmax = sb("rowmax", [P, 4], F32, mix)
        rowsum = sb("rowsum", [P, 4], F32, mix)
        rowinv = sb("rowinv", [P, 4], F32, mix)
        trig = sb("trig", [P, 32, SCHUNKS], F32, mix)
        pow_b = sb("pow_b", [P, 2, 16, SCHUNKS], F32, mix)
        pow_a = sb("pow_a", [P, 2, 16, SCHUNKS], F32, mix)
        table = sb("table", [P, 2, 2, SEQ], F32, mix)
        pool_t = sb("pool_t", [P, 2, SEQ], F32, mix)
        state = sb("state", [P, 2, SEQ], F32, mix)
        with ExitStack() as overlay:
            turn = sb("turn", [P, 2, 4, SEQ], F32, overlay)
        yb_hi = sb("yb_hi", [P, CT, SEQ], F32R, mix)
        yb_lo = sb("yb_lo", [P, CT, SEQ], F32R, mix)
        mix.close()
        gain_row = gate[:, 0, :]
        qk = h_tok[:, :, :].rearrange("p b (h d) -> p b h d", d=HD)
        mixed = h_tok
        scratch = probs

        ffn = ExitStack()
        sil = sb("sil", [P, HALF], F32, ffn)
        gain_ff = sb("gain_ff", [P, D], F32, ffn)
        hid = sb("hid", [P, HALF], F32, ffn)
        hidT_hi = sb("hidT_hi", [P, HALF], F32R, ffn)
        hidT_lo = sb("hidT_lo", [P, HALF], F32R, ffn)
        h_hi = sb("h_hi", [P, BLOCKS, D], F32R, ffn)
        h_lo = sb("h_lo", [P, BLOCKS, D], F32R, ffn)
        xg_hi = sb("xg_hi", [P, KD, P], F32R, ffn)
        xg_lo = sb("xg_lo", [P, KD, P], F32R, ffn)
        y_hi = sb("y_hi", [P, D], F32R, ffn)
        y_lo = sb("y_lo", [P, D], F32R, ffn)
        router_sb = sb("router_sb", [P, KD, EXPERTS], F32, ffn)
        slot_id = sb("slot_id", [P, 2, P], F32, ffn)
        pick = sb("pick", [P, BLOCKS, P], F32R, ffn)
        pickT = sb("pickT", [P, BLOCKS, P], F32R, ffn)
        rt = sb("rt", [P, 10, BLOCKS, EXPERTS], F32, ffn)
        rt8 = sb("rt8", [P, BLOCKS, 8], F32, ffn)
        rts = sb("rts", [P, 6, BLOCKS], F32, ffn)
        gate_of = sb("gate_of", [P, BLOCKS, EXPERTS], F32, ffn)
        slot_of = sb("slot_of", [P, BLOCKS, EXPERTS + 1], F32, ffn)
        most = sb("most", [P, 1], F32, ffn)
        most_i = sb("most_i", [1, 1], I32, ffn)
        ffn.close()

        raw_full = [sem(f"raw_full{i}") for i in range(RAW)]
        hi_done, lo_done, used = sem("hi_done"), sem("lo_done"), sem("used")
        dve_step, pool_step = sem("dve_step"), sem("pool_step")
        names = """x_loaded consts rope_loaded gain_loaded par_loaded ss_done var_done std_done h_done hT_ps
            hT_hi_done hT_lo_done x_added out_stored zero_done
            su_copied q_copied kv_copied u_copied v_made conv_done ya_hi_done ya_lo_done
            gate_done gated mixed_done mixT_ps mixT_hi_done mixT_lo_done
            sq_done qk_ss_done qk_std_done qk_inv_done rope_done qkT_ps qkT_copied
            idx_ps scored bias_ready logit_ps logit_read shifted exp_done prob_done pT_ps pT_copied
            o_ps yc_hi_done yc_lo_done
            dt_exp lrdt_done mag_exp den_done den_inv coef_done table_done table_used bu_ps turned
            scanned rotated y_ps skip_done gelu_done yg_hi_done yg_lo_done glu_sig yb_made yb_hi_done yb_lo_done
            sil_done hid_done hidT_ps hidT_hi_done hidT_lo_done ff_out
            router_loaded slots_loaded h_hi_done h_lo_done logits_ps exp_r picked rank_ps slots_done most_done top_r
            pick_done gather_ps xg_hi_done xg_lo_done pickT_ps pickT_done y_hi_done y_lo_done scatter_ps acc_done
            final_done""".split()

        S = {n: sem(n) for n in names}
        block = ctx.enter_context(nc.Block())

        streams = [mixer_stream(w_in, w_out_a, w_out_b, w_out_c, w_glu, w_o, layer) for layer in range(DEPTH)]

        def slot_view(buf, n, shape):
            k, w = shape
            return buf[:, n % (RAW if buf is raw else SPLIT), 0:k * w].rearrange("p (k n) -> p k n", k=k)

        def split_hi(act, n, turns=0, width=CHUNK):
            act.wait_ge(raw_full[n % RAW], 16 * (n // RAW + 1) + 16 * turns)
            if n >= SPLIT:
                act.wait_ge(used, n - SPLIT + 1 + 6 * turns)
            act.activation(w_hi[:, n % SPLIT, 0:width], raw[:, n % RAW, 0:width], ACT.Copy).then_inc(hi_done, 1)

        def split_lo(dve, n, seen=None, width=CHUNK):
            dve.wait_ge(hi_done, n + 1 if seen is None else seen)
            dve.tensor_tensor(w_lo[:, n % SPLIT, 0:width], raw[:, n % RAW, 0:width],
                              w_hi[:, n % SPLIT, 0:width].bitcast(F32), ALU.subtract).then_inc(lo_done, 1)

        def value(eng, v):
            return v if isinstance(v, int) else eng.snap(v)

        def mix_width(layer, c):
            k, w = streams[layer][c][1]
            return k * w

        @block.sync
        def _(sp):
            sp.dma_start(x_tok[:, :, :], x[0].rearrange("(b p) d -> p b d", p=P)).then_inc(S["x_loaded"], 16)

            def load(n, src, dst):
                if n >= RAW:
                    sp.wait_ge(lo_done, n - RAW + 1)
                sp.dma_start(dst, src).then_inc(raw_full[n % RAW], 16)

            def mixer(layer):
                for c, (src, shape) in enumerate(streams[layer]):
                    load(MIX0[layer] + c, src, slot_view(raw, MIX0[layer] + c, shape))

            w1d = ffn_w1[0].rearrange("(k p) n -> p k n", p=P)
            w3d = ffn_w3[0].rearrange("(k p) n -> p k n", p=P)
            w2d = ffn_w2[0].rearrange("(k p) n -> p k n", p=P)

            def load_at(n, turns, src):
                free = value(sp, n - RAW + 1 + 6 * turns)
                sp.wait_ge(lo_done, free)
                shape = tuple(src.shape[1:])
                sp.dma_start(slot_view(raw, n, shape), src).then_inc(raw_full[n % RAW], 16)

            def dense():
                n = DENSE0
                load(n, w1d[:, :, 0:DENSE_W], slot_view(raw, n, (KD, DENSE_W)))
                load(n + 1, w3d[:, :, 0:DENSE_W], slot_view(raw, n + 1, (KD, DENSE_W)))
                with sp.Fori(0, (DENSE_STRIPES - 1) // 2) as t:
                    for h in range(2):
                        m = n + 2 + 3 * h
                        col = sp.snap((2 * t + 1 + h) * DENSE_W)
                        row = sp.snap((2 * t + h) * 2)
                        load_at(m, t, w1d[:, :, bass.ds(col, DENSE_W)])
                        load_at(m + 1, t, w3d[:, :, bass.ds(col, DENSE_W)])
                        load_at(m + 2, t, w2d[:, bass.ds(row, 2), :])
                last = n + DENSE_CHUNKS - 1
                load(last, w2d[:, 2 * (DENSE_STRIPES - 1):2 * DENSE_STRIPES, :], slot_view(raw, last, (2, D)))

            w1e = moe_w1[0].rearrange("e (k p) n -> p (e k) n", p=P)
            w3e = moe_w3[0].rearrange("e (k p) n -> p (e k) n", p=P)
            w2e = moe_w2[0].rearrange("e (k p) n -> p (e k) n", p=P)
            K2 = FF_EXPERT // P

            def experts(rnd):
                n = MOE0 + rnd * EXPERTS * MOE_CHUNKS

                def up(m, turns, w, e, t):
                    col = value(sp, t * HALF)
                    for half in range(2):
                        row = value(sp, KD * e + 4 * half)
                        load_at(m + half, turns, w[:, bass.ds(row, 4), bass.ds(col, HALF)])

                def down(m, turns, e, t):
                    for half in range(2):
                        row = value(sp, K2 * e + 4 * t + 2 * half)
                        load_at(m + half, turns, w2e[:, bass.ds(row, 2), :])

                def expert(e, last):
                    with sp.Fori(1, MOE_STRIPES) as t:
                        turns = MOE_STRIPES * e + t - 1
                        up(n + 4, turns, w1e, e, t)
                        up(n + 6, turns, w3e, e, t)
                        down(n + 8, turns, e, t - 1)
                    turns = MOE_STRIPES * e + MOE_STRIPES - 1
                    if last:
                        down(n + 4, turns, e, MOE_STRIPES - 1)
                        return
                    up(n + 4, turns, w1e, e + 1, 0)
                    down(n + 6, turns, e, MOE_STRIPES - 1)
                    up(n + 8, turns, w3e, e + 1, 0)

                up(n, 0, w1e, 0, 0)
                up(n + 2, 0, w3e, 0, 0)
                with sp.Fori(0, EXPERTS - 1) as e:
                    expert(e, False)
                expert(EXPERTS - 1, True)

            mixer(0)
            dense()
            mixer(1)
            experts(0)
            sp.wait_ge(S["most_done"], 1)
            most_tokens = sp.value_load(most_i[0:1, 0:1])
            with sp.If(most_tokens > SLOTS):
                experts(1)
            sp.wait_ge(S["final_done"], 1)
            sp.dma_start(out[0].rearrange("(b p) d -> p b d", p=P), x_tok[:, :, :]).then_inc(S["out_stored"], 16)
            sp.wait_ge(S["out_stored"], 16)

        @block.tensor
        def _(pe):
            def three(dst, x_hi, x_lo, n, tile, first, last):
                hi, lo = tile(w_hi), tile(w_lo)
                pe.matmul(dst, x_hi, hi, start=first, stop=False, skip_group_check=True)
                pe.matmul(dst, x_hi, lo, start=False, stop=False, skip_group_check=True)
                return pe.matmul(dst, x_lo, hi, start=False, stop=last, skip_group_check=True)

            def columns(n, bank, k0, nk, width, first, last, seen=None):
                pe.wait_ge(lo_done, n + 1 if seen is None else seen)
                for k in range(nk):
                    for b in range(BLOCKS):
                        tok = slice(b * P, b * P + P)
                        mm = three(ps[:, bank + b, 0:width], hT_hi[:, k0 + k, tok], hT_lo[:, k0 + k, tok], n,
                                   lambda w: slot_view(w, n, (nk, width))[:, k, :], first and k == 0,
                                   last and k == nk - 1)
                mm.then_inc(used, 1)

            def channels(n, bank, k0, x_hi, x_lo, first, last):
                pe.wait_ge(lo_done, n + 1)
                for k in range(4):
                    for c in range(CT):
                        dst = ps[:, bank + c // 2, (c % 2) * SEQ:(c % 2 + 1) * SEQ]
                        wh = slot_view(w_hi, n, (4, HALF))[:, k, c * P:c * P + P]
                        wl = slot_view(w_lo, n, (4, HALF))[:, k, c * P:c * P + P]
                        start = first and k == 0 and c % 2 == 0
                        pe.matmul(dst, wh, x_hi[:, k0 + k, :], start=start, stop=False, skip_group_check=True)
                        pe.matmul(dst, wl, x_hi[:, k0 + k, :], start=False, stop=False, skip_group_check=True)
                        mm = pe.matmul(dst, wh, x_lo[:, k0 + k, :], start=False, stop=last and k == 3,
                                       skip_group_check=True)
                mm.then_inc(used, 1)

            def rows(n, k0, x_hi, x_lo, first, last, bank=0, blocks=BLOCKS, seen=None):
                pe.wait_ge(lo_done, n + 1 if seen is None else seen)
                for k in range(2):
                    for b in range(blocks):
                        tok = slice(b * P, b * P + P)
                        for h in range(2):
                            mm = three(ps[:, bank + 2 * b + h, :], x_hi[:, k0 + k, tok], x_lo[:, k0 + k, tok], n,
                                       lambda w: slot_view(w, n, (2, D))[:, k, h * HALF:(h + 1) * HALF],
                                       first and k == 0, last and k == 1)
                mm.then_inc(used, 1)

            def turn_rows(src, bank):
                for k in range(KD):
                    for b in range(BLOCKS):
                        at = (k % 2) * SEQ + b * P
                        tr = pe.transpose(ps[:, bank + k // 2, at:at + P], src[:, b, k * P:k * P + P], ident[:, :])
                    if k % 2:
                        yield tr

            def norm_turn(i):
                pe.wait_ge(S["h_done"], BLOCKS * (i + 1))
                for tr in turn_rows(h_tok, 0):
                    tr.then_inc(S["hT_ps"], 1)

            def bu(layer, j):
                if j == 0:
                    pe.wait_ge(S["su_copied"], layer + 1)
                    pe.wait_ge(S["par_loaded"], 16 * (layer + 1))
                else:
                    pe.wait_ge(S["turned"], 16 * layer + j)
                r = 32 * (j % 4)
                for part in range(2):
                    bt = par_sb[r:r + 32, PAR_B:PAR_B + CT * 2 * P].rearrange("p (c i n) -> p c i n", c=CT, i=2)
                    mm = pe.matmul(ps[:, 4, part * SEQ:(part + 1) * SEQ], bt[:, j // 4, part, :],
                                   su[r:r + 32, j // 4, :], start=part == 0, stop=part == 1, skip_group_check=True,
                                   tile_position=(r, 0))
                mm.then_inc(S["bu_ps"], 1)

            def y_of(layer, j):
                pe.wait_ge(S["rotated"], SCHUNKS * layer + j + 1)
                if j >= 4 and j % 4 == 0:
                    pe.wait_ge(S["skip_done"], CT * layer + j // 4)
                r, at = 32 * (j % 4), ((j // 4) % 2) * SEQ
                for part, col in ((0, PAR_CRE), (1, PAR_CIM)):
                    mm = pe.matmul(ps[r:r + 32, 5, at:at + SEQ], par_sb[:, col + 32 * j:col + 32 * j + 32],
                                   state[:, part, :], start=part == 0, stop=part == 1, skip_group_check=True,
                                   tile_position=(0, r))
                mm.then_inc(S["y_ps"], 1)

            def turn_qk(layer, half):
                if half == 0:
                    pe.wait_ge(S["rope_done"], BLOCKS * (layer + 1))
                else:
                    pe.wait_ge(S["qkT_copied"], 2 * layer + 1)
                for i in range(4):
                    pair = 4 * half + i
                    for b in range(BLOCKS):
                        at = (i % 2) * SEQ + b * P
                        tr = pe.transpose(ps[:, 6 + i // 2, at:at + P], h_tok[:, b, pair * P:pair * P + P],
                                          ident[:, :])
                tr.then_inc(S["qkT_ps"], 1)

            def index_scores(layer, b):
                if b == 0:
                    pe.wait_ge(S["qkT_copied"], 2 * layer + 2)
                else:
                    pe.wait_ge(S["scored"], 2 * layer + 1)
                keys = (b + 1) * P
                for h in range(IDX_HEADS):
                    r = HD * (h % 2)
                    at = (h // 2) * keys
                    mm = pe.matmul(ps[:, 6 + h % 2, at:at + keys],
                                   qkT[r:r + HD, 5 + h // 2, b * P:b * P + P], qkT[r:r + HD, 7, 0:keys],
                                   start=at == 0, stop=True, skip_group_check=True, tile_position=(r, 0))
                mm.then_inc(S["idx_ps"], 1)

            def logits(layer, i):
                n = 4 * layer + i
                b, g = i // 2, i % 2
                if i == 0:
                    pe.wait_ge(S["scored"], 2 * layer + 2)
                else:
                    pe.wait_ge(S["yc_lo_done"], n)
                keys = (b + 1) * P
                for h in range(4):
                    r = HD * (h % 2)
                    at = (h // 2) * keys
                    mm = pe.matmul(ps[:, 6 + h % 2, at:at + keys],
                                   qkT[r:r + HD, 2 * g + h // 2, b * P:b * P + P], qkT[r:r + HD, 4, 0:keys],
                                   start=at == 0, stop=True, skip_group_check=True, tile_position=(r, 0))
                mm.then_inc(S["logit_ps"], 1)

            def turn_probs(layer, i):
                n = 4 * layer + i
                pe.wait_ge(S["prob_done"], n + 1)
                b = i // 2
                for kt in range(b + 1):
                    for h in range(4):
                        tr = pe.transpose(ps[:, 6 + kt, h * P:h * P + P], probs[:, h, kt * P:kt * P + P], ident[:, :])
                tr.then_inc(S["pT_ps"], 1)

            def values(layer, i):
                n = 4 * layer + i
                pe.wait_ge(S["pT_copied"], n + 1)
                b = i // 2
                for q in range(4):
                    r, pair = HD * (q // 2), q % 2
                    for kt in range(b + 1):
                        mm = pe.matmul(ps[r:r + HD, 6, pair * P:pair * P + P], v_sb[:, kt, :],
                                       u_t[:, 2 * kt + q // 2, (q % 2) * P:(q % 2) * P + P],
                                       start=kt == 0, stop=kt == b, skip_group_check=True, tile_position=(0, r))
                mm.then_inc(S["o_ps"], 1)

            def mixer(layer):
                c0 = MIX0[layer]
                norm_turn(2 * layer)
                todo = {}
                for j, c in enumerate(BU_AFTER):
                    todo[c] = j

                def s5(c):
                    if c in todo:
                        j = todo[c]
                        bu(layer, j)
                        if j >= 2:
                            y_of(layer, j - 2)

                def stripe(c, bank, width=HALF):
                    columns(c0 + c, bank, 0, 4, width, True, False)
                    s5(c)
                    columns(c0 + c + 1, bank, 4, 4, width, False, True)
                    s5(c + 1)

                def held(c, bank):
                    channels(c0 + c, bank, 0, hT_hi, hT_lo, True, False)
                    s5(c)
                    channels(c0 + c + 1, bank, 4, hT_hi, hT_lo, False, True)
                    s5(c + 1)

                pe.wait_ge(S["hT_lo_done"], 4 * (2 * layer + 1))
                held(C_SU, 0)
                stripe(C_Q, 2)
                pe.wait_ge(S["su_copied"], layer + 1)
                stripe(C_KV, 0, KV_W)
                pe.wait_ge(S["q_copied"], layer + 1)
                held(C_AU, 2)
                pe.wait_ge(S["kv_copied"], 7 * (layer + 1))
                held(C_AC, 0)
                pe.wait_ge(S["u_copied"], layer + 1)
                channels(c0 + C_AB, 2, 0, hT_hi, hT_lo, True, False)
                s5(C_AB)
                turn_qk(layer, 0)
                channels(c0 + C_AB + 1, 2, 4, hT_hi, hT_lo, False, True)
                s5(C_AB + 1)
                turn_qk(layer, 1)
                pe.wait_ge(S["v_made"], layer + 1)
                columns(c0 + C_GA, 0, 0, 4, HALF, True, False)
                s5(C_GA)
                columns(c0 + C_GA + 1, 0, 4, 4, HALF, False, True)
                s5(C_GA + 1)
                index_scores(layer, 0)
                pe.wait_ge(S["conv_done"], layer + 1)
                columns(c0 + C_GA + 2, 2, 0, 4, HALF, True, False)
                s5(C_GA + 2)
                columns(c0 + C_GA + 3, 2, 4, 4, HALF, False, True)
                s5(C_GA + 3)
                index_scores(layer, 1)
                pe.wait_ge(S["gate_done"], 6 * layer + 2)
                pe.wait_ge(S["ya_lo_done"], layer + 1)
                rows(c0 + C_OA, 0, yac_hi, yac_lo, True, False)
                s5(C_OA)
                rows(c0 + C_OA + 1, 2, yac_hi, yac_lo, False, True)
                s5(C_OA + 1)
                logits(layer, 0)
                pe.wait_ge(S["gated"], 3 * layer + 1)
                columns(c0 + C_GC, 0, 0, 4, HALF, True, False)
                turn_probs(layer, 0)
                columns(c0 + C_GC + 1, 0, 4, 4, HALF, False, True)
                s5(C_GC + 1)
                values(layer, 0)
                logits(layer, 1)
                columns(c0 + C_GC + 2, 2, 0, 4, HALF, True, False)
                s5(C_GC + 2)
                turn_probs(layer, 1)
                columns(c0 + C_GC + 3, 2, 4, 4, HALF, False, True)
                values(layer, 1)
                logits(layer, 2)
                turn_probs(layer, 2)
                values(layer, 2)
                logits(layer, 3)
                turn_probs(layer, 3)
                values(layer, 3)
                pe.wait_ge(S["gate_done"], 6 * layer + 4)
                pe.wait_ge(S["yc_lo_done"], 4 * layer + 4)
                rows(c0 + C_OC, 0, yac_hi, yac_lo, True, False)
                s5(C_OC)
                rows(c0 + C_OC + 1, 2, yac_hi, yac_lo, False, True)
                s5(C_OC + 1)
                pe.wait_ge(S["gated"], 3 * layer + 2)
                columns(c0 + C_GB, 0, 0, 4, HALF, True, False)
                y_of(layer, SCHUNKS - 2)
                columns(c0 + C_GB + 1, 0, 4, 4, HALF, False, True)
                y_of(layer, SCHUNKS - 1)
                columns(c0 + C_GB + 2, 2, 0, 4, HALF, True, False)
                columns(c0 + C_GB + 3, 2, 4, 4, HALF, False, True)
                pe.wait_ge(S["yg_lo_done"], layer + 1)
                channels(c0 + C_GLU, 4, 0, yb_hi, yb_lo, True, True)
                pe.wait_ge(S["gate_done"], 6 * layer + 6)
                pe.wait_ge(S["yb_lo_done"], layer + 1)
                rows(c0 + C_OB, 0, yb_hi, yb_lo, True, False)
                rows(c0 + C_OB + 1, 2, yb_hi, yb_lo, False, True)
                pe.wait_ge(S["mixed_done"], 2 * (layer + 1))
                for tr in turn_rows(mixed, 4):
                    tr.then_inc(S["mixT_ps"], 1)
                pe.wait_ge(S["mixT_lo_done"], 4 * (layer + 1))
                for i in range(4):
                    rows(c0 + C_WO + i, 2 * i, hT_hi, hT_lo, i == 0, i == 3)

            def clear(bank, count):
                for b in range(bank, bank + count):
                    pe.matmul(ps[:, b, 0:P], zero_r[:, :], zero_r[:, :], start=True, stop=False,
                              skip_group_check=True)

            def dense():
                n0 = DENSE0

                def up(n, i, turns):
                    for which, bank, read in ((0, 0, S["sil_done"]), (1, 1, S["hid_done"])):
                        if i is not None:
                            pe.wait_ge(read, i)
                        pe.wait_ge(lo_done, n + which + 1 + 6 * turns)
                        for k in range(KD):
                            for b in range(BLOCKS):
                                tok = slice(b * P, b * P + P)
                                mm = three(ps[:, bank, b * DENSE_W:(b + 1) * DENSE_W], hT_hi[:, k, tok],
                                           hT_lo[:, k, tok], n,
                                           lambda w: slot_view(w, n + which, (KD, DENSE_W))[:, k, :],
                                           k == 0 and b == 0, k == KD - 1)
                        mm.then_inc(used, 1)

                def turn_hidden(i):
                    pe.wait_ge(S["hid_done"], i + 1)
                    for k in range(2):
                        for b in range(BLOCKS):
                            tr = pe.transpose(ps[:, 2, k * SEQ + b * P:k * SEQ + b * P + P],
                                              hid[:, b * DENSE_W + k * P:b * DENSE_W + k * P + P], ident[:, :])
                    tr.then_inc(S["hidT_ps"], 1)

                x_hi = hidT_hi[:, :].rearrange("p (k t) -> p k t", k=2)
                x_lo = hidT_lo[:, :].rearrange("p (k t) -> p k t", k=2)
                norm_turn(1)
                pe.wait_ge(S["hT_lo_done"], 8)
                clear(4, 4)
                up(n0, None, 0)
                turn_hidden(0)
                with pe.Fori(0, (DENSE_STRIPES - 1) // 2) as t:
                    for h in range(2):
                        m = n0 + 2 + 3 * h
                        i = 2 * t + 1 + h
                        up(m, i, t)
                        pe.wait_ge(S["hidT_lo_done"], i)
                        rows(m + 2, 0, x_hi, x_lo, False, False, bank=4, seen=m + 3 + 6 * t)
                        turn_hidden(i)
                pe.wait_ge(S["hidT_lo_done"], DENSE_STRIPES)
                rows(n0 + DENSE_CHUNKS - 1, 0, x_hi, x_lo, False, True, bank=4)

            def route():
                norm_turn(3)
                pe.wait_ge(S["hT_lo_done"], 16)
                pe.wait_ge(S["router_loaded"], 16)
                for b in range(BLOCKS):
                    for k in range(KD):
                        for part in (hT_hi, hT_lo):
                            mm = pe.matmul(ps[:, 4, b * 8:b * 8 + 8], part[:, k, b * P:b * P + P].bitcast(F32),
                                           router_sb[:, k, :], start=b == 0 and k == 0 and part is hT_hi,
                                           stop=k == KD - 1 and part is hT_lo, skip_group_check=True)
                mm.then_inc(S["logits_ps"], 1)
                pe.wait_ge(S["picked"], 1)
                sel = rt[:, 7]
                pe.matmul(ps[:, 5, 0:8], upper[:, :], sel[:, 0, :], start=True, stop=True, skip_group_check=True)
                pe.matmul(ps[:, 5, 8:16], ones[:, :], sel[:, 0, :], start=False, stop=False, skip_group_check=True)
                pe.matmul(ps[:, 5, 8:16], upper[:, :], sel[:, 1, :], start=False, stop=True, skip_group_check=True)
                pe.matmul(ps[:, 5, 16:24], ones[:, :], sel[:, 0, :], start=False, stop=False, skip_group_check=True)
                pe.matmul(ps[:, 5, 16:24], ones[:, :], sel[:, 1, :], start=False, stop=True,
                          skip_group_check=True).then_inc(S["rank_ps"], 1)
                pe.wait_ge(S["slots_done"], 1)

            def experts(rnd):
                n0 = MOE0 + rnd * EXPERTS * MOE_CHUNKS
                e0 = rnd * EXPERTS
                i0 = DENSE_STRIPES + e0 * MOE_STRIPES
                xT_hi = hidT_hi[:, :].rearrange("p (k t) -> p k t", k=4)
                xT_lo = hidT_lo[:, :].rearrange("p (k t) -> p k t", k=4)

                def up(n, which, i, turns):
                    pe.wait_ge(S["hid_done"] if which else S["sil_done"], i)
                    for half in range(2):
                        m = n + half
                        pe.wait_ge(lo_done, m + 1 + 6 * turns)
                        for k in range(4):
                            kk = 4 * half + k
                            mm = three(ps[:, which, :], xg_hi[:, kk, :], xg_lo[:, kk, :], m,
                                       lambda w: slot_view(w, m, (4, HALF))[:, k, :], kk == 0, kk == KD - 1)
                        mm.then_inc(used, 1)

                def turn_hidden(i):
                    pe.wait_ge(S["hid_done"], i + 1)
                    for k in range(4):
                        tr = pe.transpose(ps[:, 4, k * P:k * P + P], hid[:, k * P:k * P + P], ident[:, :])
                    tr.then_inc(S["hidT_ps"], 1)

                def down(n, i, turns, first=False):
                    pe.wait_ge(S["hidT_lo_done"], i)
                    for half in range(2):
                        rows(n + half, 2 * half, xT_hi, xT_lo, first and half == 0, False, bank=2, blocks=1,
                             seen=n + half + 1 + 6 * turns)

                def gather(e):
                    pe.wait_ge(S["pick_done"], BLOCKS * (e0 + e + 1))
                    for src, bank in ((h_hi, 4), (h_lo, 6)):
                        for k in range(KD):
                            for b in range(BLOCKS):
                                mm = pe.matmul(ps[:, bank + k // 4, (k % 4) * P:(k % 4) * P + P],
                                               src[:, b, k * P:k * P + P], pick[:, b, :],
                                               start=k % 4 == 0 and b == 0, stop=b == 1, skip_group_check=True)
                        mm.then_inc(S["gather_ps"], 1)

                def turn_pick(e):
                    for b in range(BLOCKS):
                        tr = pe.transpose(ps[:, 5, b * P:b * P + P], pick[:, b, :].bitcast(F32), ident[:, :])
                    tr.then_inc(S["pickT_ps"], 1)

                def scatter(e):
                    pe.wait_ge(S["pickT_done"], e0 + e + 1)
                    pe.wait_ge(S["y_hi_done"], e0 + e + 1)
                    pe.wait_ge(S["y_lo_done"], e0 + e + 1)
                    for b in range(BLOCKS):
                        for half in range(2):
                            dst = ps[:, 2 + half if b == 0 else 6 + half, :]
                            pe.matmul(dst, pickT[:, b, :], y_hi[:, half * HALF:(half + 1) * HALF], start=True,
                                      stop=False, skip_group_check=True)
                            mm = pe.matmul(dst, pickT[:, b, :], y_lo[:, half * HALF:(half + 1) * HALF], start=False,
                                           stop=True, skip_group_check=True)
                    mm.then_inc(S["scatter_ps"], 1)

                def expert(e, last):
                    i = i0 + MOE_STRIPES * e
                    turns = MOE_STRIPES * e
                    turn_hidden(i)
                    up(n0 + 4, 0, i + 1, turns)
                    up(n0 + 6, 1, i + 1, turns)
                    pe.wait_ge(S["acc_done"], 4 * (e0 + e) + 1)
                    down(n0 + 8, i + 1, turns, first=True)
                    turn_hidden(i + 1)
                    turn_pick(e)
                    with pe.Fori(2, MOE_STRIPES - 1) as t:
                        up(n0 + 4, 0, i + t, turns + t - 1)
                        up(n0 + 6, 1, i + t, turns + t - 1)
                        down(n0 + 8, i + t, turns + t - 1)
                        turn_hidden(i + t)
                    t = MOE_STRIPES - 1
                    up(n0 + 4, 0, i + t, turns + t - 1)
                    up(n0 + 6, 1, i + t, turns + t - 1)
                    if not last:
                        pe.wait_ge(S["hidT_lo_done"], i + t)
                        pe.wait_ge(S["pickT_done"], e0 + e + 1)
                        gather(e + 1)
                    down(n0 + 8, i + t, turns + t - 1)
                    if not last:
                        pe.wait_ge(S["xg_hi_done"], e0 + e + 2)
                    turn_hidden(i + t)
                    if last:
                        down(n0 + 4, i + t + 1, turns + t)
                    else:
                        pe.wait_ge(S["xg_lo_done"], e0 + e + 2)
                        up(n0 + 4, 0, i + t + 1, turns + t)
                        down(n0 + 6, i + t + 1, turns + t)
                        up(n0 + 8, 1, i + t + 1, turns + t)
                    scatter(e)

                if rnd == 0:
                    pe.wait_ge(S["h_lo_done"], BLOCKS)
                else:
                    pe.wait_ge(S["acc_done"], 4 * e0 + 1)
                gather(0)
                pe.wait_ge(S["xg_hi_done"], e0 + 1)
                pe.wait_ge(S["xg_lo_done"], e0 + 1)
                up(n0, 0, i0, 0)
                up(n0 + 2, 1, i0, 0)
                with pe.Fori(0, EXPERTS - 1) as e:
                    expert(e, False)
                expert(EXPERTS - 1, True)

            pe.wait_ge(S["consts"], 5)
            mixer(0)
            dense()
            mixer(1)
            route()
            experts(0)
            pe.wait_ge(S["most_done"], 1)
            most_tokens = pe.value_load(most_i[0:1, 0:1])
            with pe.If(most_tokens > SLOTS):
                experts(1)

        def banks(lo, count):
            return ps[:, lo:lo + count, :].rearrange("p a n -> p (a n)")

        def flat(t):
            return t.rearrange("p a b -> p (a b)")

        @block.scalar
        def _(act):
            act.dma_start(rope_sb[:, :, :, :], rope).then_inc(S["rope_loaded"], 16)

            def norm(i):
                if i == 0:
                    act.wait_ge(S["x_loaded"], 16)
                else:
                    act.wait_ge(S["x_added"], i)
                for b in range(BLOCKS):
                    act.activation(h_tok[:, b, :], x_tok[:, b, :], ACT.Square,
                                   accum_out=norm_ss[:, 0, b:b + 1]).then_inc(S["ss_done"], 1)
                act.wait_ge(S["var_done"], i + 1)
                act.activation(norm_ss[:, 2, :], norm_ss[:, 1, :], ACT.Sqrt).then_inc(S["std_done"], 1)

            def turned_hi(i, ready, bank, done):
                for q in range(4):
                    act.wait_ge(ready, 4 * i + q + 1)
                    act.activation(flat(hT_hi[:, 2 * q:2 * q + 2, :]), ps[:, bank + q, :], ACT.Copy)\
                       .then_inc(done, 1)

            def sigmoid_gate(layer, c, k, half):
                act.wait_ge(used, MIX0[layer] + c + 2)
                if k >= 4:
                    act.wait_ge(S["mixed_done"], 2 * layer + 1)
                elif k >= 2:
                    act.wait_ge(S["gated"], 3 * layer + 1)
                act.activation(gate[:, :, half * HALF:(half + 1) * HALF], ps[:, 2 * half:2 * half + 2, :],
                               ACT.Sigmoid).then_inc(S["gate_done"], 1)

            def softmax_exp(layer, i):
                n, keys = 4 * layer + i, (i // 2 + 1) * P
                act.wait_ge(S["shifted"], n + 1)
                for h in range(4):
                    ins = act.activation(probs[:, h, 0:keys], probs[:, h, 0:keys], ACT.Exp,
                                         bias=rowmax[:, h:h + 1], accum_out=rowsum[:, h:h + 1])
                    ins.then_inc(S["exp_done"], 1)

            def copy_pT(layer, i):
                n = 4 * layer + i
                act.wait_ge(S["pT_ps"], n + 1)
                act.activation(flat(u_t[:, 0:2 * (i // 2 + 1), :]), banks(6, i // 2 + 1), ACT.Copy)\
                   .then_inc(S["pT_copied"], 1)

            def yc_hi(layer, i):
                n, b, g = 4 * layer + i, i // 2, i % 2
                act.wait_ge(S["o_ps"], n + 1)
                if i == 0:
                    act.wait_ge(used, MIX0[layer] + C_OA + 2)
                act.activation(yac_hi[:, 2 * g:2 * g + 2, b * P:(b + 1) * P],
                               ps[:, 6, 0:2 * P].rearrange("p (a n) -> p a n", a=2), ACT.Copy)\
                   .then_inc(S["yc_hi_done"], 1)

            def copy_qkT(layer, half):
                act.wait_ge(S["qkT_ps"], 2 * layer + half + 1)
                act.activation(flat(qkT[:, 4 * half:4 * half + 4, :]), banks(6, 2), ACT.Copy)\
                   .then_inc(S["qkT_copied"], 1)

            def mixer(layer):
                c0 = MIX0[layer]
                sp = lambda c: split_hi(act, c0 + c, width=mix_width(layer, c))
                act.wait_ge(S["par_loaded"], 16 * (layer + 1))
                act.activation(trig[:, 1, :], par_sb[:, PAR_LDT:PAR_LDT + SCHUNKS], ACT.Exp).then_inc(S["dt_exp"], 1)
                act.wait_ge(S["lrdt_done"], layer + 1)
                act.activation(trig[:, 3, :], trig[:, 2, :], ACT.Exp).then_inc(S["mag_exp"], 1)
                sp(0)
                norm(2 * layer)
                sp(1)
                sp(2)
                turned_hi(2 * layer, S["hT_ps"], 0, S["hT_hi_done"])
                sp(3)
                sp(4)
                act.wait_ge(used, c0 + C_SU + 2)
                act.activation(flat(su[:, :, :]), banks(0, 2), ACT.Copy).then_inc(S["su_copied"], 1)
                sp(5)
                sp(6)
                act.wait_ge(used, c0 + C_Q + 2)
                act.wait_ge(S["hT_lo_done"], 4 * (2 * layer + 1))
                act.activation(h_tok[:, :, 0:HALF], ps[:, 2:4, :], ACT.Copy).then_inc(S["q_copied"], 1)
                sp(7)
                sp(8)
                act.wait_ge(used, c0 + C_KV + 2)
                kv = ps[:, 0:2, :]
                dst = h_tok
                for to, at, width in ((8, 0, 1), (9, 0, 1), (10, 2, IDX_HEADS), (14, 6, 1), (15, 6, 1)):
                    act.activation(dst[:, :, to * HD:(to + width) * HD], kv[:, :, at * HD:(at + width) * HD],
                                   ACT.Copy).then_inc(S["kv_copied"], 1)
                act.activation(v_sb[:, :, :], kv[:, :, HD:2 * HD], ACT.Copy).then_inc(S["kv_copied"], 1)
                act.activation(wi_sb[:, :, :], kv[:, :, 7 * HD:7 * HD + IDX_HEADS], ACT.Copy,
                               scale=IDX_HEADS ** -0.5).then_inc(S["kv_copied"], 1)
                sp(9)
                act.wait_ge(used, c0 + C_AU + 2)
                act.activation(flat(u_t[:, :, :]), banks(2, 2), ACT.Copy).then_inc(S["u_copied"], 1)
                sp(10)
                act.wait_ge(S["qk_ss_done"], layer + 1)
                act.activation(qk_ss[:, 1, :, :], qk_ss[:, 0, :, :], ACT.Sqrt).then_inc(S["qk_std_done"], 1)
                sp(11)
                sp(12)
                sp(13)
                copy_qkT(layer, 0)
                sp(14)
                copy_qkT(layer, 1)
                act.wait_ge(S["conv_done"], layer + 1)
                act.activation(flat(yac_hi[:, :, :]), flat(u_t[:, :, :]), ACT.Copy).then_inc(S["ya_hi_done"], 1)
                sp(15)
                sp(16)
                act.wait_ge(S["rope_done"], BLOCKS * (layer + 1))
                sigmoid_gate(layer, C_GA, 0, 0)
                sp(17)
                sp(18)
                sigmoid_gate(layer, C_GA + 2, 1, 1)
                sp(19)
                sp(20)
                softmax_exp(layer, 0)
                sp(21)
                sp(22)
                copy_pT(layer, 0)
                yc_hi(layer, 0)
                sigmoid_gate(layer, C_GC, 2, 0)
                softmax_exp(layer, 1)
                sp(23)
                copy_pT(layer, 1)
                sp(24)
                yc_hi(layer, 1)
                softmax_exp(layer, 2)
                copy_pT(layer, 2)
                yc_hi(layer, 2)
                softmax_exp(layer, 3)
                copy_pT(layer, 3)
                yc_hi(layer, 3)
                sigmoid_gate(layer, C_GC + 2, 3, 1)
                sp(25)
                sp(26)
                sp(27)
                sigmoid_gate(layer, C_GB, 4, 0)
                act.wait_ge(S["skip_done"], CT * (layer + 1))
                act.activation(flat(su[:, :, :]), flat(su[:, :, :]), ACT.Gelu_apprx_tanh).then_inc(S["gelu_done"], 1)
                act.wait_ge(S["gelu_done"], layer + 1)
                act.wait_ge(S["rotated"], SCHUNKS * (layer + 1))
                act.activation(flat(yb_hi[:, :, :]), flat(su[:, :, :]), ACT.Copy).then_inc(S["yg_hi_done"], 1)
                sp(28)
                sp(29)
                sp(30)
                sigmoid_gate(layer, C_GB + 2, 5, 1)
                act.wait_ge(used, c0 + C_GLU + 1)
                act.activation(flat(u_t[:, :, :]), banks(4, 2), ACT.Sigmoid).then_inc(S["glu_sig"], 1)
                act.wait_ge(S["yb_made"], layer + 1)
                act.activation(flat(yb_hi[:, :, :]), flat(su[:, :, :]), ACT.Copy).then_inc(S["yb_hi_done"], 1)
                sp(31)
                sp(32)
                sp(33)
                turned_hi(layer, S["mixT_ps"], 4, S["mixT_hi_done"])
                sp(34)

            def silu(i, after, width=HALF):
                act.wait_ge(used, after)
                act.wait_ge(S["hid_done"], i)
                act.activation(sil[:, 0:width], ps[:, 0, 0:width], ACT.Silu).then_inc(S["sil_done"], 1)

            def hidden_hi(i, bank):
                act.wait_ge(S["hidT_ps"], i + 1)
                act.activation(hidT_hi[:, :], ps[:, bank, :], ACT.Copy).then_inc(S["hidT_hi_done"], 1)

            def dense():
                n = DENSE0
                split_hi(act, n)
                split_hi(act, n + 1)
                norm(1)
                split_hi(act, n + 2)
                turned_hi(1, S["hT_ps"], 0, S["hT_hi_done"])
                split_hi(act, n + 3)
                silu(0, n + 1)
                split_hi(act, n + 4)
                hidden_hi(0, 2)
                with act.Fori(0, (DENSE_STRIPES - 3) // 2) as t:
                    for h in range(2):
                        m = n + 5 + 3 * h
                        split_hi(act, m, t)
                        silu(2 * t + h + 1, n + 3 + 3 * h + 6 * t)
                        split_hi(act, m + 1, t)
                        split_hi(act, m + 2, t)
                        hidden_hi(2 * t + h + 1, 2)
                last = n + 5 + 6 * ((DENSE_STRIPES - 3) // 2)
                i = DENSE_STRIPES - 2
                split_hi(act, last)
                silu(i, last - 2 + 0)
                split_hi(act, last + 1)
                split_hi(act, last + 2)
                hidden_hi(i, 2)
                split_hi(act, last + 3)
                silu(i + 1, last + 1)
                hidden_hi(i + 1, 2)

            def route():
                norm(3)
                turned_hi(3, S["hT_ps"], 0, S["hT_hi_done"])
                for b in range(BLOCKS):
                    act.activation(h_hi[:, b, :], h_tok[:, b, :], ACT.Copy).then_inc(S["h_hi_done"], 1)
                act.wait_ge(S["top_r"], 1)
                act.activation(flat(rt[:, 2]), flat(rt[:, 1]), ACT.Exp).then_inc(S["exp_r"], 1)

            def experts(rnd):
                n0 = MOE0 + rnd * EXPERTS * MOE_CHUNKS
                e0 = rnd * EXPERTS
                i0 = DENSE_STRIPES + e0 * MOE_STRIPES

                def xg(e):
                    act.wait_ge(S["gather_ps"], 2 * (e0 + e) + 1)
                    act.activation(flat(xg_hi[:, :, :]), banks(4, 2), ACT.Copy).then_inc(S["xg_hi_done"], 1)

                def stripe(i, t, turns):
                    split_hi(act, n0 + 6, turns)
                    hidden_hi(i + t - 1, 4)
                    split_hi(act, n0 + 7, turns)
                    silu(i + t, n0 + 6 + 6 * turns)
                    split_hi(act, n0 + 8, turns)
                    split_hi(act, n0 + 9, turns)

                def expert(e, last):
                    i = i0 + MOE_STRIPES * e
                    turns = MOE_STRIPES * e
                    stripe(i, 1, turns)
                    split_hi(act, n0 + 10, turns)
                    split_hi(act, n0 + 11, turns)
                    act.wait_ge(S["pickT_ps"], e0 + e + 1)
                    act.activation(flat(pickT[:, :, :]), ps[:, 5, 0:2 * P], ACT.Copy).then_inc(S["pickT_done"], 1)
                    with act.Fori(2, MOE_STRIPES - 1) as t:
                        stripe(i, t, turns + t - 1)
                        split_hi(act, n0 + 10, turns + t - 1)
                        split_hi(act, n0 + 11, turns + t - 1)
                    t = MOE_STRIPES - 1
                    stripe(i, t, turns + t - 1)
                    split_hi(act, n0 + 10, turns + t - 1)
                    if not last:
                        xg(e + 1)
                    split_hi(act, n0 + 11, turns + t - 1)
                    if not last:
                        split_hi(act, n0 + 6, turns + t)
                    hidden_hi(i + t, 4)
                    if not last:
                        split_hi(act, n0 + 7, turns + t)
                        silu(i + t + 1, n0 + 6 + 6 * (turns + t))
                        split_hi(act, n0 + 8, turns + t)
                        split_hi(act, n0 + 9, turns + t)
                    act.wait_ge(used, n0 + (6 if last else 8) + 6 * (turns + t))
                    act.activation(y_hi[:, :], banks(2, 2), ACT.Copy).then_inc(S["y_hi_done"], 1)
                    if not last:
                        split_hi(act, n0 + 10, turns + t)
                        split_hi(act, n0 + 11, turns + t)

                split_hi(act, n0)
                xg(0)
                split_hi(act, n0 + 1)
                split_hi(act, n0 + 2)
                split_hi(act, n0 + 3)
                silu(i0, n0 + 2)
                split_hi(act, n0 + 4)
                split_hi(act, n0 + 5)
                with act.Fori(0, EXPERTS - 1) as e:
                    expert(e, False)
                expert(EXPERTS - 1, True)

            mixer(0)
            dense()
            mixer(1)
            route()
            experts(0)
            act.wait_ge(S["most_done"], 1)
            most_tokens = act.value_load(most_i[0:1, 0:1])
            with act.If(most_tokens > SLOTS):
                experts(1)

        @block.vector
        def _(dve):
            own = Chain(dve, dve_step)

            def norm(i, gains):
                dve.wait_ge(S["ss_done"], BLOCKS * (i + 1))
                dve.tensor_scalar(norm_ss[:, 1, :], norm_ss[:, 0, :], 1.0 / D, EPS, ALU.mult, ALU.add)\
                   .then_inc(S["var_done"], 1)
                dve.wait_ge(S["std_done"], i + 1)
                own.then(dve.reciprocal(norm_ss[:, 3, :], norm_ss[:, 2, :]))
                dve.wait_ge(S["gain_loaded"], 16 * (i + 1))
                for b in range(BLOCKS):
                    dve.scalar_tensor_tensor(h_tok[:, b, :], x_tok[:, b, :], norm_ss[:, 3, b:b + 1], gains,
                                             ALU.mult, ALU.mult).then_inc(S["h_done"], 1)

            def turned_lo(i, ready, bank, done):
                for q in range(4):
                    dve.wait_ge(ready, 4 * i + q + 1)
                    dve.tensor_tensor(flat(hT_lo[:, 2 * q:2 * q + 2, :]), ps[:, bank + q, :],
                                      flat(hT_hi[:, 2 * q:2 * q + 2, :]).bitcast(F32), ALU.subtract).then_inc(done, 1)

            def rotate_in(layer, j):
                n = SCHUNKS * layer + j
                dve.wait_ge(S["bu_ps"], n + 1)
                dve.wait_ge(S["table_done"], 2 * (n + 1))
                if n >= 2:
                    dve.wait_ge(S["rotated"], n - 1)
                t = turn[:, j % 2]
                cos, sin = table[:, j % 2, 0, :], table[:, j % 2, 1, :]
                re, im = ps[:, 4, 0:SEQ], ps[:, 4, SEQ:2 * SEQ]
                own.step(dve.tensor_tensor(t[:, 0, :], re, cos, ALU.mult))
                own.step(dve.tensor_tensor(t[:, 1, :], im, sin, ALU.mult))
                own.step(dve.tensor_tensor(t[:, 2, :], im, cos, ALU.mult))
                dve.tensor_tensor(t[:, 3, :], re, sin, ALU.mult).then_inc(S["turned"], 1)
                own.join()
                own.step(dve.tensor_tensor(t[:, 0, :], t[:, 0, :], t[:, 1, :], ALU.add))
                dve.wait_ge(S["turned"], n + 1)
                own.step(dve.tensor_tensor(t[:, 2, :], t[:, 2, :], t[:, 3, :], ALU.subtract))
                own.join()
                mag = trig[:, 3, j:j + 1].broadcast_to([P, SEQ])
                dve.tensor_tensor_scan(t[:, 1, :], mag, t[:, 0, :], 0.0, ALU.mult, ALU.add).then_inc(S["scanned"], 1)
                dve.tensor_tensor_scan(t[:, 3, :], mag, t[:, 2, :], 0.0, ALU.mult, ALU.add).then_inc(S["scanned"], 1)

            def add_skip(layer, c):
                dve.wait_ge(S["y_ps"], SCHUNKS * layer + 4 * c + 4)
                at = (c % 2) * SEQ
                dve.scalar_tensor_tensor(su[:, c, :], su[:, c, :], par_sb[:, PAR_D + c:PAR_D + c + 1],
                                         ps[:, 5, at:at + SEQ], ALU.mult, ALU.add).then_inc(S["skip_done"], 1)

            def conv(layer):
                u2 = u_t
                for tap in range(3):
                    for c in range(CT):
                        w = par_sb[:, PAR_CW + tap * CT + c:PAR_CW + tap * CT + c + 1]
                        v = v_t[:, c, tap:tap + SEQ]
                        if tap == 0:
                            own.step(dve.tensor_scalar(u2[:, c, :], v, w, None, ALU.mult))
                        else:
                            own.step(dve.scalar_tensor_tensor(u2[:, c, :], v, w, u2[:, c, :], ALU.mult, ALU.add))
                    own.join()
                dve.wait_ge(used, MIX0[layer] + C_AB + 2)
                dve.tensor_tensor(flat(u_t[:, :, :]), flat(u_t[:, :, :]), banks(2, 2), ALU.mult)\
                   .then_inc(S["conv_done"], 1)

            def score(layer, b):
                dve.wait_ge(S["idx_ps"], 2 * layer + b + 1)
                keys = (b + 1) * P
                sc, tmp = scratch[:, 0, 0:keys], scratch[:, 1, 0:keys]
                for h in range(IDX_HEADS):
                    at = (h // 2) * keys
                    src = ps[:, 6 + h % 2, at:at + keys]
                    ins = dve.tensor_scalar(sc if h == 0 else scratch[:, h, 0:keys], src, 0.0,
                                            wi_sb[:, b, h:h + 1], ALU.max, ALU.mult)
                    if h < IDX_HEADS - 1:
                        own.step(ins)
                    else:
                        ins.then_inc(S["scored"], 1)
                own.join()
                dve.wait_ge(S["scored"], 2 * layer + b + 1)
                own.step(dve.tensor_tensor(sc, sc, tmp, ALU.add))
                own.then(dve.tensor_tensor(scratch[:, 2, 0:keys], scratch[:, 2, 0:keys], scratch[:, 3, 0:keys],
                                           ALU.add))
                own.then(dve.tensor_tensor(sc, sc, scratch[:, 2, 0:keys], ALU.add))
                diag = sc[:, b * P:keys]
                own.then(dve.tensor_tensor(diag, diag, causal[:, :], ALU.add))

            def choose(layer, b):
                keys = (b + 1) * P
                sc, work = scratch[:, 0, 0:keys], scratch[:, 1, 0:keys]
                gt, eq = scratch[:, 2, 0:keys], scratch[:, 3, 0:keys]
                src = sc
                for r in range(TOPK // 8):
                    own.then(dve.max(top8[:, :], src))
                    if r < TOPK // 8 - 1:
                        own.then(dve.match_replace(work, top8[:, :], src, DEAD))
                    src = work
                kth = top8[:, 7:8]
                own.step(dve.tensor_scalar(gt, sc, kth, None, ALU.is_gt))
                own.then(dve.tensor_scalar(eq, sc, kth, None, ALU.is_equal))
                own.step(dve.tensor_reduce(smalls[:, 0:1], gt, AX_X, ALU.add))
                own.then(dve.tensor_tensor_scan(work, ones_row(keys), eq, 0.0, ALU.mult, ALU.add))
                own.then(dve.tensor_scalar(smalls[:, 1:2], smalls[:, 0:1], -1.0, float(TOPK), ALU.mult, ALU.add))
                own.then(dve.scalar_tensor_tensor(work, work, smalls[:, 1:2], eq, ALU.is_le, ALU.mult))
                own.then(dve.tensor_tensor(work, work, gt, ALU.add))
                bias = keybias[:, b, 0:keys]
                own.then(dve.tensor_scalar(bias, work, -NEG, NEG, ALU.mult, ALU.add))
                diag = keybias[:, b, b * P:keys]
                own.then(dve.tensor_tensor(diag, diag, causal[:, :], ALU.add))

            def ones_row(width):
                return ones[:, 0:1].broadcast_to([P, width])

            def shift(layer, i):
                n, b = 4 * layer + i, i // 2
                keys = (b + 1) * P
                dve.wait_ge(S["logit_ps"], n + 1)
                dst = probs[:, :, 0:keys]
                bias = keybias[:, b:b + 1, 0:keys].broadcast_to([P, 2, keys])
                for odd in range(2):
                    src = ps[:, 6 + odd, 0:2 * keys].rearrange("p (h k) -> p h k", h=2)
                    own.step(dve.scalar_tensor_tensor(dst[:, 2 * odd:2 * odd + 2, :], src, HD ** -0.5, bias,
                                                      ALU.mult, ALU.add))
                own.join()
                own.then(dve.tensor_reduce(rowinv[:, :], dst, AX_X, ALU.max))
                dve.tensor_scalar(rowmax[:, :], rowinv[:, :], -1.0, None, ALU.mult).then_inc(S["shifted"], 1)

            def normalise(layer, i):
                n, keys = 4 * layer + i, (i // 2 + 1) * P
                dve.wait_ge(S["exp_done"], 4 * (n + 1))
                own.then(dve.reciprocal(rowinv[:, :], rowsum[:, :]))
                dst = probs[:, :, 0:keys]
                dve.tensor_tensor(dst, dst, rowinv[:, :].unsqueeze(2).broadcast_to([P, 4, keys]), ALU.mult)\
                   .then_inc(S["prob_done"], 1)

            def yc_lo(layer, i):
                n, b, g = 4 * layer + i, i // 2, i % 2
                dve.wait_ge(S["yc_hi_done"], n + 1)
                at = slice(b * P, (b + 1) * P)
                dve.tensor_tensor(yac_lo[:, 2 * g:2 * g + 2, at], ps[:, 6, 0:2 * P].rearrange("p (a n) -> p a n", a=2),
                                  yac_hi[:, 2 * g:2 * g + 2, at].bitcast(F32), ALU.subtract).then_inc(S["yc_lo_done"], 1)

            def merge(layer, branch, c):
                dve.wait_ge(used, MIX0[layer] + c + 2)
                dve.wait_ge(S["gate_done"], 6 * layer + 2 * (branch + 1))
                y = banks(0, 4)
                if branch == 0:
                    dve.tensor_tensor(flat(mixed[:, :, :]), flat(gate[:, :, :]), y, ALU.mult).then_inc(S["gated"], 1)
                    return
                dve.tensor_tensor(flat(gate[:, :, :]), flat(gate[:, :, :]), y, ALU.mult).then_inc(S["gated"], 1)
                dve.wait_ge(S["gated"], 3 * layer + branch + 1)
                if branch == 2:
                    dve.wait_ge(S["mixed_done"], 2 * layer + 1)
                dve.tensor_tensor(flat(mixed[:, :, :]), flat(mixed[:, :, :]), flat(gate[:, :, :]), ALU.add)\
                   .then_inc(S["mixed_done"], 1)

            def sub_hi(dst, whole, hi, done):
                dve.tensor_tensor(dst, whole, hi.bitcast(F32), ALU.subtract).then_inc(done, 1)

            def mixer(layer):
                c0 = MIX0[layer]
                chunk = lambda c: split_lo(dve, c0 + c, width=mix_width(layer, c))
                turn_j = lambda j: rotate_in(layer, j)
                dve.wait_ge(S["den_done"], layer + 1)
                dve.reciprocal(trig[:, 20, :], trig[:, 19, :]).then_inc(S["den_inv"], 1)
                chunk(0)
                norm(2 * layer, gain_row)
                chunk(1)
                chunk(2)
                dve.wait_ge(S["hT_hi_done"], 4 * (2 * layer + 1))
                turned_lo(2 * layer, S["hT_ps"], 0, S["hT_lo_done"])
                chunk(3)
                chunk(4)
                chunk(5)
                turn_j(0)
                chunk(6)
                turn_j(1)
                chunk(7)
                turn_j(2)
                chunk(8)
                turn_j(3)
                chunk(9)
                dve.wait_ge(S["sq_done"], layer + 1)
                own.then(dve.tensor_reduce(qk_ss[:, 2, :, :], gate_sq, AX_X, ALU.add))
                dve.tensor_scalar(qk_ss[:, 0, :, :], qk_ss[:, 2, :, :], 1.0 / HD, EPS, ALU.mult, ALU.add)\
                   .then_inc(S["qk_ss_done"], 1)
                chunk(10)
                turn_j(4)
                dve.wait_ge(S["qk_std_done"], layer + 1)
                dve.reciprocal(qk_ss[:, 2, :, :], qk_ss[:, 1, :, :]).then_inc(S["qk_inv_done"], 1)
                chunk(11)
                add_skip(layer, 0)
                turn_j(5)
                chunk(12)
                own.then(dve.memset(v_t[:, :, 0:2], 0.0))
                dve.wait_ge(used, c0 + C_AC + 2)
                dve.wait_ge(S["u_copied"], layer + 1)
                dve.tensor_tensor(v_t[:, :, 2:SEQ + 2], u_t[:, :, :],
                                  banks(0, 2).rearrange("p (c n) -> p c n", c=CT), ALU.mult).then_inc(S["v_made"], 1)
                chunk(13)
                turn_j(6)
                dve.wait_ge(S["v_made"], layer + 1)
                chunk(14)
                turn_j(7)
                conv(layer)
                chunk(15)
                dve.wait_ge(S["ya_hi_done"], layer + 1)
                sub_hi(flat(yac_lo[:, :, :]), flat(u_t[:, :, :]), flat(yac_hi[:, :, :]), S["ya_lo_done"])
                chunk(16)
                turn_j(8)
                score(layer, 0)
                choose(layer, 0)
                chunk(17)
                add_skip(layer, 1)
                turn_j(9)
                chunk(18)
                score(layer, 1)
                chunk(19)
                choose(layer, 1)
                turn_j(10)
                chunk(20)
                shift(layer, 0)
                merge(layer, 0, C_OA)
                turn_j(11)
                normalise(layer, 0)
                chunk(21)
                chunk(22)
                turn_j(12)
                yc_lo(layer, 0)
                shift(layer, 1)
                normalise(layer, 1)
                chunk(23)
                add_skip(layer, 2)
                turn_j(13)
                chunk(24)
                for i in (1, 2, 3):
                    yc_lo(layer, i)
                    if i < 3:
                        shift(layer, i + 1)
                        normalise(layer, i + 1)
                chunk(25)
                turn_j(14)
                chunk(26)
                turn_j(15)
                merge(layer, 1, C_OC)
                chunk(27)
                add_skip(layer, 3)
                chunk(28)
                dve.wait_ge(S["yg_hi_done"], layer + 1)
                sub_hi(flat(yb_lo[:, :, :]), flat(su[:, :, :]), flat(yb_hi[:, :, :]), S["yg_lo_done"])
                chunk(29)
                chunk(30)
                dve.wait_ge(S["glu_sig"], layer + 1)
                dve.tensor_tensor(flat(su[:, :, :]), flat(su[:, :, :]), flat(u_t[:, :, :]), ALU.mult)\
                   .then_inc(S["yb_made"], 1)
                dve.wait_ge(S["yb_hi_done"], layer + 1)
                sub_hi(flat(yb_lo[:, :, :]), flat(su[:, :, :]), flat(yb_hi[:, :, :]), S["yb_lo_done"])
                chunk(31)
                chunk(32)
                chunk(33)
                merge(layer, 2, C_OB)
                dve.wait_ge(S["mixT_hi_done"], 4 * (layer + 1))
                turned_lo(layer, S["mixT_ps"], 4, S["mixT_lo_done"])
                chunk(34)
                add_x(c0 + MIX_CHUNKS, 0)

            def add_x(after, bank):
                dve.wait_ge(used, after)
                dve.tensor_tensor(flat(x_tok[:, :, :]), flat(x_tok[:, :, :]), banks(bank, 4), ALU.add)\
                   .then_inc(S["x_added"], 1)

            def times_up(sil_seen, w3_used, turned, width=HALF):
                dve.wait_ge(S["sil_done"], sil_seen)
                dve.wait_ge(used, w3_used)
                if turned is not None:
                    dve.wait_ge(S["hidT_ps"], turned)
                dve.tensor_tensor(hid[:, 0:width], sil[:, 0:width], ps[:, 1, 0:width], ALU.mult)\
                   .then_inc(S["hid_done"], 1)

            def hidden_lo(seen, bank):
                dve.wait_ge(S["hidT_hi_done"], seen)
                dve.tensor_tensor(hidT_lo[:, :], ps[:, bank, :], hidT_hi[:, :].bitcast(F32), ALU.subtract)\
                   .then_inc(S["hidT_lo_done"], 1)

            def dense():
                n = DENSE0
                split_lo(dve, n)
                split_lo(dve, n + 1)
                norm(1, gain_ff[:, :])
                split_lo(dve, n + 2)
                dve.wait_ge(S["hT_hi_done"], 8)
                turned_lo(1, S["hT_ps"], 0, S["hT_lo_done"])
                split_lo(dve, n + 3)
                split_lo(dve, n + 4)
                times_up(1, n + 2, None)
                split_lo(dve, n + 5)
                hidden_lo(1, 2)
                split_lo(dve, n + 6)
                with dve.Fori(0, (DENSE_STRIPES - 3) // 2) as t:
                    hi_at = [dve.snap(n + 7 + k + 1 + 6 * t) for k in range(6)]
                    w3_at = [dve.snap(n + 4 + 3 * h + 6 * t) for h in range(2)]
                    i_at = [dve.snap(2 * t + k) for k in range(1, 4)]
                    for h in range(2):
                        m = n + 7 + 3 * h
                        times_up(i_at[h + 1], w3_at[h], i_at[h])
                        split_lo(dve, m, hi_at[3 * h])
                        split_lo(dve, m + 1, hi_at[3 * h + 1])
                        hidden_lo(i_at[h + 1], 2)
                        split_lo(dve, m + 2, hi_at[3 * h + 2])
                m = n + 7 + 6 * ((DENSE_STRIPES - 3) // 2)
                i = DENSE_STRIPES - 2
                times_up(i + 1, m - 3, i)
                split_lo(dve, m)
                split_lo(dve, m + 1)
                hidden_lo(i + 1, 2)
                times_up(i + 2, m, i + 1)
                hidden_lo(i + 2, 2)
                add_x(n + DENSE_CHUNKS, 4)

            def route():
                norm(3, gain_ff[:, :])
                dve.wait_ge(S["hT_hi_done"], 16)
                turned_lo(3, S["hT_ps"], 0, S["hT_lo_done"])
                for b in range(BLOCKS):
                    dve.wait_ge(S["h_hi_done"], b + 1)
                    dve.tensor_tensor(h_lo[:, b, :], h_tok[:, b, :], h_hi[:, b, :].bitcast(F32), ALU.subtract)\
                       .then_inc(S["h_lo_done"], 1)
                dve.wait_ge(S["logits_ps"], 1)
                lg, shifted_l, ex, gt, eq, rank, keep, sel, tmp = (rt[:, k] for k in range(9))
                own.then(dve.tensor_copy(flat(lg), ps[:, 4, 0:16]))
                for b in range(BLOCKS):
                    own.step(dve.max(rt8[:, b, :], lg[:, b, :]))
                own.join()
                for b in range(BLOCKS):
                    own.step(dve.tensor_scalar(gt[:, b, :], lg[:, b, :], rt8[:, b, 1:2], None, ALU.is_gt))
                    own.step(dve.tensor_scalar(eq[:, b, :], lg[:, b, :], rt8[:, b, 1:2], None, ALU.is_equal))
                    own.step(dve.tensor_scalar(shifted_l[:, b, :], lg[:, b, :], rt8[:, b, 0:1], None, ALU.subtract))
                own.join()
                dve.tensor_reduce(rts[:, 0, :], gt, AX_X, ALU.add).then_inc(S["top_r"], 1)
                for b in range(BLOCKS):
                    own.step(dve.tensor_tensor_scan(rank[:, b, :], ones_row(EXPERTS), eq[:, b, :], 0.0, ALU.mult,
                                                    ALU.add))
                dve.wait_ge(S["top_r"], 1)
                own.then(dve.tensor_scalar(rts[:, 1, :], rts[:, 0, :], -1.0, 2.0, ALU.mult, ALU.add))
                for b in range(BLOCKS):
                    own.step(dve.scalar_tensor_tensor(keep[:, b, :], rank[:, b, :], rts[:, 1, b:b + 1], eq[:, b, :],
                                                      ALU.is_le, ALU.mult))
                own.join()
                dve.tensor_tensor(flat(sel), flat(keep), flat(gt), ALU.add).then_inc(S["picked"], 1)
                dve.wait_ge(S["picked"], 1)
                dve.wait_ge(S["exp_r"], 1)
                own.then(dve.tensor_tensor(flat(tmp), flat(ex), flat(sel), ALU.mult))
                own.then(dve.tensor_reduce(rts[:, 2, :], tmp, AX_X, ALU.add))
                own.then(dve.reciprocal(rts[:, 3, :], rts[:, 2, :]))
                for b in range(BLOCKS):
                    own.step(dve.tensor_scalar(gate_of[:, b, :], tmp[:, b, :], rts[:, 3, b:b + 1], None, ALU.mult))
                dve.wait_ge(S["rank_ps"], 1)
                own.step(dve.tensor_reduce(most[:, :], ps[:, 5, 16:24], AX_X, ALU.max))
                dve.memset(slot_of[:, :, :], -1.0).then_inc(S["acc_done"], 1)
                dve.wait_ge(S["acc_done"], 1)
                own.then(dve.tensor_tensor(flat(rank), ps[:, 5, 0:16], flat(sel), ALU.mult))
                dve.tensor_scalar(slot_of[:, :, 0:EXPERTS], rank, -1.0, None, ALU.add).then_inc(S["slots_done"], 1)
                dve.wait_ge(S["slots_done"], 1)
                dve.tensor_copy(most_i[:, :], most[0:1, :]).then_inc(S["most_done"], 1)

            def pick_slots(e, rnd):
                for b in range(BLOCKS):
                    dve.tensor_scalar(pick[:, b, :], slot_id[:, rnd, :], slot_of[:, b, bass.ds(e, 1)], None,
                                      ALU.is_equal).then_inc(S["pick_done"], 1)

            def experts(rnd):
                n0 = MOE0 + rnd * EXPERTS * MOE_CHUNKS
                e0 = rnd * EXPERTS
                i0 = DENSE_STRIPES + e0 * MOE_STRIPES

                def lo(n, turns):
                    split_lo(dve, n, value(dve, n + 1 + 6 * turns))

                def xg(e):
                    seen = value(dve, 2 * (e0 + e + 1))
                    dve.wait_ge(S["gather_ps"], seen)
                    dve.tensor_copy(flat(xg_lo[:, :, :]), banks(6, 2)).then_inc(S["xg_lo_done"], 1)

                def stripe(i, t, turns):
                    prev, this = value(dve, i + t), value(dve, i + t + 1)
                    w3_at = value(dve, n0 + 8 + 6 * turns)
                    lo(n0 + 6, turns)
                    hidden_lo(prev, 4)
                    lo(n0 + 7, turns)
                    lo(n0 + 8, turns)
                    lo(n0 + 9, turns)
                    times_up(this, w3_at, prev)

                def y(e, y_used):
                    e_at = value(dve, e0 + e + 1)
                    dve.wait_ge(used, y_used)
                    dve.wait_ge(S["y_hi_done"], e_at)
                    dve.tensor_tensor(y_lo[:, :], banks(2, 2), y_hi[:, :].bitcast(F32), ALU.subtract)\
                       .then_inc(S["y_lo_done"], 1)

                def add_to_x(e):
                    e_at, a_at = value(dve, e0 + e + 1), value(dve, 4 * (e0 + e) + 1)
                    dve.wait_ge(S["scatter_ps"], e_at)
                    dve.wait_ge(S["acc_done"], a_at)
                    for b in range(BLOCKS):
                        for half in range(2):
                            dst = x_tok[:, b, half * HALF:(half + 1) * HALF]
                            dve.scalar_tensor_tensor(dst, ps[:, 2 + half if b == 0 else 6 + half, :],
                                                     gate_of[:, b, bass.ds(e, 1)], dst, ALU.mult, ALU.add)\
                               .then_inc(S["acc_done"], 1)

                def expert(e, last):
                    i = i0 + MOE_STRIPES * e
                    turns = MOE_STRIPES * e
                    stripe(i, 1, turns)
                    lo(n0 + 10, turns)
                    if not last:
                        e_at = value(dve, e0 + e + 1)
                        dve.wait_ge(S["pickT_ps"], e_at)
                        pick_slots(value(dve, e + 1), rnd)
                    lo(n0 + 11, turns)
                    with dve.Fori(2, MOE_STRIPES - 1) as t:
                        stripe(i, t, turns + t - 1)
                        lo(n0 + 10, turns + t - 1)
                        lo(n0 + 11, turns + t - 1)
                    t = MOE_STRIPES - 1
                    stripe(i, t, turns + t - 1)
                    lo(n0 + 10, turns + t - 1)
                    if not last:
                        xg(e + 1)
                    lo(n0 + 11, turns + t - 1)
                    if last:
                        hidden_lo(i + t + 1, 4)
                        y(e, n0 + 6 + 6 * (turns + t))
                        add_to_x(e)
                        return
                    turned, y_used = value(dve, i + t + 1), value(dve, n0 + 8 + 6 * (turns + t))
                    next_i, w3_at = value(dve, i + t + 2), value(dve, n0 + 10 + 6 * (turns + t))
                    lo(n0 + 6, turns + t)
                    hidden_lo(turned, 4)
                    lo(n0 + 7, turns + t)
                    lo(n0 + 8, turns + t)
                    lo(n0 + 9, turns + t)
                    y(e, y_used)
                    lo(n0 + 10, turns + t)
                    times_up(next_i, w3_at, turned)
                    lo(n0 + 11, turns + t)
                    add_to_x(e)

                dve.wait_ge(S["slots_loaded"], 16)
                pick_slots(0, rnd)
                lo(n0, 0)
                xg(0)
                for k in range(1, 5):
                    lo(n0 + k, 0)
                times_up(i0 + 1, n0 + 4, i0)
                lo(n0 + 5, 0)
                with dve.Fori(0, EXPERTS - 1) as e:
                    expert(e, False)
                expert(EXPERTS - 1, True)

            gate_sq = flat(gate[:, :, :]).rearrange("p (b h d) -> p b h d", b=BLOCKS, d=HD)[:, :, 0:10, :]
            mixer(0)
            dense()
            mixer(1)
            route()
            experts(0)
            dve.wait_ge(S["most_done"], 1)
            most_tokens = dve.value_load(most_i[0:1, 0:1])
            with dve.If(most_tokens > SLOTS):
                experts(1)
                dve.wait_ge(S["acc_done"], 4 * 2 * EXPERTS + 1)
            dve.wait_ge(S["acc_done"], 4 * EXPERTS + 1)
            dve.tensor_copy(most[:, :], ones[:, 0:1]).then_inc(S["final_done"], 1)

        @block.gpsimd
        def _(pool):
            own = Chain(pool, pool_step)

            def constants():
                for t in (ident, upper, causal):
                    own.step(pool.memset(t[:, :], 1.0 if t is upper else 0.0))
                pool.memset(ones[:, :], 1.0).then_inc(S["consts"], 1)
                pool.memset(zero_r[:, :].bitcast(F32), 0.0).then_inc(S["consts"], 1)
                own.join()
                pool.affine_select(out=ident[:, :], in_=ident[:, :], compare_op=ALU.not_equal, fill=1.0, base=0,
                                   pattern=[[-1, P]], channel_multiplier=1).then_inc(S["consts"], 1)
                pool.affine_select(out=upper[:, :], in_=upper[:, :], compare_op=ALU.is_ge, fill=0.0, base=0,
                                   pattern=[[1, P]], channel_multiplier=-1).then_inc(S["consts"], 1)
                pool.affine_select(out=causal[:, :], in_=causal[:, :], compare_op=ALU.is_ge, fill=NEG, base=0,
                                   pattern=[[-1, P]], channel_multiplier=1).then_inc(S["consts"], 1)

            def load_gain(i, dst):
                pool.dma_start(dst, gains[i].partition_broadcast(P)).then_inc(S["gain_loaded"], 16)

            def tt(o, a, b, op):
                own.then(pool.tensor_tensor(o, a, b, op))

            def ts(o, a, c1, op1, c2=None, op2=None):
                own.then(pool.tensor_scalar(o, a, c1, c2, op1, op2) if op2 is not None else
                         pool.tensor_scalar(o, a, c1, None, op1))

            def discretise(layer):
                lr, dt, lrdt, mag, k, r, r2, sn, cs, m, m2, cq, sq, t1, t2, sin, cos, nr, ni, den, inv, cre, cim, ang\
                    = (trig[:, i, :] for i in range(24))
                li = par_sb[:, PAR_LIM:PAR_LIM + SCHUNKS]
                ts(lr, par_sb[:, PAR_LRE:PAR_LRE + SCHUNKS], -1e-4, ALU.min)
                pool.wait_ge(S["dt_exp"], layer + 1)
                pool.tensor_tensor(lrdt, lr, dt, ALU.mult).then_inc(S["lrdt_done"], 1)
                tt(t1, lr, lr, ALU.mult)
                tt(t2, li, li, ALU.mult)
                pool.tensor_tensor(den, t1, t2, ALU.add).then_inc(S["den_done"], 1)
                tt(ang, li, dt, ALU.mult)
                ts(k, ang, 2.0 / float(np.pi), ALU.mult)
                ts(k, k, MAGIC, ALU.add)
                ts(k, k, -MAGIC, ALU.add)
                ts(t1, k, -PIO2[0], ALU.mult)
                tt(r, ang, t1, ALU.add)
                for part in PIO2[1:]:
                    ts(t1, k, -part, ALU.mult)
                    tt(r, r, t1, ALU.add)
                tt(r2, r, r, ALU.mult)
                ts(sn, r2, 1.0 / 362880, ALU.mult, -1.0 / 5040, ALU.add)
                for c in (1.0 / 120, -1.0 / 6, 1.0):
                    tt(sn, sn, r2, ALU.mult)
                    ts(sn, sn, c, ALU.add)
                tt(sn, sn, r, ALU.mult)
                ts(cs, r2, -1.0 / 3628800, ALU.mult, 1.0 / 40320, ALU.add)
                for c in (-1.0 / 720, 1.0 / 24, -0.5, 1.0):
                    tt(cs, cs, r2, ALU.mult)
                    ts(cs, cs, c, ALU.add)
                ts(m, k, 0.25, ALU.mult)
                ts(m, m, MAGIC, ALU.add)
                ts(m, m, -MAGIC, ALU.add, -4.0, ALU.mult)
                tt(m, m, k, ALU.add)
                tt(m2, m, m, ALU.mult)
                ts(cq, m2, 0.0, ALU.is_equal)
                ts(t1, m2, 4.0, ALU.is_equal)
                tt(cq, cq, t1, ALU.subtract)
                ts(sq, m2, 1.0, ALU.is_equal)
                tt(sq, sq, m, ALU.mult)
                tt(t1, cs, cq, ALU.mult)
                tt(t2, sn, sq, ALU.mult)
                tt(cos, t1, t2, ALU.subtract)
                tt(t1, sn, cq, ALU.mult)
                tt(t2, cs, sq, ALU.mult)
                tt(sin, t1, t2, ALU.add)
                pool.wait_ge(S["mag_exp"], layer + 1)
                tt(nr, mag, cos, ALU.mult)
                ts(nr, nr, -1.0, ALU.add)
                tt(ni, mag, sin, ALU.mult)
                tt(t1, nr, lr, ALU.mult)
                tt(t2, ni, li, ALU.mult)
                tt(cre, t1, t2, ALU.add)
                tt(t1, ni, lr, ALU.mult)
                tt(t2, nr, li, ALU.mult)
                tt(cim, t1, t2, ALU.subtract)
                pool.wait_ge(S["den_inv"], layer + 1)
                tt(cre, cre, inv, ALU.mult)
                tt(cim, cim, inv, ALU.mult)
                c_re, c_im = (par_sb[:, o:o + SCHUNKS * 32].rearrange("p (j c) -> p j c", c=32)
                              for o in (PAR_CRE, PAR_CIM))
                ta, tb = (table[:, i, :, :].rearrange("p a (j c) -> p (a j) c", c=32) for i in range(2))
                tc = pool_t[:, :, :].rearrange("p a (j c) -> p (a j) c", c=32)
                kr, ki = (v.unsqueeze(2).broadcast_to([P, SCHUNKS, 32]) for v in (cre, cim))
                tt(ta, c_re, kr, ALU.mult)
                tt(tb, c_im, ki, ALU.mult)
                tt(tc, c_re, ki, ALU.mult)
                tt(c_im, c_im, kr, ALU.mult)
                tt(c_re, ta, tb, ALU.subtract)
                tt(c_im, c_im, tc, ALU.add)
                ts(c_im, c_im, -1.0, ALU.mult)
                powers(pow_b, cos, sin, t1, t2, nr, ni)
                powers(pow_a, cos, sin, t1, t2, nr, ni)

            def powers(dst, wr, wi, t1, t2, nr, ni):
                own.step(pool.memset(dst[:, 0, 0, :], 1.0))
                own.then(pool.memset(dst[:, 1, 0, :], 0.0))
                n = 1
                while n < 16:
                    a_r, a_i = dst[:, 0, 0:n, :], dst[:, 1, 0:n, :]
                    b_r, b_i = dst[:, 0, n:2 * n, :], dst[:, 1, n:2 * n, :]
                    w_r, w_i = (w.unsqueeze(1).broadcast_to([P, n, SCHUNKS]) for w in (wr, wi))
                    s1 = pool_t[:, 0, 0:n * SCHUNKS].rearrange("p (n j) -> p n j", n=n)
                    s2 = pool_t[:, 1, 0:n * SCHUNKS].rearrange("p (n j) -> p n j", n=n)
                    tt(s1, a_r, w_r, ALU.mult)
                    tt(s2, a_i, w_i, ALU.mult)
                    tt(b_r, s1, s2, ALU.subtract)
                    tt(s1, a_r, w_i, ALU.mult)
                    tt(s2, a_i, w_r, ALU.mult)
                    tt(b_i, s1, s2, ALU.add)
                    tt(t1, wr, wr, ALU.mult)
                    tt(t2, wi, wi, ALU.mult)
                    tt(ni, wr, wi, ALU.mult)
                    tt(wr, t1, t2, ALU.subtract)
                    ts(wi, ni, 2.0, ALU.mult)
                    n *= 2

            def make_table(layer, j):
                n = SCHUNKS * layer + j
                if n >= 2:
                    pool.wait_ge(S["turned"], n - 1)
                a_r, a_i = (pow_a[:, i, :, j:j + 1].broadcast_to([P, 16, 16]) for i in range(2))
                b_r, b_i = (pow_b[:, i, :, j].unsqueeze(1).broadcast_to([P, 16, 16]) for i in range(2))
                cos, sin = (table[:, j % 2, i, :].rearrange("p (a b) -> p a b", a=16) for i in range(2))
                s1, s2 = (pool_t[:, i, :].rearrange("p (a b) -> p a b", a=16) for i in range(2))
                own.step(pool.tensor_tensor(s1, a_r, b_r, ALU.mult))
                own.then(pool.tensor_tensor(s2, a_i, b_i, ALU.mult))
                pool.tensor_tensor(cos, s1, s2, ALU.subtract).then_inc(S["table_done"], 1)
                pool.wait_ge(S["table_done"], 2 * n + 1)
                own.step(pool.tensor_tensor(s1, a_r, b_i, ALU.mult))
                own.then(pool.tensor_tensor(s2, a_i, b_r, ALU.mult))
                pool.tensor_tensor(sin, s1, s2, ALU.add).then_inc(S["table_done"], 1)
                pool.wait_ge(S["table_done"], 2 * n + 2)

            def rotate_out(layer, j):
                n = SCHUNKS * layer + j
                pool.wait_ge(S["scanned"], 2 * (n + 1))
                if n >= 1:
                    pool.wait_ge(S["y_ps"], n)
                g_re, g_im = turn[:, j % 2, 1, :], turn[:, j % 2, 3, :]
                cos, sin = table[:, j % 2, 0, :], table[:, j % 2, 1, :]
                own.step(pool.tensor_tensor(pool_t[:, 0, :], g_re, cos, ALU.mult))
                own.then(pool.tensor_tensor(pool_t[:, 1, :], g_im, sin, ALU.mult))
                own.then(pool.tensor_tensor(state[:, 0, :], pool_t[:, 0, :], pool_t[:, 1, :], ALU.subtract))
                own.step(pool.tensor_tensor(pool_t[:, 0, :], g_re, sin, ALU.mult))
                own.then(pool.tensor_tensor(pool_t[:, 1, :], g_im, cos, ALU.mult))
                pool.tensor_tensor(state[:, 1, :], pool_t[:, 0, :], pool_t[:, 1, :], ALU.add).then_inc(S["rotated"], 1)
                pool.wait_ge(S["rotated"], n + 1)

            def square(layer):
                pool.wait_ge(S["q_copied"], layer + 1)
                pool.wait_ge(S["kv_copied"], 7 * (layer + 1))
                heads = qk[:, :, 0:10, :]
                tmp = flat(gate[:, :, :]).rearrange("p (b h d) -> p b h d", b=BLOCKS, d=HD)[:, :, 0:10, :]
                pool.tensor_tensor(tmp, heads, heads, ALU.mult).then_inc(S["sq_done"], 1)

            def norm_and_rope(layer):
                pool.wait_ge(S["qk_inv_done"], layer + 1)
                heads = qk[:, :, 0:10, :]
                tt(heads, heads, qk_ss[:, 2, :, :].unsqueeze(3).broadcast_to([P, BLOCKS, 10, HD]), ALU.mult)
                gain = par_sb[:, PAR_GAIN:PAR_GAIN + 10 * HD].unsqueeze(1).broadcast_to([P, BLOCKS, 10 * HD])
                part = h_tok[:, :, 0:10 * HD]
                tt(part, part, gain, ALU.mult)
                if layer == 0:
                    pool.wait_ge(S["rope_loaded"], 16)
                for b in range(BLOCKS):
                    xv = h_tok[:, b, :].rearrange("p (h i d) -> p h i d", i=2, d=32)
                    tv = gate[:, b, :].rearrange("p (h i d) -> p h i d", i=2, d=32)
                    for i in range(2):
                        sin = rope_sb[:, b, 1 + i, :].unsqueeze(1).broadcast_to([P, 16, 32])
                        own.step(pool.tensor_tensor(tv[:, :, i, :], xv[:, :, 1 - i, :], sin, ALU.mult))
                    own.join()
                    cos = rope_sb[:, b, 0:1, :].broadcast_to([P, 32, 32])
                    x3 = h_tok[:, b, :].rearrange("p (h d) -> p h d", d=32)
                    tt(x3, x3, cos, ALU.mult)
                    pool.tensor_tensor(h_tok[:, b, :], h_tok[:, b, :], gate[:, b, :], ALU.add)\
                        .then_inc(S["rope_done"], 1)

            def mixer(layer):
                make_table(layer, 0)
                make_table(layer, 1)
                for j in range(SCHUNKS):
                    if j == 2:
                        square(layer)
                    if j == 4:
                        norm_and_rope(layer)
                    rotate_out(layer, j)
                    if j + 2 < SCHUNKS:
                        make_table(layer, j + 2)

            pool.dma_start(par_sb[:, :], par[0]).then_inc(S["par_loaded"], 16)
            load_gain(0, gain_row)
            constants()
            pool.wait_ge(S["par_loaded"], 16)
            discretise(0)
            mixer(0)
            pool.wait_ge(S["mixed_done"], 2)
            load_gain(1, gain_ff[:, :])
            pool.wait_ge(S["x_added"], 1)
            pool.dma_start(par_sb[:, :], par[1]).then_inc(S["par_loaded"], 16)
            pool.wait_ge(S["par_loaded"], 32)
            discretise(1)
            pool.wait_ge(S["x_added"], 2)
            load_gain(2, gain_row)
            mixer(1)
            pool.wait_ge(S["mixed_done"], 4)
            load_gain(3, gain_ff[:, :])
            pool.wait_ge(S["x_added"], 3)
            pool.dma_start(router_sb[:, :, :], router_w[0].rearrange("(k p) e -> p k e", p=P))\
                .then_inc(S["router_loaded"], 16)
            pool.dma_start(slot_id[:, :, :], slot_ids.rearrange("p (r s) -> p r s", r=2)).then_inc(S["slots_loaded"], 16)


def rope_rows():
    pos = np.arange(SEQ, dtype=np.float32)
    inv = np.float32(10000.0) ** (-np.arange(HD // 2, dtype=np.float32) / np.float32(HD // 2))
    ang = (pos[:, None] * inv[None, :].astype(np.float32)).astype(np.float32)
    t = np.stack([np.cos(ang), -np.sin(ang), np.sin(ang)], 1).astype(np.float32)
    return np.ascontiguousarray(t.reshape(BLOCKS, P, 3, HD // 2).transpose(1, 0, 2, 3))


def small_parameters(i):
    groups = SSM // GROUP
    out = np.zeros((DEPTH, P, PAR_W), np.float32)
    states = lambda a: a.reshape(DEPTH, SCHUNKS, P).transpose(0, 2, 1)
    out[:, :, PAR_LRE:PAR_LRE + SCHUNKS] = states(i["ssm_lam_re"])
    out[:, :, PAR_LIM:PAR_LIM + SCHUNKS] = states(i["ssm_lam_im"])
    out[:, :, PAR_LDT:PAR_LDT + SCHUNKS] = states(np.repeat(i["ssm_log_dt"][:, :, None], STATE, 2))
    out[:, :, PAR_CW:PAR_CW + 3 * CT] = i["conv_w"].reshape(DEPTH, 3 * CT, P).transpose(0, 2, 1)
    out[:, :, PAR_D:PAR_D + CT] = i["ssm_d"].reshape(DEPTH, CT, P).transpose(0, 2, 1)
    gain = np.concatenate([np.tile(i["q_norm_g"], (1, HEADS)), np.tile(i["k_norm_g"], (1, 2))], 1)
    out[:, :, PAR_GAIN:PAR_GAIN + 10 * HD] = gain[:, None, :]
    c_re = out[:, :, PAR_CRE:PAR_CRE + SCHUNKS * 32].reshape(DEPTH, P, SCHUNKS, 32)
    c_im = np.zeros_like(c_re)
    c_re = np.zeros_like(c_re)
    b = np.zeros((DEPTH, P, CT, 2, P), np.float32)
    for g in range(groups):
        j, odd = g // 2, g % 2
        rows = slice(STATE * odd, STATE * odd + STATE)
        cols = slice(GROUP * odd, GROUP * odd + GROUP)
        c_re[:, rows, j, cols] = i["ssm_c_re"][:, g].transpose(0, 2, 1)
        c_im[:, rows, j, cols] = i["ssm_c_im"][:, g].transpose(0, 2, 1)
        at = slice(32 * (j % 4) + GROUP * odd, 32 * (j % 4) + GROUP * odd + GROUP)
        b[:, at, j // 4, 0, rows] = i["ssm_b_re"][:, g].transpose(0, 2, 1)
        b[:, at, j // 4, 1, rows] = i["ssm_b_im"][:, g].transpose(0, 2, 1)
    out[:, :, PAR_CRE:PAR_CRE + SCHUNKS * 32] = c_re.reshape(DEPTH, P, -1)
    out[:, :, PAR_CIM:PAR_CIM + SCHUNKS * 32] = c_im.reshape(DEPTH, P, -1)
    out[:, :, PAR_B:PAR_W] = b.reshape(DEPTH, P, -1)
    return out


def kernel(**inputs):
    import concourse.bacc as bacc
    from concourse.bass_utils import run_bass_kernel_spmd

    i = {name: np.asarray(a) for name, a in inputs.items()}
    slots = np.broadcast_to(np.arange(2 * P, dtype=np.float32), (P, 2 * P))
    arrays = {
        "x": i["x"], "gains": np.stack([i["ln1_g"], i["ln2_g"]], 1).reshape(2 * DEPTH, D), "w_in": i["w_in"],
        "par": small_parameters(i), "w_glu": i["ssm_w_glu"], "w_out_a": i["w_out_a"], "w_out_b": i["w_out_b"],
        "w_out_c": i["w_out_c"], "w_o": i["w_o"], "rope": rope_rows(), "slot_ids": slots, "ffn_w1": i["ffn_w1"],
        "ffn_w3": i["ffn_w3"], "ffn_w2": i["ffn_w2"], "router_w": i["router_w"], "moe_w1": i["moe_w1"],
        "moe_w3": i["moe_w3"], "moe_w2": i["moe_w2"],
    }
    arrays = {name: np.ascontiguousarray(a) for name, a in arrays.items()}
    nc = bacc.Bacc("TRN2", target_bir_lowering=False, num_devices=1)
    args = {name: nc.dram_tensor(name, a.shape, F32, kind="ExternalInput").ap() for name, a in arrays.items()}
    out = nc.dram_tensor("out", (1, SEQ, D), F32, kind="ExternalOutput").ap()
    trunk(nc, **args, out=out)
    result = run_bass_kernel_spmd(nc, [arrays], core_ids=[0])
    return result.results[0]["out"]
```

```python
from contextlib import ExitStack

import numpy as np
import concourse.bass as bass
from concourse import mybir

ALU = mybir.AluOpType
ACT = mybir.ActivationFunctionType
F32 = mybir.dt.float32
F32R = mybir.dt.float32r
I32 = mybir.dt.int32
AX_X = mybir.AxisListType.X

P = 128
D = 1024
SEQ = 256
BLOCKS = SEQ // P
DEPTH = 2
KD = D // P
CONV = 512
SSM = 512
CT = CONV // P
GROUP = 16
STATE = 64
SCHUNKS = (SSM // GROUP) * STATE // P
HEADS = 8
HD = 64
IDX_HEADS = 4
TOPK = min(256, SEQ // 4)
FF_DENSE = 2816
EXPERTS = 8
FF_EXPERT = 3584
EPS = 1e-6
SLOTS = P
NEG = -1e30
DEAD = -3e38
HALF = 512

CHUNK = 2048
RAW = 6
SPLIT = 3
DENSE_W = 256
DENSE_STRIPES = FF_DENSE // DENSE_W
MOE_STRIPES = FF_EXPERT // HALF
MIX_CHUNKS = 35
DENSE_CHUNKS = 3 * DENSE_STRIPES
MOE_CHUNKS = 6 * MOE_STRIPES
MIX0 = [0, MIX_CHUNKS + DENSE_CHUNKS]
DENSE0 = MIX_CHUNKS
MOE0 = 2 * MIX_CHUNKS + DENSE_CHUNKS
C_KV, C_Q, C_SU, C_AU, C_AC, C_AB, C_GA, C_OA, C_GC, C_OC, C_GB, C_GLU, C_GB2, C_OB, C_WO = (
    0, 2, 4, 6, 8, 10, 12, 16, 18, 22, 24, 26, 27, 29, 31)
COL_AU, COL_AB, COL_AC, COL_SU, COL_Q, COL_KV = 0, 512, 1024, 1536, 2048, 2560
KV_W = 2 * HD + IDX_HEADS * HD + HD + IDX_HEADS
COL_G = COL_KV + KV_W
BU_FROM = C_AU

PAR_LRE, PAR_LIM, PAR_LDT = 0, SCHUNKS, 2 * SCHUNKS
PAR_CW = 3 * SCHUNKS
PAR_D = PAR_CW + 3 * CT
PAR_GAIN = PAR_D + CT
PAR_CRE = PAR_GAIN + 10 * HD
PAR_CIM = PAR_CRE + SCHUNKS * 32
PAR_B = PAR_CIM + SCHUNKS * 32
PAR_W = PAR_B + CT * 2 * P

MAGIC = 12582912.0
PIO2 = (1.5703125, 4.837512969970703e-4, 7.54978995489188216e-8)


def mixer_stream(w_in, w_out_a, w_out_b, w_out_c, w_glu, w_o, layer):
    wi = w_in[layer].rearrange("(k p) n -> p k n", p=P)
    stripe = lambda col, width: [(wi[:, 4 * h:4 * h + 4, col:col + width], (4, width)) for h in range(2)]
    rows = lambda w: [(w.rearrange("(k p) n -> p k n", p=P)[:, 2 * h:2 * h + 2, :], (2, D))
                      for h in range(w.shape[0] // (2 * P))]
    gates = lambda branch: stripe(COL_G + branch * D, HALF) + stripe(COL_G + branch * D + HALF, HALF)
    chunks = stripe(COL_KV, KV_W) + stripe(COL_Q, HALF) + stripe(COL_SU, SSM)
    chunks += stripe(COL_AU, CONV) + stripe(COL_AC, CONV) + stripe(COL_AB, CONV)
    chunks += gates(0) + rows(w_out_a[layer]) + gates(2) + rows(w_out_c[layer]) + gates(1)
    chunks.insert(C_GLU, (w_glu[layer].rearrange("(k p) n -> p k n", p=P), (4, SSM)))
    chunks += rows(w_out_b[layer]) + rows(w_o[layer])
    assert len(chunks) == MIX_CHUNKS
    return chunks


class Chain:

    def __init__(self, eng, sem):
        self.eng, self.sem, self.n = eng, sem, 0

    def step(self, ins):
        ins.then_inc(self.sem, 1)
        self.n += 1

    def join(self):
        self.eng.wait_ge(self.sem, self.n)

    def then(self, ins):
        self.step(ins)
        self.join()


def trunk(nc, x, gains, w_in, par, w_glu, w_out_a, w_out_b, w_out_c, w_o, rope, slot_ids, ffn_w1, ffn_w3, ffn_w2,
          router_w, moe_w1, moe_w3, moe_w2, table_store, out):
    with ExitStack() as ctx:
        def sb(name, shape, dt=F32, scope=ctx):
            return scope.enter_context(nc.sbuf_tensor(name, shape, dt))

        def sem(name):
            return ctx.enter_context(nc.semaphore(name))

        ps = ctx.enter_context(nc.psum_tensor("ps", [P, 8, HALF], F32))

        raw = sb("raw", [P, RAW, CHUNK])
        w_hi = sb("w_hi", [P, SPLIT, CHUNK], F32R)
        w_lo = sb("w_lo", [P, SPLIT, CHUNK], F32R)
        x_tok = sb("x_tok", [P, BLOCKS, D])
        h_tok = sb("h_tok", [P, BLOCKS, D])
        hT_hi = sb("hT_hi", [P, KD, SEQ], F32R)
        hT_lo = sb("hT_lo", [P, KD, SEQ], F32R)
        ident = sb("ident", [P, P])
        upper = sb("upper", [P, P])
        ones = sb("ones", [P, P])
        causal = sb("causal", [P, P])
        rope_sb = sb("rope_sb", [P, BLOCKS, 3, 32])
        zero_r = sb("zero_r", [P, P], F32R)
        norm_ss = sb("norm_ss", [P, 4, BLOCKS])

        mix = ExitStack()
        gate = sb("gate", [P, BLOCKS, D], F32, mix)
        yac_hi = sb("yac_hi", [P, CT, SEQ], F32R, mix)
        yac_lo = sb("yac_lo", [P, CT, SEQ], F32R, mix)
        su = sb("su", [P, CT, SEQ], F32, mix)
        u_t = sb("u_t", [P, CT, SEQ], F32, mix)
        v_t = sb("v_t", [P, CT, SEQ + 2], F32, mix)
        par_sb = sb("par_sb", [P, PAR_W], F32, mix)
        qkT = sb("qkT", [P, 8, SEQ], F32, mix)
        v_sb = sb("v_sb", [P, BLOCKS, HD], F32, mix)
        wi_sb = sb("wi_sb", [P, BLOCKS, IDX_HEADS], F32, mix)
        probs = sb("probs", [P, 4, SEQ], F32, mix)
        keybias = sb("keybias", [P, BLOCKS, SEQ], F32, mix)
        top8 = sb("top8", [P, 8], F32, mix)
        smalls = sb("smalls", [P, 8], F32, mix)
        qk_ss = sb("qk_ss", [P, 3, BLOCKS, 10], F32, mix)
        rowmax = sb("rowmax", [P, 4], F32, mix)
        rowsum = sb("rowsum", [P, 4], F32, mix)
        rowinv = sb("rowinv", [P, 4], F32, mix)
        trig = sb("trig", [P, 32, SCHUNKS], F32, mix)
        pow_b = sb("pow_b", [P, 2, 16, SCHUNKS], F32, mix)
        pow_a = sb("pow_a", [P, 2, 16, SCHUNKS], F32, mix)
        table = sb("table", [P, 2, 2, SEQ], F32, mix)
        pool_t = sb("pool_t", [P, 2, SEQ], F32, mix)
        state = sb("state", [P, 2, SEQ], F32, mix)
        with ExitStack() as overlay:
            turn = sb("turn", [P, 2, 4, SEQ], F32, overlay)
        yb_hi = sb("yb_hi", [P, CT, SEQ], F32R, mix)
        yb_lo = sb("yb_lo", [P, CT, SEQ], F32R, mix)
        mix.close()
        gain_row = gate[:, 0, :]
        qk = h_tok[:, :, :].rearrange("p b (h d) -> p b h d", d=HD)
        mixed = h_tok
        scratch = probs

        ffn = ExitStack()
        sil = sb("sil", [P, HALF], F32, ffn)
        gain_ff = sb("gain_ff", [P, D], F32, ffn)
        hid = sb("hid", [P, HALF], F32, ffn)
        hidT_hi = sb("hidT_hi", [P, HALF], F32R, ffn)
        hidT_lo = sb("hidT_lo", [P, HALF], F32R, ffn)
        h_hi = sb("h_hi", [P, BLOCKS, D], F32R, ffn)
        h_lo = sb("h_lo", [P, BLOCKS, D], F32R, ffn)
        xg_hi = sb("xg_hi", [P, KD, P], F32R, ffn)
        xg_lo = sb("xg_lo", [P, KD, P], F32R, ffn)
        y_hi = sb("y_hi", [P, D], F32R, ffn)
        y_lo = sb("y_lo", [P, D], F32R, ffn)
        router_sb = sb("router_sb", [P, KD, EXPERTS], F32, ffn)
        slot_id = sb("slot_id", [P, 2, P], F32, ffn)
        pick = sb("pick", [P, BLOCKS, P], F32R, ffn)
        pickT = sb("pickT", [P, BLOCKS, P], F32R, ffn)
        rt = sb("rt", [P, 10, BLOCKS, EXPERTS], F32, ffn)
        rt8 = sb("rt8", [P, BLOCKS, 8], F32, ffn)
        rts = sb("rts", [P, 6, BLOCKS], F32, ffn)
        gate_of = sb("gate_of", [P, BLOCKS, EXPERTS], F32, ffn)
        slot_of = sb("slot_of", [P, BLOCKS, EXPERTS + 1], F32, ffn)
        most = sb("most", [P, 1], F32, ffn)
        most_i = sb("most_i", [1, 1], I32, ffn)
        ffn.close()

        raw_full = [sem(f"raw_full{i}") for i in range(RAW)]
        hi_done, lo_done, used = sem("hi_done"), sem("lo_done"), sem("used")
        dve_step, pool_step = sem("dve_step"), sem("pool_step")
        names = """x_loaded consts rope_loaded gain_loaded par_loaded ss_done var_done std_done h_done hT_ps
            hT_hi_done hT_lo_done x_added out_stored zero_done
            su_copied q_copied kv_copied u_copied v_made conv_done ya_hi_done ya_lo_done
            gate_done gated mixed_done mixT_ps mixT_hi_done mixT_lo_done
            sq_done qk_ss_done qk_std_done qk_inv_done idx_rope_done idxT_ps idxT_copied rope_done qkT_ps qkT_copied
            idx_ps scored logit_ps shifted exp_done row_inv_done prob_done pT_ps pT_copied
            o_ps o_copied yc_hi_done yc_lo_done
            dt_exp lrdt_done mag_exp den_done den_inv powers_done table_done table_stored0 table_stored1 table_loaded0 table_loaded1 bu_ps turned
            scanned rotated y_ps skip_done gelu_done yg_hi_done yg_lo_done glu_sig yb_made yb_hi_done yb_lo_done
            sil_done hid_done hidT_ps hidT_hi_done hidT_lo_done ff_out
            router_loaded slots_loaded h_hi_done h_lo_done logits_ps exp_r picked rank_ps slots_done most_done top_r
            pick_done gather_ps xg_hi_done xg_lo_done pickT_ps pickT_done y_hi_done y_lo_done scatter_ps acc_done
            final_done""".split()

        S = {n: sem(n) for n in names}
        block = ctx.enter_context(nc.Block())

        streams = [mixer_stream(w_in, w_out_a, w_out_b, w_out_c, w_glu, w_o, layer) for layer in range(DEPTH)]

        def slot_view(buf, n, shape):
            k, w = shape
            return buf[:, n % (RAW if buf is raw else SPLIT), 0:k * w].rearrange("p (k n) -> p k n", k=k)

        def split_hi(act, n, turns=0, width=CHUNK):
            act.wait_ge(raw_full[n % RAW], 16 * (n // RAW + 1) + 16 * turns)
            if n >= SPLIT:
                act.wait_ge(used, n - SPLIT + 1 + 6 * turns)
            act.activation(w_hi[:, n % SPLIT, 0:width], raw[:, n % RAW, 0:width], ACT.Copy).then_inc(hi_done, 1)

        def split_lo(dve, n, seen=None, width=CHUNK):
            dve.wait_ge(hi_done, n + 1 if seen is None else seen)
            dve.tensor_tensor(w_lo[:, n % SPLIT, 0:width], raw[:, n % RAW, 0:width],
                              w_hi[:, n % SPLIT, 0:width].bitcast(F32), ALU.subtract).then_inc(lo_done, 1)

        def value(eng, v):
            return v if isinstance(v, int) else eng.snap(v)

        def trig_row(i, count=1):
            return trig[:, i, :] if count == 1 else trig[:, i:i + count, :]

        (LR, DT, LRDT, MAG, K, R, R2, SN, CS, M, M2, CQ, SQ, T1, T2, SIN, COS, NR, NI, DEN, INV, CRE, CIM,
         ANG) = range(24)
        W_ROWS, SQ_ROWS = (24, 26), 28

        def ops(eng, own):
            def tt(o, a, b, op):
                own.step(eng.tensor_tensor(o, a, b, op))

            def ts(o, a, c1, op1, c2=None, op2=None):
                own.step(eng.tensor_scalar(o, a, c1, c2, op1, op2) if op2 is not None else
                         eng.tensor_scalar(o, a, c1, None, op1))
            return tt, ts

        def s5_rates(eng, own, layer):
            tt, ts = ops(eng, own)
            li = par_sb[:, PAR_LIM:PAR_LIM + SCHUNKS]
            eng.wait_ge(S["par_loaded"], 16 * (layer + 1))
            ts(trig_row(LR), par_sb[:, PAR_LRE:PAR_LRE + SCHUNKS], -1e-4, ALU.min)
            tt(trig_row(T2), li, li, ALU.mult)
            own.join()
            tt(trig_row(T1), trig_row(LR), trig_row(LR), ALU.mult)
            own.join()
            eng.tensor_tensor(trig_row(DEN), trig_row(T1), trig_row(T2), ALU.add).then_inc(S["den_done"], 1)
            eng.wait_ge(S["dt_exp"], layer + 1)
            eng.tensor_tensor(trig_row(LRDT), trig_row(LR), trig_row(DT), ALU.mult).then_inc(S["lrdt_done"], 1)

        def s5_angles(eng, own, layer):
            tt, ts = ops(eng, own)
            k, r, r2, sn, cs, m, m2, cq, sq, t1, t2, sin, cos, ang = (
                trig_row(i) for i in (K, R, R2, SN, CS, M, M2, CQ, SQ, T1, T2, SIN, COS, ANG))
            li = par_sb[:, PAR_LIM:PAR_LIM + SCHUNKS]
            tt(ang, li, trig_row(DT), ALU.mult)
            own.join()
            ts(k, ang, 2.0 / float(np.pi), ALU.mult)
            own.join()
            ts(k, k, MAGIC, ALU.add)
            own.join()
            ts(k, k, -MAGIC, ALU.add)
            own.join()
            ts(t1, k, -PIO2[0], ALU.mult)
            ts(t2, k, -PIO2[1], ALU.mult)
            ts(sq, k, -PIO2[2], ALU.mult)
            ts(m, k, 0.25, ALU.mult)
            own.join()
            tt(r, ang, t1, ALU.add)
            ts(m, m, MAGIC, ALU.add)
            own.join()
            tt(r, r, t2, ALU.add)
            ts(m, m, -MAGIC, ALU.add, -4.0, ALU.mult)
            own.join()
            tt(r, r, sq, ALU.add)
            tt(m, m, k, ALU.add)
            own.join()
            tt(r2, r, r, ALU.mult)
            tt(m2, m, m, ALU.mult)
            own.join()
            ts(sn, r2, 1.0 / 362880, ALU.mult, -1.0 / 5040, ALU.add)
            ts(cs, r2, -1.0 / 3628800, ALU.mult, 1.0 / 40320, ALU.add)
            ts(cq, m2, 0.0, ALU.is_equal)
            ts(t1, m2, 4.0, ALU.is_equal)
            ts(sq, m2, 1.0, ALU.is_equal)
            own.join()
            tt(cq, cq, t1, ALU.subtract)
            tt(sq, sq, m, ALU.mult)
            for c_sin, c_cos in ((1.0 / 120, -1.0 / 720), (-1.0 / 6, 1.0 / 24), (1.0, -0.5)):
                tt(sn, sn, r2, ALU.mult)
                tt(cs, cs, r2, ALU.mult)
                own.join()
                ts(sn, sn, c_sin, ALU.add)
                ts(cs, cs, c_cos, ALU.add)
                own.join()
            tt(sn, sn, r, ALU.mult)
            tt(cs, cs, r2, ALU.mult)
            own.join()
            ts(cs, cs, 1.0, ALU.add)
            own.join()
            tt(t1, cs, cq, ALU.mult)
            tt(t2, sn, sq, ALU.mult)
            tt(m, sn, cq, ALU.mult)
            tt(m2, cs, sq, ALU.mult)
            own.join()
            tt(cos, t1, t2, ALU.subtract)
            tt(sin, m, m2, ALU.add)
            own.join()

        def s5_powers(eng, own):
            tt, ts = ops(eng, own)
            for dst in (pow_b, pow_a):
                own.step(eng.memset(dst[:, 0, 0, :], 1.0))
                own.step(eng.memset(dst[:, 1, 0, :], 0.0))
            own.join()
            w_re, w_im = trig_row(COS), trig_row(SIN)
            for level in range(8):
                dst, n = (pow_b, pow_a)[level // 4], 1 << (level % 4)
                a = dst[:, :, 0:n, :]
                by_re, by_im = (turn[:, i, :, :].rearrange("p a t -> p (a t)")[:, 0:2 * n * SCHUNKS]
                                .rearrange("p (c n j) -> p c n j", c=2, n=n) for i in range(2))
                wide = lambda w: w.unsqueeze(1).unsqueeze(1).broadcast_to([P, 2, n, SCHUNKS])
                sq_re, sq_im = trig_row(SQ_ROWS), trig_row(SQ_ROWS + 1)
                to = W_ROWS[level % 2]
                tt(by_re, a, wide(w_re), ALU.mult)
                tt(by_im, a, wide(w_im), ALU.mult)
                tt(sq_re, w_re, w_re, ALU.mult)
                tt(sq_im, w_im, w_im, ALU.mult)
                tt(trig_row(to + 1), w_re, w_im, ALU.mult)
                own.join()
                tt(dst[:, 0, n:2 * n, :], by_re[:, 0], by_im[:, 1], ALU.subtract)
                tt(trig_row(to), sq_re, sq_im, ALU.subtract)
                ts(trig_row(to + 1), trig_row(to + 1), 2.0, ALU.mult)
                last = eng.tensor_tensor(dst[:, 1, n:2 * n, :], by_re[:, 1], by_im[:, 0], ALU.add)
                if level < 7:
                    own.step(last)
                else:
                    last.then_inc(S["powers_done"], 1)
                own.join()
                w_re, w_im = trig_row(to), trig_row(to + 1)

        def s5_fold(eng, own, layer):
            tt, ts = ops(eng, own)
            lr, mag, nr, ni, t1, t2, m, m2, cre, cim, inv = (
                trig_row(i) for i in (LR, MAG, NR, NI, T1, T2, M, M2, CRE, CIM, INV))
            li = par_sb[:, PAR_LIM:PAR_LIM + SCHUNKS]
            eng.wait_ge(S["mag_exp"], layer + 1)
            tt(nr, mag, trig_row(COS), ALU.mult)
            tt(ni, mag, trig_row(SIN), ALU.mult)
            own.join()
            ts(nr, nr, -1.0, ALU.add)
            own.join()
            tt(t1, nr, lr, ALU.mult)
            tt(t2, ni, li, ALU.mult)
            tt(m, ni, lr, ALU.mult)
            tt(m2, nr, li, ALU.mult)
            own.join()
            tt(cre, t1, t2, ALU.add)
            tt(cim, m, m2, ALU.subtract)
            own.join()
            eng.wait_ge(S["den_inv"], layer + 1)
            tt(cre, cre, inv, ALU.mult)
            tt(cim, cim, inv, ALU.mult)
            own.join()
            c_re, c_im = (par_sb[:, o:o + SCHUNKS * 32].rearrange("p (j c) -> p j c", c=32)
                          for o in (PAR_CRE, PAR_CIM))
            ta, tb, tc, td = (turn[:, i // 2, 2 * (i % 2):2 * (i % 2) + 2, :].rearrange("p a (j c) -> p (a j) c", c=32)
                              for i in range(4))
            kr, ki = (v.unsqueeze(2).broadcast_to([P, SCHUNKS, 32]) for v in (cre, cim))
            tt(ta, c_re, kr, ALU.mult)
            tt(tb, c_im, ki, ALU.mult)
            tt(tc, c_re, ki, ALU.mult)
            tt(td, c_im, kr, ALU.mult)
            own.join()
            tt(c_re, ta, tb, ALU.subtract)
            tt(c_im, td, tc, ALU.add)
            own.join()
            ts(c_im, c_im, -1.0, ALU.mult)
            own.join()

        squares = gate

        def banks(lo, count):
            return ps[:, lo:lo + count, :].rearrange("p a n -> p (a n)")

        def flat(t):
            return t.rearrange("p a b -> p (a b)")

        def probs_T(kt, q):
            return flat(probs[:, :, :])[:, (4 * kt + q) * P:(4 * kt + q + 1) * P]

        def mix_width(layer, c):
            k, w = streams[layer][c][1]
            return k * w

        @block.sync
        def _(sp):
            sp.dma_start(x_tok[:, :, :], x[0].rearrange("(b p) d -> p b d", p=P)).then_inc(S["x_loaded"], 16)

            def load(n, src, dst):
                if n >= RAW:
                    sp.wait_ge(lo_done, n - RAW + 1)
                sp.dma_start(dst, src).then_inc(raw_full[n % RAW], 16)

            def mixer(layer):
                for c, (src, shape) in enumerate(streams[layer]):
                    load(MIX0[layer] + c, src, slot_view(raw, MIX0[layer] + c, shape))

            w1d = ffn_w1[0].rearrange("(k p) n -> p k n", p=P)
            w3d = ffn_w3[0].rearrange("(k p) n -> p k n", p=P)
            w2d = ffn_w2[0].rearrange("(k p) n -> p k n", p=P)

            def load_at(n, turns, src):
                free = value(sp, n - RAW + 1 + 6 * turns)
                sp.wait_ge(lo_done, free)
                shape = tuple(src.shape[1:])
                sp.dma_start(slot_view(raw, n, shape), src).then_inc(raw_full[n % RAW], 16)

            def dense():
                n = DENSE0
                load(n, w1d[:, :, 0:DENSE_W], slot_view(raw, n, (KD, DENSE_W)))
                load(n + 1, w3d[:, :, 0:DENSE_W], slot_view(raw, n + 1, (KD, DENSE_W)))
                with sp.Fori(0, (DENSE_STRIPES - 1) // 2) as t:
                    for h in range(2):
                        m = n + 2 + 3 * h
                        col = sp.snap((2 * t + 1 + h) * DENSE_W)
                        row = sp.snap((2 * t + h) * 2)
                        load_at(m, t, w1d[:, :, bass.ds(col, DENSE_W)])
                        load_at(m + 1, t, w3d[:, :, bass.ds(col, DENSE_W)])
                        load_at(m + 2, t, w2d[:, bass.ds(row, 2), :])
                last = n + DENSE_CHUNKS - 1
                load(last, w2d[:, 2 * (DENSE_STRIPES - 1):2 * DENSE_STRIPES, :], slot_view(raw, last, (2, D)))

            w1e = moe_w1[0].rearrange("e (k p) n -> p (e k) n", p=P)
            w3e = moe_w3[0].rearrange("e (k p) n -> p (e k) n", p=P)
            w2e = moe_w2[0].rearrange("e (k p) n -> p (e k) n", p=P)
            K2 = FF_EXPERT // P

            def experts(rnd):
                n = MOE0 + rnd * EXPERTS * MOE_CHUNKS

                def up(m, turns, w, e, t):
                    col = value(sp, t * HALF)
                    for half in range(2):
                        row = value(sp, KD * e + 4 * half)
                        load_at(m + half, turns, w[:, bass.ds(row, 4), bass.ds(col, HALF)])

                def down(m, turns, e, t):
                    for half in range(2):
                        row = value(sp, K2 * e + 4 * t + 2 * half)
                        load_at(m + half, turns, w2e[:, bass.ds(row, 2), :])

                def expert(e, last):
                    with sp.Fori(1, MOE_STRIPES) as t:
                        turns = MOE_STRIPES * e + t - 1
                        up(n + 4, turns, w1e, e, t)
                        up(n + 6, turns, w3e, e, t)
                        down(n + 8, turns, e, t - 1)
                    turns = MOE_STRIPES * e + MOE_STRIPES - 1
                    if last:
                        down(n + 4, turns, e, MOE_STRIPES - 1)
                        return
                    up(n + 4, turns, w1e, e + 1, 0)
                    down(n + 6, turns, e, MOE_STRIPES - 1)
                    up(n + 8, turns, w3e, e + 1, 0)

                up(n, 0, w1e, 0, 0)
                up(n + 2, 0, w3e, 0, 0)
                with sp.Fori(0, EXPERTS - 1) as e:
                    expert(e, False)
                expert(EXPERTS - 1, True)

            mixer(0)
            dense()
            mixer(1)
            experts(0)
            sp.wait_ge(S["most_done"], 1)
            most_tokens = sp.value_load(most_i[0:1, 0:1])
            with sp.If(most_tokens > SLOTS):
                experts(1)
            sp.wait_ge(S["final_done"], 1)
            sp.dma_start(out[0].rearrange("(b p) d -> p b d", p=P), x_tok[:, :, :]).then_inc(S["out_stored"], 16)
            sp.wait_ge(S["out_stored"], 16)

        @block.tensor
        def _(pe):
            def three(dst, x_hi, x_lo, n, tile, first, last):
                hi, lo = tile(w_hi), tile(w_lo)
                pe.matmul(dst, x_hi, hi, start=first, stop=False, skip_group_check=True)
                pe.matmul(dst, x_hi, lo, start=False, stop=False, skip_group_check=True)
                return pe.matmul(dst, x_lo, hi, start=False, stop=last, skip_group_check=True)

            def columns(n, bank, k0, nk, width, first, last, seen=None):
                pe.wait_ge(lo_done, n + 1 if seen is None else seen)
                for k in range(nk):
                    for b in range(BLOCKS):
                        tok = slice(b * P, b * P + P)
                        mm = three(ps[:, bank + b, 0:width], hT_hi[:, k0 + k, tok], hT_lo[:, k0 + k, tok], n,
                                   lambda w: slot_view(w, n, (nk, width))[:, k, :], first and k == 0,
                                   last and k == nk - 1)
                mm.then_inc(used, 1)

            def channels(n, bank, k0, x_hi, x_lo, first, last):
                pe.wait_ge(lo_done, n + 1)
                for k in range(4):
                    for c in range(CT):
                        dst = ps[:, bank + c // 2, (c % 2) * SEQ:(c % 2 + 1) * SEQ]
                        wh = slot_view(w_hi, n, (4, HALF))[:, k, c * P:c * P + P]
                        wl = slot_view(w_lo, n, (4, HALF))[:, k, c * P:c * P + P]
                        start = first and k == 0 and c % 2 == 0
                        pe.matmul(dst, wh, x_hi[:, k0 + k, :], start=start, stop=False, skip_group_check=True)
                        pe.matmul(dst, wl, x_hi[:, k0 + k, :], start=False, stop=False, skip_group_check=True)
                        mm = pe.matmul(dst, wh, x_lo[:, k0 + k, :], start=False, stop=last and k == 3,
                                       skip_group_check=True)
                mm.then_inc(used, 1)

            def rows(n, k0, x_hi, x_lo, first, last, bank=0, blocks=BLOCKS, seen=None):
                pe.wait_ge(lo_done, n + 1 if seen is None else seen)
                for k in range(2):
                    for b in range(blocks):
                        tok = slice(b * P, b * P + P)
                        for h in range(2):
                            mm = three(ps[:, bank + 2 * b + h, :], x_hi[:, k0 + k, tok], x_lo[:, k0 + k, tok], n,
                                       lambda w: slot_view(w, n, (2, D))[:, k, h * HALF:(h + 1) * HALF],
                                       first and k == 0, last and k == 1)
                mm.then_inc(used, 1)

            def turn_rows(src, bank):
                for k in range(KD):
                    for b in range(BLOCKS):
                        at = (k % 2) * SEQ + b * P
                        tr = pe.transpose(ps[:, bank + k // 2, at:at + P], src[:, b, k * P:k * P + P], ident[:, :])
                    if k % 2:
                        yield tr

            def norm_turn(i):
                pe.wait_ge(S["h_done"], BLOCKS * (i + 1))
                for tr in turn_rows(h_tok, 0):
                    tr.then_inc(S["hT_ps"], 1)

            def bu(layer, j):
                if j == 0:
                    pe.wait_ge(S["su_copied"], layer + 1)
                    pe.wait_ge(S["par_loaded"], 16 * (layer + 1))
                else:
                    pe.wait_ge(S["turned"], 16 * layer + j)
                r = 32 * (j % 4)
                for part in range(2):
                    bt = par_sb[r:r + 32, PAR_B:PAR_B + CT * 2 * P].rearrange("p (c i n) -> p c i n", c=CT, i=2)
                    mm = pe.matmul(ps[:, 4, part * SEQ:(part + 1) * SEQ], bt[:, j // 4, part, :],
                                   su[r:r + 32, j // 4, :], start=part == 0, stop=part == 1, skip_group_check=True,
                                   tile_position=(r, 0))
                mm.then_inc(S["bu_ps"], 1)

            def y_of(layer, j):
                pe.wait_ge(S["rotated"], SCHUNKS * layer + j + 1)
                if j >= 4 and j % 4 == 0:
                    pe.wait_ge(S["skip_done"], CT * layer + j // 4)
                r, at = 32 * (j % 4), ((j // 4) % 2) * SEQ
                for part, col in ((0, PAR_CRE), (1, PAR_CIM)):
                    mm = pe.matmul(ps[r:r + 32, 5, at:at + SEQ], par_sb[:, col + 32 * j:col + 32 * j + 32],
                                   state[:, part, :], start=part == 0, stop=part == 1, skip_group_check=True,
                                   tile_position=(0, r))
                mm.then_inc(S["y_ps"], 1)

            def turn_heads(layer, pairs, done):
                for i, pair in enumerate(pairs):
                    for b in range(BLOCKS):
                        at = (i % 2) * SEQ + b * P
                        tr = pe.transpose(ps[:, 6 + i // 2, at:at + P], h_tok[:, b, pair * P:pair * P + P],
                                          ident[:, :])
                tr.then_inc(S[done], 1)

            def index_scores(layer, b):
                if b == 0:
                    pe.wait_ge(S["idxT_copied"], layer + 1)
                else:
                    pe.wait_ge(S["scored"], 2 * layer + 1)
                keys = (b + 1) * P
                for h in range(IDX_HEADS):
                    r = HD * (h % 2)
                    at = (h // 2) * keys
                    mm = pe.matmul(ps[:, 6 + h % 2, at:at + keys],
                                   qkT[r:r + HD, 5 + h // 2, b * P:b * P + P], qkT[r:r + HD, 7, 0:keys],
                                   start=at == 0, stop=True, skip_group_check=True, tile_position=(r, 0))
                mm.then_inc(S["idx_ps"], 1)

            def logits(layer, i):
                n = 4 * layer + i
                b, g = i // 2, i % 2
                if i == 0:
                    pe.wait_ge(S["qkT_copied"], 2 * layer + 2)
                else:
                    pe.wait_ge(S["o_copied"], n)
                keys = (b + 1) * P
                for h in range(4):
                    r = HD * (h % 2)
                    at = (h // 2) * keys
                    mm = pe.matmul(ps[:, 6 + h % 2, at:at + keys],
                                   qkT[r:r + HD, 2 * g + h // 2, b * P:b * P + P], qkT[r:r + HD, 4, 0:keys],
                                   start=at == 0, stop=True, skip_group_check=True, tile_position=(r, 0))
                mm.then_inc(S["logit_ps"], 1)

            def turn_probs(layer, i):
                n = 4 * layer + i
                pe.wait_ge(S["prob_done"], 4 * (n + 1))
                b = i // 2
                for kt in range(b + 1):
                    for h in range(4):
                        tr = pe.transpose(ps[:, 6 + kt, h * P:h * P + P], probs[:, h, kt * P:kt * P + P], ident[:, :])
                tr.then_inc(S["pT_ps"], 1)

            def values(layer, i):
                n = 4 * layer + i
                pe.wait_ge(S["pT_copied"], n + 1)
                b = i // 2
                for q in range(4):
                    r, pair = HD * (q // 2), q % 2
                    for kt in range(b + 1):
                        mm = pe.matmul(ps[r:r + HD, 6, pair * P:pair * P + P], v_sb[:, kt, :],
                                       probs_T(kt, q),
                                       start=kt == 0, stop=kt == b, skip_group_check=True, tile_position=(0, r))
                mm.then_inc(S["o_ps"], 1)

            def mixer(layer):
                c0 = MIX0[layer]
                norm_turn(2 * layer)

                def s5(c):
                    j = c - BU_FROM
                    if 0 <= j - 3 < SCHUNKS:
                        y_of(layer, j - 3)
                    if 0 <= j < SCHUNKS:
                        bu(layer, j)

                def stripe(c, bank, half, width=HALF):
                    columns(c0 + c + half, bank, 4 * half, 4, width, half == 0, half == 1)

                def held(c, bank, half):
                    channels(c0 + c + half, bank, 4 * half, hT_hi, hT_lo, half == 0, half == 1)

                pe.wait_ge(S["hT_lo_done"], 4 * (2 * layer + 1))
                stripe(C_KV, 0, 0, KV_W)
                stripe(C_KV, 0, 1, KV_W)
                stripe(C_Q, 2, 0)
                stripe(C_Q, 2, 1)
                pe.wait_ge(S["idx_rope_done"], BLOCKS * (layer + 1))
                turn_heads(layer, (5, 6, 7), "idxT_ps")
                pe.wait_ge(S["kv_copied"], 7 * (layer + 1))
                pe.wait_ge(S["sq_done"], 3 * layer + 2)
                held(C_SU, 0, 0)
                index_scores(layer, 0)
                held(C_SU, 0, 1)
                index_scores(layer, 1)
                pe.wait_ge(S["q_copied"], layer + 1)
                pe.wait_ge(S["sq_done"], 3 * layer + 3)
                held(C_AU, 2, 0)
                s5(C_AU)
                held(C_AU, 2, 1)
                pe.wait_ge(S["scored"], 2 * layer + 2)
                pe.wait_ge(S["rope_done"], BLOCKS * (layer + 1))
                turn_heads(layer, (0, 1, 2, 3), "qkT_ps")
                s5(C_AU + 1)
                pe.wait_ge(S["su_copied"], layer + 1)
                held(C_AC, 0, 0)
                pe.wait_ge(S["qkT_copied"], 2 * layer + 1)
                turn_heads(layer, (4,), "qkT_ps")
                s5(C_AC)
                held(C_AC, 0, 1)
                logits(layer, 0)
                s5(C_AC + 1)
                pe.wait_ge(S["u_copied"], layer + 1)
                held(C_AB, 2, 0)
                turn_probs(layer, 0)
                s5(C_AB)
                held(C_AB, 2, 1)
                values(layer, 0)
                logits(layer, 1)
                s5(C_AB + 1)
                pe.wait_ge(S["v_made"], layer + 1)
                stripe(C_GA, 0, 0)
                turn_probs(layer, 1)
                s5(C_GA)
                stripe(C_GA, 0, 1)
                values(layer, 1)
                logits(layer, 2)
                s5(C_GA + 1)
                pe.wait_ge(S["conv_done"], layer + 1)
                stripe(C_GA + 2, 2, 0)
                s5(C_GA + 2)
                stripe(C_GA + 2, 2, 1)
                turn_probs(layer, 2)
                s5(C_GA + 3)
                pe.wait_ge(S["gate_done"], 6 * layer + 2)
                pe.wait_ge(S["ya_lo_done"], layer + 1)
                rows(c0 + C_OA, 0, yac_hi, yac_lo, True, False)
                values(layer, 2)
                logits(layer, 3)
                s5(C_OA)
                rows(c0 + C_OA + 1, 2, yac_hi, yac_lo, False, True)
                s5(C_OA + 1)
                pe.wait_ge(S["gated"], 3 * layer + 1)
                stripe(C_GC, 0, 0)
                turn_probs(layer, 3)
                s5(C_GC)
                stripe(C_GC, 0, 1)
                values(layer, 3)
                s5(C_GC + 1)
                stripe(C_GC + 2, 2, 0)
                s5(C_GC + 2)
                stripe(C_GC + 2, 2, 1)
                s5(C_GC + 3)
                pe.wait_ge(S["gate_done"], 6 * layer + 4)
                pe.wait_ge(S["yc_lo_done"], layer + 1)
                rows(c0 + C_OC, 0, yac_hi, yac_lo, True, False)
                s5(C_OC)
                rows(c0 + C_OC + 1, 2, yac_hi, yac_lo, False, True)
                s5(C_OC + 1)
                pe.wait_ge(S["gated"], 3 * layer + 2)
                stripe(C_GB, 0, 0)
                s5(C_GB)
                stripe(C_GB, 0, 1)
                pe.wait_ge(S["yg_lo_done"], layer + 1)
                channels(c0 + C_GLU, 4, 0, yb_hi, yb_lo, True, True)
                stripe(C_GB2, 2, 0)
                stripe(C_GB2, 2, 1)
                pe.wait_ge(S["gate_done"], 6 * layer + 6)
                pe.wait_ge(S["yb_lo_done"], layer + 1)
                rows(c0 + C_OB, 0, yb_hi, yb_lo, True, False)
                rows(c0 + C_OB + 1, 2, yb_hi, yb_lo, False, True)
                pe.wait_ge(S["mixed_done"], 2 * (layer + 1))
                for tr in turn_rows(mixed, 4):
                    tr.then_inc(S["mixT_ps"], 1)
                pe.wait_ge(S["mixT_lo_done"], 4 * (layer + 1))
                for i in range(4):
                    rows(c0 + C_WO + i, 2 * i, hT_hi, hT_lo, i == 0, i == 3)

            def clear(bank, count):
                for b in range(bank, bank + count):
                    pe.matmul(ps[:, b, 0:P], zero_r[:, :], zero_r[:, :], start=True, stop=False,
                              skip_group_check=True)

            def dense():
                n0 = DENSE0

                def up(n, i, turns):
                    for which, bank, read in ((0, 0, S["sil_done"]), (1, 1, S["hid_done"])):
                        if i is not None:
                            pe.wait_ge(read, i)
                        pe.wait_ge(lo_done, n + which + 1 + 6 * turns)
                        for k in range(KD):
                            for b in range(BLOCKS):
                                tok = slice(b * P, b * P + P)
                                mm = three(ps[:, bank, b * DENSE_W:(b + 1) * DENSE_W], hT_hi[:, k, tok],
                                           hT_lo[:, k, tok], n,
                                           lambda w: slot_view(w, n + which, (KD, DENSE_W))[:, k, :],
                                           k == 0 and b == 0, k == KD - 1)
                        mm.then_inc(used, 1)

                def turn_hidden(i):
                    pe.wait_ge(S["hid_done"], i + 1)
                    for k in range(2):
                        for b in range(BLOCKS):
                            tr = pe.transpose(ps[:, 2, k * SEQ + b * P:k * SEQ + b * P + P],
                                              hid[:, b * DENSE_W + k * P:b * DENSE_W + k * P + P], ident[:, :])
                    tr.then_inc(S["hidT_ps"], 1)

                x_hi = hidT_hi[:, :].rearrange("p (k t) -> p k t", k=2)
                x_lo = hidT_lo[:, :].rearrange("p (k t) -> p k t", k=2)
                norm_turn(1)
                pe.wait_ge(S["hT_lo_done"], 8)
                clear(4, 4)
                up(n0, None, 0)
                turn_hidden(0)
                with pe.Fori(0, (DENSE_STRIPES - 1) // 2) as t:
                    for h in range(2):
                        m = n0 + 2 + 3 * h
                        i = 2 * t + 1 + h
                        up(m, i, t)
                        pe.wait_ge(S["hidT_lo_done"], i)
                        rows(m + 2, 0, x_hi, x_lo, False, False, bank=4, seen=m + 3 + 6 * t)
                        turn_hidden(i)
                pe.wait_ge(S["hidT_lo_done"], DENSE_STRIPES)
                rows(n0 + DENSE_CHUNKS - 1, 0, x_hi, x_lo, False, True, bank=4)

            def route():
                norm_turn(3)
                pe.wait_ge(S["hT_lo_done"], 16)
                pe.wait_ge(S["router_loaded"], 16)
                for b in range(BLOCKS):
                    for k in range(KD):
                        for part in (hT_hi, hT_lo):
                            mm = pe.matmul(ps[:, 4, b * 8:b * 8 + 8], part[:, k, b * P:b * P + P].bitcast(F32),
                                           router_sb[:, k, :], start=b == 0 and k == 0 and part is hT_hi,
                                           stop=k == KD - 1 and part is hT_lo, skip_group_check=True)
                mm.then_inc(S["logits_ps"], 1)
                pe.wait_ge(S["picked"], 1)
                sel = rt[:, 7]
                pe.matmul(ps[:, 5, 0:8], upper[:, :], sel[:, 0, :], start=True, stop=True, skip_group_check=True)
                pe.matmul(ps[:, 5, 8:16], ones[:, :], sel[:, 0, :], start=False, stop=False, skip_group_check=True)
                pe.matmul(ps[:, 5, 8:16], upper[:, :], sel[:, 1, :], start=False, stop=True, skip_group_check=True)
                pe.matmul(ps[:, 5, 16:24], ones[:, :], sel[:, 0, :], start=False, stop=False, skip_group_check=True)
                pe.matmul(ps[:, 5, 16:24], ones[:, :], sel[:, 1, :], start=False, stop=True,
                          skip_group_check=True).then_inc(S["rank_ps"], 1)
                pe.wait_ge(S["slots_done"], 1)

            def experts(rnd):
                n0 = MOE0 + rnd * EXPERTS * MOE_CHUNKS
                e0 = rnd * EXPERTS
                i0 = DENSE_STRIPES + e0 * MOE_STRIPES
                xT_hi = hidT_hi[:, :].rearrange("p (k t) -> p k t", k=4)
                xT_lo = hidT_lo[:, :].rearrange("p (k t) -> p k t", k=4)

                def up(n, which, i, turns):
                    pe.wait_ge(S["hid_done"] if which else S["sil_done"], i)
                    for half in range(2):
                        m = n + half
                        pe.wait_ge(lo_done, m + 1 + 6 * turns)
                        for k in range(4):
                            kk = 4 * half + k
                            mm = three(ps[:, which, :], xg_hi[:, kk, :], xg_lo[:, kk, :], m,
                                       lambda w: slot_view(w, m, (4, HALF))[:, k, :], kk == 0, kk == KD - 1)
                        mm.then_inc(used, 1)

                def turn_hidden(i):
                    pe.wait_ge(S["hid_done"], i + 1)
                    for k in range(4):
                        tr = pe.transpose(ps[:, 4, k * P:k * P + P], hid[:, k * P:k * P + P], ident[:, :])
                    tr.then_inc(S["hidT_ps"], 1)

                def down(n, i, turns, first=False):
                    pe.wait_ge(S["hidT_lo_done"], i)
                    for half in range(2):
                        rows(n + half, 2 * half, xT_hi, xT_lo, first and half == 0, False, bank=2, blocks=1,
                             seen=n + half + 1 + 6 * turns)

                def gather(e):
                    pe.wait_ge(S["pick_done"], BLOCKS * (e0 + e + 1))
                    for src, bank in ((h_hi, 4), (h_lo, 6)):
                        for k in range(KD):
                            for b in range(BLOCKS):
                                mm = pe.matmul(ps[:, bank + k // 4, (k % 4) * P:(k % 4) * P + P],
                                               src[:, b, k * P:k * P + P], pick[:, b, :],
                                               start=k % 4 == 0 and b == 0, stop=b == 1, skip_group_check=True)
                        mm.then_inc(S["gather_ps"], 1)

                def turn_pick(e):
                    for b in range(BLOCKS):
                        tr = pe.transpose(ps[:, 5, b * P:b * P + P], pick[:, b, :].bitcast(F32), ident[:, :])
                    tr.then_inc(S["pickT_ps"], 1)

                def scatter(e):
                    pe.wait_ge(S["pickT_done"], e0 + e + 1)
                    pe.wait_ge(S["y_hi_done"], e0 + e + 1)
                    pe.wait_ge(S["y_lo_done"], e0 + e + 1)
                    for b in range(BLOCKS):
                        for half in range(2):
                            dst = ps[:, 2 + half if b == 0 else 6 + half, :]
                            pe.matmul(dst, pickT[:, b, :], y_hi[:, half * HALF:(half + 1) * HALF], start=True,
                                      stop=False, skip_group_check=True)
                            mm = pe.matmul(dst, pickT[:, b, :], y_lo[:, half * HALF:(half + 1) * HALF], start=False,
                                           stop=True, skip_group_check=True)
                    mm.then_inc(S["scatter_ps"], 1)

                def expert(e, last):
                    i = i0 + MOE_STRIPES * e
                    turns = MOE_STRIPES * e
                    turn_hidden(i)
                    up(n0 + 4, 0, i + 1, turns)
                    up(n0 + 6, 1, i + 1, turns)
                    pe.wait_ge(S["acc_done"], 4 * (e0 + e) + 1)
                    down(n0 + 8, i + 1, turns, first=True)
                    turn_hidden(i + 1)
                    turn_pick(e)
                    with pe.Fori(2, MOE_STRIPES - 1) as t:
                        up(n0 + 4, 0, i + t, turns + t - 1)
                        up(n0 + 6, 1, i + t, turns + t - 1)
                        down(n0 + 8, i + t, turns + t - 1)
                        turn_hidden(i + t)
                    t = MOE_STRIPES - 1
                    up(n0 + 4, 0, i + t, turns + t - 1)
                    up(n0 + 6, 1, i + t, turns + t - 1)
                    if not last:
                        pe.wait_ge(S["hidT_lo_done"], i + t)
                        pe.wait_ge(S["pickT_done"], e0 + e + 1)
                        gather(e + 1)
                    down(n0 + 8, i + t, turns + t - 1)
                    if not last:
                        pe.wait_ge(S["xg_hi_done"], e0 + e + 2)
                    turn_hidden(i + t)
                    if last:
                        down(n0 + 4, i + t + 1, turns + t)
                    else:
                        pe.wait_ge(S["xg_lo_done"], e0 + e + 2)
                        up(n0 + 4, 0, i + t + 1, turns + t)
                        down(n0 + 6, i + t + 1, turns + t)
                        up(n0 + 8, 1, i + t + 1, turns + t)
                    scatter(e)

                if rnd == 0:
                    pe.wait_ge(S["h_lo_done"], BLOCKS)
                else:
                    pe.wait_ge(S["acc_done"], 4 * e0 + 1)
                gather(0)
                pe.wait_ge(S["xg_hi_done"], e0 + 1)
                pe.wait_ge(S["xg_lo_done"], e0 + 1)
                up(n0, 0, i0, 0)
                up(n0 + 2, 1, i0, 0)
                with pe.Fori(0, EXPERTS - 1) as e:
                    expert(e, False)
                expert(EXPERTS - 1, True)

            pe.wait_ge(S["consts"], 5)
            mixer(0)
            dense()
            mixer(1)
            route()
            experts(0)
            pe.wait_ge(S["most_done"], 1)
            most_tokens = pe.value_load(most_i[0:1, 0:1])
            with pe.If(most_tokens > SLOTS):
                experts(1)

        @block.scalar
        def _(act):
            act.dma_start(rope_sb[:, :, :, :], rope).then_inc(S["rope_loaded"], 16)

            def norm(i):
                if i == 0:
                    act.wait_ge(S["x_loaded"], 16)
                else:
                    act.wait_ge(S["x_added"], i)
                for b in range(BLOCKS):
                    act.activation(h_tok[:, b, :], x_tok[:, b, :], ACT.Square,
                                   accum_out=norm_ss[:, 0, b:b + 1]).then_inc(S["ss_done"], 1)
                act.wait_ge(S["var_done"], i + 1)
                act.activation(norm_ss[:, 2, :], norm_ss[:, 1, :], ACT.Sqrt).then_inc(S["std_done"], 1)

            def turned_hi(i, ready, bank, done):
                for q in range(4):
                    act.wait_ge(ready, 4 * i + q + 1)
                    act.activation(flat(hT_hi[:, 2 * q:2 * q + 2, :]), ps[:, bank + q, :], ACT.Copy)\
                       .then_inc(done, 1)

            def sigmoid_gate(layer, c, k, half):
                act.wait_ge(used, MIX0[layer] + c + 2)
                if k >= 4:
                    act.wait_ge(S["mixed_done"], 2 * layer + 1)
                elif k >= 2:
                    act.wait_ge(S["gated"], 3 * layer + 1)
                act.activation(gate[:, :, half * HALF:(half + 1) * HALF], ps[:, 2 * half:2 * half + 2, :],
                               ACT.Sigmoid).then_inc(S["gate_done"], 1)

            def softmax_exp(layer, i):
                n, keys = 4 * layer + i, (i // 2 + 1) * P
                act.wait_ge(S["shifted"], n + 1)
                for h in range(4):
                    ins = act.activation(probs[:, h, 0:keys], probs[:, h, 0:keys], ACT.Exp,
                                         bias=rowmax[:, h:h + 1], accum_out=rowsum[:, h:h + 1])
                    ins.then_inc(S["exp_done"], 1)

            def normalise(layer, i):
                n, keys = 4 * layer + i, (i // 2 + 1) * P
                act.wait_ge(S["row_inv_done"], n + 1)
                for h in range(4):
                    act.activation(probs[:, h, 0:keys], probs[:, h, 0:keys], ACT.Copy, scale=rowinv[:, h:h + 1])\
                       .then_inc(S["prob_done"], 1)

            def copy_pT(layer, i):
                n, tiles = 4 * layer + i, i // 2 + 1
                act.wait_ge(S["pT_ps"], n + 1)
                act.activation(flat(probs[:, :, :])[:, 0:tiles * 4 * P], banks(6, tiles), ACT.Copy)\
                   .then_inc(S["pT_copied"], 1)

            def copy_o(layer, i):
                n, b, g = 4 * layer + i, i // 2, i % 2
                act.wait_ge(S["o_ps"], n + 1)
                act.activation(qkT[:, 2 * g:2 * g + 2, b * P:(b + 1) * P],
                               ps[:, 6, 0:2 * P].rearrange("p (a n) -> p a n", a=2), ACT.Copy)\
                   .then_inc(S["o_copied"], 1)

            def yc_hi(layer):
                act.wait_ge(S["o_copied"], 4 * (layer + 1))
                act.wait_ge(used, MIX0[layer] + C_OA + 2)
                act.activation(flat(yac_hi[:, :, :]), flat(qkT[:, 0:4, :]), ACT.Copy).then_inc(S["yc_hi_done"], 1)

            def step_sizes(layer):
                act.wait_ge(S["par_loaded"], 16 * (layer + 1))
                act.activation(trig_row(DT), par_sb[:, PAR_LDT:PAR_LDT + SCHUNKS], ACT.Exp).then_inc(S["dt_exp"], 1)

            def decays(layer):
                act.wait_ge(S["lrdt_done"], layer + 1)
                act.activation(trig_row(MAG), trig_row(LRDT), ACT.Exp).then_inc(S["mag_exp"], 1)

            def mixer(layer):
                c0 = MIX0[layer]
                sp = lambda c: split_hi(act, c0 + c, width=mix_width(layer, c))
                if layer == 0:
                    norm(0)
                    step_sizes(0)
                    sp(0)
                    sp(1)
                    decays(0)
                else:
                    sp(0)
                    norm(2 * layer)
                    sp(1)
                sp(2)
                turned_hi(2 * layer, S["hT_ps"], 0, S["hT_hi_done"])
                sp(3)
                act.wait_ge(used, c0 + C_KV + 2)
                act.wait_ge(S["hT_lo_done"], 4 * (2 * layer + 1))
                kv = ps[:, 0:2, :]
                for to, at, width in ((10, 2, IDX_HEADS), (14, 6, 1), (15, 6, 1), (8, 0, 1), (9, 0, 1)):
                    act.activation(h_tok[:, :, to * HD:(to + width) * HD], kv[:, :, at * HD:(at + width) * HD],
                                   ACT.Copy).then_inc(S["kv_copied"], 1)
                act.activation(v_sb[:, :, :], kv[:, :, HD:2 * HD], ACT.Copy).then_inc(S["kv_copied"], 1)
                act.activation(wi_sb[:, :, :], kv[:, :, 7 * HD:7 * HD + IDX_HEADS], ACT.Copy,
                               scale=IDX_HEADS ** -0.5).then_inc(S["kv_copied"], 1)
                for head in (8, 9):
                    act.activation(squares[:, :, head * HD:(head + 1) * HD], kv[:, :, 0:HD], ACT.Square)\
                       .then_inc(S["sq_done"], 1)
                sp(4)
                sp(5)
                act.wait_ge(used, c0 + C_Q + 2)
                act.activation(squares[:, :, 0:HALF], ps[:, 2:4, :], ACT.Square).then_inc(S["sq_done"], 1)
                act.activation(h_tok[:, :, 0:HALF], ps[:, 2:4, :], ACT.Copy).then_inc(S["q_copied"], 1)
                act.wait_ge(S["idxT_ps"], layer + 1)
                act.activation(flat(qkT[:, 5:8, :]), banks(6, 2)[:, 0:3 * SEQ], ACT.Copy).then_inc(S["idxT_copied"], 1)
                act.wait_ge(S["qk_ss_done"], layer + 1)
                act.activation(qk_ss[:, 1, :, :], qk_ss[:, 0, :, :], ACT.Sqrt).then_inc(S["qk_std_done"], 1)
                sp(6)
                sp(7)
                act.wait_ge(used, c0 + C_SU + 2)
                act.activation(flat(su[:, :, :]), banks(0, 2), ACT.Copy).then_inc(S["su_copied"], 1)
                sp(8)
                sp(9)
                act.wait_ge(used, c0 + C_AU + 2)
                act.activation(flat(u_t[:, :, :]), banks(2, 2), ACT.Copy).then_inc(S["u_copied"], 1)
                act.wait_ge(S["qkT_ps"], 2 * layer + 1)
                act.activation(flat(qkT[:, 0:4, :]), banks(6, 2), ACT.Copy).then_inc(S["qkT_copied"], 1)
                sp(10)
                act.wait_ge(S["qkT_ps"], 2 * layer + 2)
                act.activation(qkT[:, 4, :], ps[:, 6, 0:SEQ], ACT.Copy).then_inc(S["qkT_copied"], 1)
                sp(11)
                sp(12)
                softmax_exp(layer, 0)
                normalise(layer, 0)
                copy_pT(layer, 0)
                sp(13)
                copy_o(layer, 0)
                sp(14)
                softmax_exp(layer, 1)
                normalise(layer, 1)
                copy_pT(layer, 1)
                sp(15)
                act.wait_ge(S["conv_done"], layer + 1)
                act.activation(flat(yac_hi[:, :, :]), flat(u_t[:, :, :]), ACT.Copy).then_inc(S["ya_hi_done"], 1)
                copy_o(layer, 1)
                sp(16)
                sigmoid_gate(layer, C_GA, 0, 0)
                softmax_exp(layer, 2)
                sp(17)
                normalise(layer, 2)
                sigmoid_gate(layer, C_GA + 2, 1, 1)
                copy_pT(layer, 2)
                sp(18)
                copy_o(layer, 2)
                sp(19)
                softmax_exp(layer, 3)
                sp(20)
                normalise(layer, 3)
                copy_pT(layer, 3)
                sp(21)
                sigmoid_gate(layer, C_GC, 2, 0)
                copy_o(layer, 3)
                yc_hi(layer)
                sp(22)
                sp(23)
                sigmoid_gate(layer, C_GC + 2, 3, 1)
                sp(24)
                sp(25)
                sp(26)
                act.wait_ge(S["skip_done"], CT * (layer + 1))
                act.activation(flat(su[:, :, :]), flat(su[:, :, :]), ACT.Gelu_apprx_tanh).then_inc(S["gelu_done"], 1)
                act.wait_ge(S["gelu_done"], layer + 1)
                act.wait_ge(S["rotated"], SCHUNKS * (layer + 1))
                act.activation(flat(yb_hi[:, :, :]), flat(su[:, :, :]), ACT.Copy).then_inc(S["yg_hi_done"], 1)
                sp(27)
                sigmoid_gate(layer, C_GB, 4, 0)
                sp(28)
                act.wait_ge(used, c0 + C_GLU + 1)
                act.activation(flat(u_t[:, :, :]), banks(4, 2), ACT.Sigmoid).then_inc(S["glu_sig"], 1)
                sp(29)
                act.wait_ge(S["yb_made"], layer + 1)
                act.activation(flat(yb_hi[:, :, :]), flat(su[:, :, :]), ACT.Copy).then_inc(S["yb_hi_done"], 1)
                sp(30)
                sigmoid_gate(layer, C_GB2, 5, 1)
                sp(31)
                sp(32)
                sp(33)
                turned_hi(layer, S["mixT_ps"], 4, S["mixT_hi_done"])
                sp(34)

            def silu(i, after, width=HALF):
                act.wait_ge(used, after)
                act.wait_ge(S["hid_done"], i)
                act.activation(sil[:, 0:width], ps[:, 0, 0:width], ACT.Silu).then_inc(S["sil_done"], 1)

            def hidden_hi(i, bank):
                act.wait_ge(S["hidT_ps"], i + 1)
                act.activation(hidT_hi[:, :], ps[:, bank, :], ACT.Copy).then_inc(S["hidT_hi_done"], 1)

            def dense():
                n = DENSE0
                split_hi(act, n)
                split_hi(act, n + 1)
                norm(1)
                split_hi(act, n + 2)
                turned_hi(1, S["hT_ps"], 0, S["hT_hi_done"])
                split_hi(act, n + 3)
                silu(0, n + 1)
                split_hi(act, n + 4)
                step_sizes(1)
                hidden_hi(0, 2)
                decays(1)
                with act.Fori(0, (DENSE_STRIPES - 3) // 2) as t:
                    for h in range(2):
                        m = n + 5 + 3 * h
                        split_hi(act, m, t)
                        silu(2 * t + h + 1, n + 3 + 3 * h + 6 * t)
                        split_hi(act, m + 1, t)
                        split_hi(act, m + 2, t)
                        hidden_hi(2 * t + h + 1, 2)
                last = n + 5 + 6 * ((DENSE_STRIPES - 3) // 2)
                i = DENSE_STRIPES - 2
                split_hi(act, last)
                silu(i, last - 2 + 0)
                split_hi(act, last + 1)
                split_hi(act, last + 2)
                hidden_hi(i, 2)
                split_hi(act, last + 3)
                silu(i + 1, last + 1)
                hidden_hi(i + 1, 2)

            def route():
                norm(3)
                turned_hi(3, S["hT_ps"], 0, S["hT_hi_done"])
                for b in range(BLOCKS):
                    act.activation(h_hi[:, b, :], h_tok[:, b, :], ACT.Copy).then_inc(S["h_hi_done"], 1)
                act.wait_ge(S["top_r"], 1)
                act.activation(flat(rt[:, 2]), flat(rt[:, 1]), ACT.Exp).then_inc(S["exp_r"], 1)

            def experts(rnd):
                n0 = MOE0 + rnd * EXPERTS * MOE_CHUNKS
                e0 = rnd * EXPERTS
                i0 = DENSE_STRIPES + e0 * MOE_STRIPES

                def xg(e):
                    act.wait_ge(S["gather_ps"], 2 * (e0 + e) + 1)
                    act.activation(flat(xg_hi[:, :, :]), banks(4, 2), ACT.Copy).then_inc(S["xg_hi_done"], 1)

                def stripe(i, t, turns):
                    split_hi(act, n0 + 6, turns)
                    hidden_hi(i + t - 1, 4)
                    split_hi(act, n0 + 7, turns)
                    silu(i + t, n0 + 6 + 6 * turns)
                    split_hi(act, n0 + 8, turns)
                    split_hi(act, n0 + 9, turns)

                def expert(e, last):
                    i = i0 + MOE_STRIPES * e
                    turns = MOE_STRIPES * e
                    stripe(i, 1, turns)
                    split_hi(act, n0 + 10, turns)
                    split_hi(act, n0 + 11, turns)
                    act.wait_ge(S["pickT_ps"], e0 + e + 1)
                    act.activation(flat(pickT[:, :, :]), ps[:, 5, 0:2 * P], ACT.Copy).then_inc(S["pickT_done"], 1)
                    with act.Fori(2, MOE_STRIPES - 1) as t:
                        stripe(i, t, turns + t - 1)
                        split_hi(act, n0 + 10, turns + t - 1)
                        split_hi(act, n0 + 11, turns + t - 1)
                    t = MOE_STRIPES - 1
                    stripe(i, t, turns + t - 1)
                    split_hi(act, n0 + 10, turns + t - 1)
                    if not last:
                        xg(e + 1)
                    split_hi(act, n0 + 11, turns + t - 1)
                    if not last:
                        split_hi(act, n0 + 6, turns + t)
                    hidden_hi(i + t, 4)
                    if not last:
                        split_hi(act, n0 + 7, turns + t)
                        silu(i + t + 1, n0 + 6 + 6 * (turns + t))
                        split_hi(act, n0 + 8, turns + t)
                        split_hi(act, n0 + 9, turns + t)
                    act.wait_ge(used, n0 + (6 if last else 8) + 6 * (turns + t))
                    act.activation(y_hi[:, :], banks(2, 2), ACT.Copy).then_inc(S["y_hi_done"], 1)
                    if not last:
                        split_hi(act, n0 + 10, turns + t)
                        split_hi(act, n0 + 11, turns + t)

                split_hi(act, n0)
                xg(0)
                split_hi(act, n0 + 1)
                split_hi(act, n0 + 2)
                split_hi(act, n0 + 3)
                silu(i0, n0 + 2)
                split_hi(act, n0 + 4)
                split_hi(act, n0 + 5)
                with act.Fori(0, EXPERTS - 1) as e:
                    expert(e, False)
                expert(EXPERTS - 1, True)

            mixer(0)
            dense()
            mixer(1)
            route()
            experts(0)
            act.wait_ge(S["most_done"], 1)
            most_tokens = act.value_load(most_i[0:1, 0:1])
            with act.If(most_tokens > SLOTS):
                experts(1)

        @block.vector
        def _(dve):
            own = Chain(dve, dve_step)

            def norm(i, gains):
                dve.wait_ge(S["ss_done"], BLOCKS * (i + 1))
                dve.tensor_scalar(norm_ss[:, 1, :], norm_ss[:, 0, :], 1.0 / D, EPS, ALU.mult, ALU.add)\
                   .then_inc(S["var_done"], 1)
                dve.wait_ge(S["std_done"], i + 1)
                own.then(dve.reciprocal(norm_ss[:, 3, :], norm_ss[:, 2, :]))
                dve.wait_ge(S["gain_loaded"], 16 * (i + 1))
                for b in range(BLOCKS):
                    dve.scalar_tensor_tensor(h_tok[:, b, :], x_tok[:, b, :], norm_ss[:, 3, b:b + 1], gains,
                                             ALU.mult, ALU.mult).then_inc(S["h_done"], 1)

            def turned_lo(i, ready, bank, done):
                for q in range(4):
                    dve.wait_ge(ready, 4 * i + q + 1)
                    dve.tensor_tensor(flat(hT_lo[:, 2 * q:2 * q + 2, :]), ps[:, bank + q, :],
                                      flat(hT_hi[:, 2 * q:2 * q + 2, :]).bitcast(F32), ALU.subtract).then_inc(done, 1)

            def rotate_in(layer, j):
                n = SCHUNKS * layer + j
                dve.wait_ge(S["bu_ps"], n + 1)
                if layer == 0:
                    dve.wait_ge(S["table_done"], 2 * (j + 1))
                else:
                    dve.wait_ge(S[f"table_loaded{j % 2}"], 16 * (j // 2 + 1))
                if n >= 2:
                    dve.wait_ge(S["rotated"], n - 1)
                t = turn[:, j % 2]
                cos, sin = table[:, j % 2, 0, :], table[:, j % 2, 1, :]
                re, im = ps[:, 4, 0:SEQ], ps[:, 4, SEQ:2 * SEQ]
                own.step(dve.tensor_tensor(t[:, 0, :], re, cos, ALU.mult))
                own.step(dve.tensor_tensor(t[:, 1, :], im, sin, ALU.mult))
                own.step(dve.tensor_tensor(t[:, 2, :], im, cos, ALU.mult))
                dve.tensor_tensor(t[:, 3, :], re, sin, ALU.mult).then_inc(S["turned"], 1)
                own.join()
                own.step(dve.tensor_tensor(t[:, 0, :], t[:, 0, :], t[:, 1, :], ALU.add))
                dve.wait_ge(S["turned"], n + 1)
                own.step(dve.tensor_tensor(t[:, 2, :], t[:, 2, :], t[:, 3, :], ALU.subtract))
                own.join()
                mag = trig[:, 3, j:j + 1].broadcast_to([P, SEQ])
                dve.tensor_tensor_scan(t[:, 1, :], mag, t[:, 0, :], 0.0, ALU.mult, ALU.add).then_inc(S["scanned"], 1)
                dve.tensor_tensor_scan(t[:, 3, :], mag, t[:, 2, :], 0.0, ALU.mult, ALU.add).then_inc(S["scanned"], 1)

            def add_skip(layer, c):
                dve.wait_ge(S["y_ps"], SCHUNKS * layer + 4 * c + 4)
                at = (c % 2) * SEQ
                dve.scalar_tensor_tensor(su[:, c, :], su[:, c, :], par_sb[:, PAR_D + c:PAR_D + c + 1],
                                         ps[:, 5, at:at + SEQ], ALU.mult, ALU.add).then_inc(S["skip_done"], 1)

            def conv(layer):
                u2 = u_t
                for tap in range(3):
                    for c in range(CT):
                        w = par_sb[:, PAR_CW + tap * CT + c:PAR_CW + tap * CT + c + 1]
                        v = v_t[:, c, tap:tap + SEQ]
                        if tap == 0:
                            own.step(dve.tensor_scalar(u2[:, c, :], v, w, None, ALU.mult))
                        else:
                            own.step(dve.scalar_tensor_tensor(u2[:, c, :], v, w, u2[:, c, :], ALU.mult, ALU.add))
                    own.join()
                dve.wait_ge(used, MIX0[layer] + C_AB + 2)
                dve.tensor_tensor(flat(u_t[:, :, :]), flat(u_t[:, :, :]), banks(2, 2), ALU.mult)\
                   .then_inc(S["conv_done"], 1)

            def score(layer, b):
                dve.wait_ge(S["idx_ps"], 2 * layer + b + 1)
                keys = (b + 1) * P
                sc, tmp = scratch[:, 0, 0:keys], scratch[:, 1, 0:keys]
                for h in range(IDX_HEADS):
                    at = (h // 2) * keys
                    src = ps[:, 6 + h % 2, at:at + keys]
                    ins = dve.tensor_scalar(sc if h == 0 else scratch[:, h, 0:keys], src, 0.0,
                                            wi_sb[:, b, h:h + 1], ALU.max, ALU.mult)
                    if h < IDX_HEADS - 1:
                        own.step(ins)
                    else:
                        ins.then_inc(S["scored"], 1)
                own.join()
                dve.wait_ge(S["scored"], 2 * layer + b + 1)
                own.step(dve.tensor_tensor(sc, sc, tmp, ALU.add))
                own.then(dve.tensor_tensor(scratch[:, 2, 0:keys], scratch[:, 2, 0:keys], scratch[:, 3, 0:keys],
                                           ALU.add))
                own.then(dve.tensor_tensor(sc, sc, scratch[:, 2, 0:keys], ALU.add))
                diag = sc[:, b * P:keys]
                own.then(dve.tensor_tensor(diag, diag, causal[:, :], ALU.add))

            def choose(layer, b):
                keys = (b + 1) * P
                sc, work = scratch[:, 0, 0:keys], scratch[:, 1, 0:keys]
                gt, eq = scratch[:, 2, 0:keys], scratch[:, 3, 0:keys]
                src = sc
                for r in range(TOPK // 8):
                    own.then(dve.max(top8[:, :], src))
                    if r < TOPK // 8 - 1:
                        own.then(dve.match_replace(work, top8[:, :], src, DEAD))
                    src = work
                kth = top8[:, 7:8]
                own.step(dve.tensor_scalar(gt, sc, kth, None, ALU.is_gt))
                own.then(dve.tensor_scalar(eq, sc, kth, None, ALU.is_equal))
                own.step(dve.tensor_reduce(smalls[:, 0:1], gt, AX_X, ALU.add))
                own.then(dve.tensor_tensor_scan(work, ones_row(keys), eq, 0.0, ALU.mult, ALU.add))
                own.then(dve.tensor_scalar(smalls[:, 1:2], smalls[:, 0:1], -1.0, float(TOPK), ALU.mult, ALU.add))
                own.then(dve.scalar_tensor_tensor(work, work, smalls[:, 1:2], eq, ALU.is_le, ALU.mult))
                own.then(dve.tensor_tensor(work, work, gt, ALU.add))
                bias = keybias[:, b, 0:keys]
                own.then(dve.tensor_scalar(bias, work, -NEG, NEG, ALU.mult, ALU.add))
                diag = keybias[:, b, b * P:keys]
                own.then(dve.tensor_tensor(diag, diag, causal[:, :], ALU.add))

            def ones_row(width):
                return ones[:, 0:1].broadcast_to([P, width])

            def shift(layer, i):
                n, b = 4 * layer + i, i // 2
                keys = (b + 1) * P
                dve.wait_ge(S["logit_ps"], n + 1)
                dst = probs[:, :, 0:keys]
                bias = keybias[:, b:b + 1, 0:keys].broadcast_to([P, 2, keys])
                for odd in range(2):
                    src = ps[:, 6 + odd, 0:2 * keys].rearrange("p (h k) -> p h k", h=2)
                    own.step(dve.scalar_tensor_tensor(dst[:, 2 * odd:2 * odd + 2, :], src, HD ** -0.5, bias,
                                                      ALU.mult, ALU.add))
                own.join()
                own.then(dve.tensor_reduce(rowinv[:, :], dst, AX_X, ALU.max))
                dve.tensor_scalar(rowmax[:, :], rowinv[:, :], -1.0, None, ALU.mult).then_inc(S["shifted"], 1)

            def invert_sums(layer, i):
                n = 4 * layer + i
                dve.wait_ge(S["exp_done"], 4 * (n + 1))
                dve.reciprocal(rowinv[:, :], rowsum[:, :]).then_inc(S["row_inv_done"], 1)

            def merge(layer, branch, c):
                dve.wait_ge(used, MIX0[layer] + c + 2)
                dve.wait_ge(S["gate_done"], 6 * layer + 2 * (branch + 1))
                y = banks(0, 4)
                if branch == 0:
                    dve.tensor_tensor(flat(mixed[:, :, :]), flat(gate[:, :, :]), y, ALU.mult).then_inc(S["gated"], 1)
                    return
                dve.tensor_tensor(flat(gate[:, :, :]), flat(gate[:, :, :]), y, ALU.mult).then_inc(S["gated"], 1)
                dve.wait_ge(S["gated"], 3 * layer + branch + 1)
                if branch == 2:
                    dve.wait_ge(S["mixed_done"], 2 * layer + 1)
                dve.tensor_tensor(flat(mixed[:, :, :]), flat(mixed[:, :, :]), flat(gate[:, :, :]), ALU.add)\
                   .then_inc(S["mixed_done"], 1)

            def sub_hi(dst, whole, hi, done):
                dve.tensor_tensor(dst, whole, hi.bitcast(F32), ALU.subtract).then_inc(done, 1)

            def invert_den(layer):
                dve.wait_ge(S["den_done"], layer + 1)
                dve.reciprocal(trig_row(INV), trig_row(DEN)).then_inc(S["den_inv"], 1)

            def mixer(layer):
                c0 = MIX0[layer]
                chunk = lambda c: split_lo(dve, c0 + c, width=mix_width(layer, c))
                turn_j = lambda j: rotate_in(layer, j)
                if layer == 0:
                    norm(0, gain_row)
                    s5_rates(dve, own, 0)
                    invert_den(0)
                    chunk(0)
                else:
                    chunk(0)
                    norm(2 * layer, gain_row)
                chunk(1)
                chunk(2)
                dve.wait_ge(S["hT_hi_done"], 4 * (2 * layer + 1))
                turned_lo(2 * layer, S["hT_ps"], 0, S["hT_lo_done"])
                if layer == 0:
                    s5_angles(dve, own, 0)
                    s5_powers(dve, own)
                    dve.wait_ge(S["powers_done"], 1)
                chunk(3)
                chunk(4)
                if layer == 0:
                    s5_fold(dve, own, 0)
                chunk(5)
                dve.wait_ge(S["sq_done"], 3 * (layer + 1))
                own.then(dve.tensor_reduce(qk_ss[:, 2, :, :], gate_sq, AX_X, ALU.add))
                dve.tensor_scalar(qk_ss[:, 0, :, :], qk_ss[:, 2, :, :], 1.0 / HD, EPS, ALU.mult, ALU.add)\
                   .then_inc(S["qk_ss_done"], 1)
                dve.wait_ge(S["qk_std_done"], layer + 1)
                dve.reciprocal(qk_ss[:, 2, :, :], qk_ss[:, 1, :, :]).then_inc(S["qk_inv_done"], 1)
                chunk(6)
                score(layer, 0)
                chunk(7)
                choose(layer, 0)
                chunk(8)
                score(layer, 1)
                turn_j(0)
                chunk(9)
                choose(layer, 1)
                turn_j(1)
                chunk(10)
                turn_j(2)
                chunk(11)
                shift(layer, 0)
                own.then(dve.memset(v_t[:, :, 0:2], 0.0))
                dve.wait_ge(used, c0 + C_AC + 2)
                dve.wait_ge(S["u_copied"], layer + 1)
                dve.tensor_tensor(v_t[:, :, 2:SEQ + 2], u_t[:, :, :],
                                  banks(0, 2).rearrange("p (c n) -> p c n", c=CT), ALU.mult).then_inc(S["v_made"], 1)
                turn_j(3)
                chunk(12)
                invert_sums(layer, 0)
                turn_j(4)
                chunk(13)
                shift(layer, 1)
                turn_j(5)
                chunk(14)
                invert_sums(layer, 1)
                dve.wait_ge(S["v_made"], layer + 1)
                conv(layer)
                add_skip(layer, 0)
                turn_j(6)
                chunk(15)
                dve.wait_ge(S["ya_hi_done"], layer + 1)
                sub_hi(flat(yac_lo[:, :, :]), flat(u_t[:, :, :]), flat(yac_hi[:, :, :]), S["ya_lo_done"])
                turn_j(7)
                shift(layer, 2)
                chunk(16)
                turn_j(8)
                invert_sums(layer, 2)
                chunk(17)
                turn_j(9)
                chunk(18)
                shift(layer, 3)
                add_skip(layer, 1)
                turn_j(10)
                chunk(19)
                invert_sums(layer, 3)
                merge(layer, 0, C_OA)
                turn_j(11)
                chunk(20)
                turn_j(12)
                chunk(21)
                turn_j(13)
                chunk(22)
                add_skip(layer, 2)
                dve.wait_ge(S["yc_hi_done"], layer + 1)
                sub_hi(flat(yac_lo[:, :, :]), flat(qkT[:, 0:4, :]), flat(yac_hi[:, :, :]), S["yc_lo_done"])
                turn_j(14)
                chunk(23)
                turn_j(15)
                chunk(24)
                chunk(25)
                merge(layer, 1, C_OC)
                chunk(26)
                add_skip(layer, 3)
                dve.wait_ge(S["yg_hi_done"], layer + 1)
                sub_hi(flat(yb_lo[:, :, :]), flat(su[:, :, :]), flat(yb_hi[:, :, :]), S["yg_lo_done"])
                chunk(27)
                chunk(28)
                dve.wait_ge(S["glu_sig"], layer + 1)
                dve.tensor_tensor(flat(su[:, :, :]), flat(su[:, :, :]), flat(u_t[:, :, :]), ALU.mult)\
                   .then_inc(S["yb_made"], 1)
                chunk(29)
                dve.wait_ge(S["yb_hi_done"], layer + 1)
                sub_hi(flat(yb_lo[:, :, :]), flat(su[:, :, :]), flat(yb_hi[:, :, :]), S["yb_lo_done"])
                chunk(30)
                chunk(31)
                chunk(32)
                chunk(33)
                merge(layer, 2, C_OB)
                dve.wait_ge(S["mixT_hi_done"], 4 * (layer + 1))
                turned_lo(layer, S["mixT_ps"], 4, S["mixT_lo_done"])
                chunk(34)
                add_x(c0 + MIX_CHUNKS, 0)

            def add_x(after, bank):
                dve.wait_ge(used, after)
                dve.tensor_tensor(flat(x_tok[:, :, :]), flat(x_tok[:, :, :]), banks(bank, 4), ALU.add)\
                   .then_inc(S["x_added"], 1)

            def times_up(sil_seen, w3_used, turned, width=HALF):
                dve.wait_ge(S["sil_done"], sil_seen)
                dve.wait_ge(used, w3_used)
                if turned is not None:
                    dve.wait_ge(S["hidT_ps"], turned)
                dve.tensor_tensor(hid[:, 0:width], sil[:, 0:width], ps[:, 1, 0:width], ALU.mult)\
                   .then_inc(S["hid_done"], 1)

            def hidden_lo(seen, bank):
                dve.wait_ge(S["hidT_hi_done"], seen)
                dve.tensor_tensor(hidT_lo[:, :], ps[:, bank, :], hidT_hi[:, :].bitcast(F32), ALU.subtract)\
                   .then_inc(S["hidT_lo_done"], 1)

            def dense():
                n = DENSE0
                split_lo(dve, n)
                split_lo(dve, n + 1)
                norm(1, gain_ff[:, :])
                split_lo(dve, n + 2)
                dve.wait_ge(S["hT_hi_done"], 8)
                turned_lo(1, S["hT_ps"], 0, S["hT_lo_done"])
                split_lo(dve, n + 3)
                split_lo(dve, n + 4)
                times_up(1, n + 2, None)
                split_lo(dve, n + 5)
                hidden_lo(1, 2)
                split_lo(dve, n + 6)
                invert_den(1)
                with dve.Fori(0, (DENSE_STRIPES - 3) // 2) as t:
                    hi_at = [dve.snap(n + 7 + k + 1 + 6 * t) for k in range(6)]
                    w3_at = [dve.snap(n + 4 + 3 * h + 6 * t) for h in range(2)]
                    i_at = [dve.snap(2 * t + k) for k in range(1, 4)]
                    for h in range(2):
                        m = n + 7 + 3 * h
                        times_up(i_at[h + 1], w3_at[h], i_at[h])
                        split_lo(dve, m, hi_at[3 * h])
                        split_lo(dve, m + 1, hi_at[3 * h + 1])
                        hidden_lo(i_at[h + 1], 2)
                        split_lo(dve, m + 2, hi_at[3 * h + 2])
                m = n + 7 + 6 * ((DENSE_STRIPES - 3) // 2)
                i = DENSE_STRIPES - 2
                times_up(i + 1, m - 3, i)
                split_lo(dve, m)
                split_lo(dve, m + 1)
                hidden_lo(i + 1, 2)
                times_up(i + 2, m, i + 1)
                hidden_lo(i + 2, 2)
                add_x(n + DENSE_CHUNKS, 4)

            def route():
                norm(3, gain_ff[:, :])
                dve.wait_ge(S["hT_hi_done"], 16)
                turned_lo(3, S["hT_ps"], 0, S["hT_lo_done"])
                for b in range(BLOCKS):
                    dve.wait_ge(S["h_hi_done"], b + 1)
                    dve.tensor_tensor(h_lo[:, b, :], h_tok[:, b, :], h_hi[:, b, :].bitcast(F32), ALU.subtract)\
                       .then_inc(S["h_lo_done"], 1)
                dve.wait_ge(S["logits_ps"], 1)
                lg, shifted_l, ex, gt, eq, rank, keep, sel, tmp = (rt[:, k] for k in range(9))
                own.then(dve.tensor_copy(flat(lg), ps[:, 4, 0:16]))
                for b in range(BLOCKS):
                    own.step(dve.max(rt8[:, b, :], lg[:, b, :]))
                own.join()
                for b in range(BLOCKS):
                    own.step(dve.tensor_scalar(gt[:, b, :], lg[:, b, :], rt8[:, b, 1:2], None, ALU.is_gt))
                    own.step(dve.tensor_scalar(eq[:, b, :], lg[:, b, :], rt8[:, b, 1:2], None, ALU.is_equal))
                    own.step(dve.tensor_scalar(shifted_l[:, b, :], lg[:, b, :], rt8[:, b, 0:1], None, ALU.subtract))
                own.join()
                dve.tensor_reduce(rts[:, 0, :], gt, AX_X, ALU.add).then_inc(S["top_r"], 1)
                for b in range(BLOCKS):
                    own.step(dve.tensor_tensor_scan(rank[:, b, :], ones_row(EXPERTS), eq[:, b, :], 0.0, ALU.mult,
                                                    ALU.add))
                dve.wait_ge(S["top_r"], 1)
                own.then(dve.tensor_scalar(rts[:, 1, :], rts[:, 0, :], -1.0, 2.0, ALU.mult, ALU.add))
                for b in range(BLOCKS):
                    own.step(dve.scalar_tensor_tensor(keep[:, b, :], rank[:, b, :], rts[:, 1, b:b + 1], eq[:, b, :],
                                                      ALU.is_le, ALU.mult))
                own.join()
                dve.tensor_tensor(flat(sel), flat(keep), flat(gt), ALU.add).then_inc(S["picked"], 1)
                dve.wait_ge(S["picked"], 1)
                dve.wait_ge(S["exp_r"], 1)
                own.then(dve.tensor_tensor(flat(tmp), flat(ex), flat(sel), ALU.mult))
                own.then(dve.tensor_reduce(rts[:, 2, :], tmp, AX_X, ALU.add))
                own.then(dve.reciprocal(rts[:, 3, :], rts[:, 2, :]))
                for b in range(BLOCKS):
                    own.step(dve.tensor_scalar(gate_of[:, b, :], tmp[:, b, :], rts[:, 3, b:b + 1], None, ALU.mult))
                dve.wait_ge(S["rank_ps"], 1)
                own.step(dve.tensor_reduce(most[:, :], ps[:, 5, 16:24], AX_X, ALU.max))
                dve.memset(slot_of[:, :, :], -1.0).then_inc(S["acc_done"], 1)
                dve.wait_ge(S["acc_done"], 1)
                own.then(dve.tensor_tensor(flat(rank), ps[:, 5, 0:16], flat(sel), ALU.mult))
                dve.tensor_scalar(slot_of[:, :, 0:EXPERTS], rank, -1.0, None, ALU.add).then_inc(S["slots_done"], 1)
                dve.wait_ge(S["slots_done"], 1)
                dve.tensor_copy(most_i[:, :], most[0:1, :]).then_inc(S["most_done"], 1)

            def pick_slots(e, rnd):
                for b in range(BLOCKS):
                    dve.tensor_scalar(pick[:, b, :], slot_id[:, rnd, :], slot_of[:, b, bass.ds(e, 1)], None,
                                      ALU.is_equal).then_inc(S["pick_done"], 1)

            def experts(rnd):
                n0 = MOE0 + rnd * EXPERTS * MOE_CHUNKS
                e0 = rnd * EXPERTS
                i0 = DENSE_STRIPES + e0 * MOE_STRIPES

                def lo(n, turns):
                    split_lo(dve, n, value(dve, n + 1 + 6 * turns))

                def xg(e):
                    seen = value(dve, 2 * (e0 + e + 1))
                    dve.wait_ge(S["gather_ps"], seen)
                    dve.tensor_copy(flat(xg_lo[:, :, :]), banks(6, 2)).then_inc(S["xg_lo_done"], 1)

                def stripe(i, t, turns):
                    prev, this = value(dve, i + t), value(dve, i + t + 1)
                    w3_at = value(dve, n0 + 8 + 6 * turns)
                    lo(n0 + 6, turns)
                    hidden_lo(prev, 4)
                    lo(n0 + 7, turns)
                    lo(n0 + 8, turns)
                    lo(n0 + 9, turns)
                    times_up(this, w3_at, prev)

                def y(e, y_used):
                    e_at = value(dve, e0 + e + 1)
                    dve.wait_ge(used, y_used)
                    dve.wait_ge(S["y_hi_done"], e_at)
                    dve.tensor_tensor(y_lo[:, :], banks(2, 2), y_hi[:, :].bitcast(F32), ALU.subtract)\
                       .then_inc(S["y_lo_done"], 1)

                def add_to_x(e):
                    e_at, a_at = value(dve, e0 + e + 1), value(dve, 4 * (e0 + e) + 1)
                    dve.wait_ge(S["scatter_ps"], e_at)
                    dve.wait_ge(S["acc_done"], a_at)
                    for b in range(BLOCKS):
                        for half in range(2):
                            dst = x_tok[:, b, half * HALF:(half + 1) * HALF]
                            dve.scalar_tensor_tensor(dst, ps[:, 2 + half if b == 0 else 6 + half, :],
                                                     gate_of[:, b, bass.ds(e, 1)], dst, ALU.mult, ALU.add)\
                               .then_inc(S["acc_done"], 1)

                def expert(e, last):
                    i = i0 + MOE_STRIPES * e
                    turns = MOE_STRIPES * e
                    stripe(i, 1, turns)
                    lo(n0 + 10, turns)
                    if not last:
                        e_at = value(dve, e0 + e + 1)
                        dve.wait_ge(S["pickT_ps"], e_at)
                        pick_slots(value(dve, e + 1), rnd)
                    lo(n0 + 11, turns)
                    with dve.Fori(2, MOE_STRIPES - 1) as t:
                        stripe(i, t, turns + t - 1)
                        lo(n0 + 10, turns + t - 1)
                        lo(n0 + 11, turns + t - 1)
                    t = MOE_STRIPES - 1
                    stripe(i, t, turns + t - 1)
                    lo(n0 + 10, turns + t - 1)
                    if not last:
                        xg(e + 1)
                    lo(n0 + 11, turns + t - 1)
                    if last:
                        hidden_lo(i + t + 1, 4)
                        y(e, n0 + 6 + 6 * (turns + t))
                        add_to_x(e)
                        return
                    turned, y_used = value(dve, i + t + 1), value(dve, n0 + 8 + 6 * (turns + t))
                    next_i, w3_at = value(dve, i + t + 2), value(dve, n0 + 10 + 6 * (turns + t))
                    lo(n0 + 6, turns + t)
                    hidden_lo(turned, 4)
                    lo(n0 + 7, turns + t)
                    lo(n0 + 8, turns + t)
                    lo(n0 + 9, turns + t)
                    y(e, y_used)
                    lo(n0 + 10, turns + t)
                    times_up(next_i, w3_at, turned)
                    lo(n0 + 11, turns + t)
                    add_to_x(e)

                dve.wait_ge(S["slots_loaded"], 16)
                pick_slots(0, rnd)
                lo(n0, 0)
                xg(0)
                for k in range(1, 5):
                    lo(n0 + k, 0)
                times_up(i0 + 1, n0 + 4, i0)
                lo(n0 + 5, 0)
                with dve.Fori(0, EXPERTS - 1) as e:
                    expert(e, False)
                expert(EXPERTS - 1, True)

            gate_sq = flat(gate[:, :, :]).rearrange("p (b h d) -> p b h d", b=BLOCKS, d=HD)[:, :, 0:10, :]
            mixer(0)
            dense()
            mixer(1)
            route()
            experts(0)
            dve.wait_ge(S["most_done"], 1)
            most_tokens = dve.value_load(most_i[0:1, 0:1])
            with dve.If(most_tokens > SLOTS):
                experts(1)
                dve.wait_ge(S["acc_done"], 4 * 2 * EXPERTS + 1)
            dve.wait_ge(S["acc_done"], 4 * EXPERTS + 1)
            dve.tensor_copy(most[:, :], ones[:, 0:1]).then_inc(S["final_done"], 1)

        @block.gpsimd
        def _(pool):
            own = Chain(pool, pool_step)

            def constants():
                for t in (ident, upper, causal):
                    own.step(pool.memset(t[:, :], 1.0 if t is upper else 0.0))
                pool.memset(ones[:, :], 1.0).then_inc(S["consts"], 1)
                pool.memset(zero_r[:, :].bitcast(F32), 0.0).then_inc(S["consts"], 1)
                own.join()
                pool.affine_select(out=ident[:, :], in_=ident[:, :], compare_op=ALU.not_equal, fill=1.0, base=0,
                                   pattern=[[-1, P]], channel_multiplier=1).then_inc(S["consts"], 1)
                pool.affine_select(out=upper[:, :], in_=upper[:, :], compare_op=ALU.is_ge, fill=0.0, base=0,
                                   pattern=[[1, P]], channel_multiplier=-1).then_inc(S["consts"], 1)
                pool.affine_select(out=causal[:, :], in_=causal[:, :], compare_op=ALU.is_ge, fill=NEG, base=0,
                                   pattern=[[-1, P]], channel_multiplier=1).then_inc(S["consts"], 1)

            def load_gain(i, dst):
                pool.dma_start(dst, gains[i].partition_broadcast(P)).then_inc(S["gain_loaded"], 16)

            def make_table(layer, j):
                n = SCHUNKS * layer + j
                if layer == 0 and j >= 2:
                    pool.wait_ge(S["turned"], j - 1)
                if layer == 1 and j >= 2:
                    pool.wait_ge(S[f"table_stored{j % 2}"], 16 * (j // 2))
                a_r, a_i = (pow_a[:, i, :, j:j + 1].broadcast_to([P, 16, 16]) for i in range(2))
                b_r, b_i = (pow_b[:, i, :, j].unsqueeze(1).broadcast_to([P, 16, 16]) for i in range(2))
                cos, sin = (table[:, j % 2, i, :].rearrange("p (a b) -> p a b", a=16) for i in range(2))
                s1, s2 = (pool_t[:, i, :].rearrange("p (a b) -> p a b", a=16) for i in range(2))
                own.step(pool.tensor_tensor(s1, a_r, b_r, ALU.mult))
                own.then(pool.tensor_tensor(s2, a_i, b_i, ALU.mult))
                pool.tensor_tensor(cos, s1, s2, ALU.subtract).then_inc(S["table_done"], 1)
                pool.wait_ge(S["table_done"], 2 * n + 1)
                own.step(pool.tensor_tensor(s1, a_r, b_i, ALU.mult))
                own.then(pool.tensor_tensor(s2, a_i, b_r, ALU.mult))
                pool.tensor_tensor(sin, s1, s2, ALU.add).then_inc(S["table_done"], 1)
                pool.wait_ge(S["table_done"], 2 * n + 2)

            def store_table(j):
                make_table(1, j)
                pool.dma_start(table_store[j], flat_table(j)).then_inc(S[f"table_stored{j % 2}"], 16)

            def load_table(j):
                pool.wait_ge(S[f"table_stored{j % 2}"], 16 * (SCHUNKS // 2))
                if j >= 2:
                    pool.wait_ge(S["turned"], SCHUNKS + j - 1)
                pool.dma_start(flat_table(j), table_store[j]).then_inc(S[f"table_loaded{j % 2}"], 16)

            def flat_table(j):
                return table[:, j % 2, :, :].rearrange("p a t -> p (a t)")

            def rotate_out(layer, j):
                n = SCHUNKS * layer + j
                pool.wait_ge(S["scanned"], 2 * (n + 1))
                if layer == 1:
                    pool.wait_ge(S[f"table_loaded{j % 2}"], 16 * (j // 2 + 1))
                if n >= 1:
                    pool.wait_ge(S["y_ps"], n)
                g_re, g_im = turn[:, j % 2, 1, :], turn[:, j % 2, 3, :]
                cos, sin = table[:, j % 2, 0, :], table[:, j % 2, 1, :]
                own.step(pool.tensor_tensor(pool_t[:, 0, :], g_re, cos, ALU.mult))
                own.then(pool.tensor_tensor(pool_t[:, 1, :], g_im, sin, ALU.mult))
                own.then(pool.tensor_tensor(state[:, 0, :], pool_t[:, 0, :], pool_t[:, 1, :], ALU.subtract))
                own.step(pool.tensor_tensor(pool_t[:, 0, :], g_re, sin, ALU.mult))
                own.then(pool.tensor_tensor(pool_t[:, 1, :], g_im, cos, ALU.mult))
                pool.tensor_tensor(state[:, 1, :], pool_t[:, 0, :], pool_t[:, 1, :], ALU.add).then_inc(S["rotated"], 1)
                pool.wait_ge(S["rotated"], n + 1)

            def rotary(lo, heads, done):
                cols = slice(lo * HD, (lo + heads) * HD)
                for b in range(BLOCKS):
                    xv = h_tok[:, b, cols].rearrange("p (h i d) -> p h i d", i=2, d=32)
                    tv = gate[:, b, cols].rearrange("p (h i d) -> p h i d", i=2, d=32)
                    for i in range(2):
                        sin = rope_sb[:, b, 1 + i, :].unsqueeze(1).broadcast_to([P, heads, 32])
                        own.step(pool.tensor_tensor(tv[:, :, i, :], xv[:, :, 1 - i, :], sin, ALU.mult))
                    own.join()
                    cos = rope_sb[:, b, 0:1, :].broadcast_to([P, 2 * heads, 32])
                    x3 = h_tok[:, b, cols].rearrange("p (h d) -> p h d", d=32)
                    own.then(pool.tensor_tensor(x3, x3, cos, ALU.mult))
                    pool.tensor_tensor(h_tok[:, b, cols], h_tok[:, b, cols], gate[:, b, cols], ALU.add)\
                        .then_inc(S[done], 1)

            def index_rope(layer):
                pool.wait_ge(S["kv_copied"], 7 * layer + 3)
                if layer == 0:
                    pool.wait_ge(S["rope_loaded"], 16)
                rotary(10, 6, "idx_rope_done")

            def norm_and_rope(layer):
                pool.wait_ge(S["qk_inv_done"], layer + 1)
                pool.wait_ge(S["q_copied"], layer + 1)
                pool.wait_ge(S["kv_copied"], 7 * layer + 5)
                heads = qk[:, :, 0:10, :]
                own.then(pool.tensor_tensor(heads, heads, qk_ss[:, 2, :, :].unsqueeze(3)
                                            .broadcast_to([P, BLOCKS, 10, HD]), ALU.mult))
                gain = par_sb[:, PAR_GAIN:PAR_GAIN + 10 * HD].unsqueeze(1).broadcast_to([P, BLOCKS, 10 * HD])
                part = h_tok[:, :, 0:10 * HD]
                own.then(pool.tensor_tensor(part, part, gain, ALU.mult))
                rotary(0, 10, "rope_done")

            def mixer(layer):
                table_of = load_table if layer else lambda j: make_table(0, j)
                index_rope(layer)
                if layer == 0:
                    pool.wait_ge(S["powers_done"], 1)
                    table_of(0)
                norm_and_rope(layer)
                if layer == 0:
                    table_of(1)
                for j in range(SCHUNKS):
                    rotate_out(layer, j)
                    if j + 2 < SCHUNKS:
                        table_of(j + 2)

            pool.dma_start(par_sb[:, :], par[0]).then_inc(S["par_loaded"], 16)
            load_gain(0, gain_row)
            constants()
            mixer(0)
            pool.wait_ge(S["mixed_done"], 2)
            load_gain(1, gain_ff[:, :])
            pool.wait_ge(S["x_added"], 1)
            pool.dma_start(par_sb[:, :], par[1]).then_inc(S["par_loaded"], 16)
            s5_rates(pool, own, 1)
            s5_angles(pool, own, 1)
            s5_powers(pool, own)
            pool.wait_ge(S["powers_done"], 2)
            s5_fold(pool, own, 1)
            for j in range(SCHUNKS):
                store_table(j)
            load_table(0)
            load_table(1)
            pool.wait_ge(S["x_added"], 2)
            load_gain(2, gain_row)
            mixer(1)
            pool.wait_ge(S["mixed_done"], 4)
            load_gain(3, gain_ff[:, :])
            pool.wait_ge(S["x_added"], 3)
            pool.dma_start(router_sb[:, :, :], router_w[0].rearrange("(k p) e -> p k e", p=P))\
                .then_inc(S["router_loaded"], 16)
            pool.dma_start(slot_id[:, :, :], slot_ids.rearrange("p (r s) -> p r s", r=2)).then_inc(S["slots_loaded"], 16)


def rope_rows():
    pos = np.arange(SEQ, dtype=np.float32)
    inv = np.float32(10000.0) ** (-np.arange(HD // 2, dtype=np.float32) / np.float32(HD // 2))
    ang = (pos[:, None] * inv[None, :].astype(np.float32)).astype(np.float32)
    t = np.stack([np.cos(ang), -np.sin(ang), np.sin(ang)], 1).astype(np.float32)
    return np.ascontiguousarray(t.reshape(BLOCKS, P, 3, HD // 2).transpose(1, 0, 2, 3))


def small_parameters(i):
    groups = SSM // GROUP
    out = np.zeros((DEPTH, P, PAR_W), np.float32)
    states = lambda a: a.reshape(DEPTH, SCHUNKS, P).transpose(0, 2, 1)
    out[:, :, PAR_LRE:PAR_LRE + SCHUNKS] = states(i["ssm_lam_re"])
    out[:, :, PAR_LIM:PAR_LIM + SCHUNKS] = states(i["ssm_lam_im"])
    out[:, :, PAR_LDT:PAR_LDT + SCHUNKS] = states(np.repeat(i["ssm_log_dt"][:, :, None], STATE, 2))
    out[:, :, PAR_CW:PAR_CW + 3 * CT] = i["conv_w"].reshape(DEPTH, 3 * CT, P).transpose(0, 2, 1)
    out[:, :, PAR_D:PAR_D + CT] = i["ssm_d"].reshape(DEPTH, CT, P).transpose(0, 2, 1)
    gain = np.concatenate([np.tile(i["q_norm_g"], (1, HEADS)), np.tile(i["k_norm_g"], (1, 2))], 1)
    out[:, :, PAR_GAIN:PAR_GAIN + 10 * HD] = gain[:, None, :]
    c_re = out[:, :, PAR_CRE:PAR_CRE + SCHUNKS * 32].reshape(DEPTH, P, SCHUNKS, 32)
    c_im = np.zeros_like(c_re)
    c_re = np.zeros_like(c_re)
    b = np.zeros((DEPTH, P, CT, 2, P), np.float32)
    for g in range(groups):
        j, odd = g // 2, g % 2
        rows = slice(STATE * odd, STATE * odd + STATE)
        cols = slice(GROUP * odd, GROUP * odd + GROUP)
        c_re[:, rows, j, cols] = i["ssm_c_re"][:, g].transpose(0, 2, 1)
        c_im[:, rows, j, cols] = i["ssm_c_im"][:, g].transpose(0, 2, 1)
        at = slice(32 * (j % 4) + GROUP * odd, 32 * (j % 4) + GROUP * odd + GROUP)
        b[:, at, j // 4, 0, rows] = i["ssm_b_re"][:, g].transpose(0, 2, 1)
        b[:, at, j // 4, 1, rows] = i["ssm_b_im"][:, g].transpose(0, 2, 1)
    out[:, :, PAR_CRE:PAR_CRE + SCHUNKS * 32] = c_re.reshape(DEPTH, P, -1)
    out[:, :, PAR_CIM:PAR_CIM + SCHUNKS * 32] = c_im.reshape(DEPTH, P, -1)
    out[:, :, PAR_B:PAR_W] = b.reshape(DEPTH, P, -1)
    return out


def kernel(**inputs):
    import concourse.bacc as bacc
    from concourse.bass_utils import run_bass_kernel_spmd

    i = {name: np.asarray(a) for name, a in inputs.items()}
    slots = np.broadcast_to(np.arange(2 * P, dtype=np.float32), (P, 2 * P))
    arrays = {
        "x": i["x"], "gains": np.stack([i["ln1_g"], i["ln2_g"]], 1).reshape(2 * DEPTH, D), "w_in": i["w_in"],
        "par": small_parameters(i), "w_glu": i["ssm_w_glu"], "w_out_a": i["w_out_a"], "w_out_b": i["w_out_b"],
        "w_out_c": i["w_out_c"], "w_o": i["w_o"], "rope": rope_rows(), "slot_ids": slots, "ffn_w1": i["ffn_w1"],
        "ffn_w3": i["ffn_w3"], "ffn_w2": i["ffn_w2"], "router_w": i["router_w"], "moe_w1": i["moe_w1"],
        "moe_w3": i["moe_w3"], "moe_w2": i["moe_w2"],
    }
    arrays = {name: np.ascontiguousarray(a) for name, a in arrays.items()}
    nc = bacc.Bacc("TRN2", target_bir_lowering=False, num_devices=1)
    args = {name: nc.dram_tensor(name, a.shape, F32, kind="ExternalInput").ap() for name, a in arrays.items()}
    out = nc.dram_tensor("out", (1, SEQ, D), F32, kind="ExternalOutput").ap()
    table_store = nc.dram_tensor("table_store", (SCHUNKS, P, 2 * SEQ), F32, kind="Internal").ap()
    trunk(nc, **args, table_store=table_store, out=out)
    result = run_bass_kernel_spmd(nc, [arrays], core_ids=[0])
    return result.results[0]["out"]
```

```python
from contextlib import ExitStack

import numpy as np
import concourse.bass as bass
from concourse import mybir

ALU = mybir.AluOpType
ACT = mybir.ActivationFunctionType
F32 = mybir.dt.float32
F32R = mybir.dt.float32r
I32 = mybir.dt.int32
AX_X = mybir.AxisListType.X

P = 128
D = 1024
SEQ = 256
BLOCKS = SEQ // P
DEPTH = 2
KD = D // P
CONV = 512
SSM = 512
CT = CONV // P
GROUP = 16
STATE = 64
SCHUNKS = (SSM // GROUP) * STATE // P
HEADS = 8
HD = 64
IDX_HEADS = 4
TOPK = min(256, SEQ // 4)
FF_DENSE = 2816
EXPERTS = 8
FF_EXPERT = 3584
EPS = 1e-6
SLOTS = P
NEG = -1e30
DEAD = -3e38
HALF = 512

CHUNK = 2048
RAW = 6
SPLIT = 3
DENSE_W = 256
DENSE_STRIPES = FF_DENSE // DENSE_W
MOE_STRIPES = FF_EXPERT // HALF
MIX_CHUNKS = 35
DENSE_CHUNKS = 3 * DENSE_STRIPES
MOE_CHUNKS = 6 * MOE_STRIPES
MIX0 = [0, MIX_CHUNKS + DENSE_CHUNKS]
DENSE0 = MIX_CHUNKS
MOE0 = 2 * MIX_CHUNKS + DENSE_CHUNKS
C_KV, C_Q, C_SU, C_AU, C_AC, C_AB, C_GA, C_OA, C_GC, C_OC, C_GB, C_GLU, C_GB2, C_OB, C_WO = (
    0, 2, 4, 6, 8, 10, 12, 16, 18, 22, 24, 26, 27, 29, 31)
COL_AU, COL_AB, COL_AC, COL_SU, COL_Q, COL_KV = 0, 512, 1024, 1536, 2048, 2560
KV_W = 2 * HD + IDX_HEADS * HD + HD + IDX_HEADS
COL_G = COL_KV + KV_W
BU_FROM = C_AU

PAR_LRE, PAR_LIM, PAR_LDT = 0, SCHUNKS, 2 * SCHUNKS
PAR_CW = 3 * SCHUNKS
PAR_D = PAR_CW + 3 * CT
PAR_GAIN = PAR_D + CT
PAR_CRE = PAR_GAIN + 10 * HD
PAR_CIM = PAR_CRE + SCHUNKS * 32
PAR_B = PAR_CIM + SCHUNKS * 32
PAR_W = PAR_B + CT * 2 * P

MAGIC = 12582912.0
PIO2 = (1.5703125, 4.837512969970703e-4, 7.54978995489188216e-8)


def mixer_stream(w_in, w_out_a, w_out_b, w_out_c, w_glu, w_o, layer):
    wi = w_in[layer].rearrange("(k p) n -> p k n", p=P)
    stripe = lambda col, width: [(wi[:, 4 * h:4 * h + 4, col:col + width], (4, width)) for h in range(2)]
    rows = lambda w: [(w.rearrange("(k p) n -> p k n", p=P)[:, 2 * h:2 * h + 2, :], (2, D))
                      for h in range(w.shape[0] // (2 * P))]
    gates = lambda branch: stripe(COL_G + branch * D, HALF) + stripe(COL_G + branch * D + HALF, HALF)
    chunks = stripe(COL_KV, KV_W) + stripe(COL_Q, HALF) + stripe(COL_SU, SSM)
    chunks += stripe(COL_AU, CONV) + stripe(COL_AC, CONV) + stripe(COL_AB, CONV)
    chunks += gates(0) + rows(w_out_a[layer]) + gates(2) + rows(w_out_c[layer]) + gates(1)
    chunks.insert(C_GLU, (w_glu[layer].rearrange("(k p) n -> p k n", p=P), (4, SSM)))
    chunks += rows(w_out_b[layer]) + rows(w_o[layer])
    assert len(chunks) == MIX_CHUNKS
    return chunks


class Chain:

    def __init__(self, eng, sem):
        self.eng, self.sem, self.n = eng, sem, 0

    def step(self, ins):
        ins.then_inc(self.sem, 1)
        self.n += 1

    def join(self):
        self.eng.wait_ge(self.sem, self.n)

    def then(self, ins):
        self.step(ins)
        self.join()


def trunk(nc, x, gains, w_in, par, w_glu, w_out_a, w_out_b, w_out_c, w_o, rope, slot_ids, ffn_w1, ffn_w3, ffn_w2,
          router_w, moe_w1, moe_w3, moe_w2, table_store, out):
    with ExitStack() as ctx:
        def sb(name, shape, dt=F32, scope=ctx):
            return scope.enter_context(nc.sbuf_tensor(name, shape, dt))

        def sem(name):
            return ctx.enter_context(nc.semaphore(name))

        ps = ctx.enter_context(nc.psum_tensor("ps", [P, 8, HALF], F32))

        raw = sb("raw", [P, RAW, CHUNK])
        w_hi = sb("w_hi", [P, SPLIT, CHUNK], F32R)
        w_lo = sb("w_lo", [P, SPLIT, CHUNK], F32R)
        x_tok = sb("x_tok", [P, BLOCKS, D])
        h_tok = sb("h_tok", [P, BLOCKS, D])
        hT_hi = sb("hT_hi", [P, KD, SEQ], F32R)
        hT_lo = sb("hT_lo", [P, KD, SEQ], F32R)
        ident = sb("ident", [P, P])
        ones = sb("ones", [P, P])
        causal = sb("causal", [P, P])
        rope_sb = sb("rope_sb", [P, BLOCKS, 3, 32])
        norm_ss = sb("norm_ss", [P, 4, BLOCKS])

        mix = ExitStack()
        gate = sb("gate", [P, BLOCKS, D], F32, mix)
        yac_hi = sb("yac_hi", [P, CT, SEQ], F32R, mix)
        yac_lo = sb("yac_lo", [P, CT, SEQ], F32R, mix)
        su = sb("su", [P, CT, SEQ], F32, mix)
        u_t = sb("u_t", [P, CT, SEQ], F32, mix)
        v_t = sb("v_t", [P, CT, SEQ + 2], F32, mix)
        par_sb = sb("par_sb", [P, PAR_W], F32, mix)
        qkT = sb("qkT", [P, 8, SEQ], F32, mix)
        v_sb = sb("v_sb", [P, BLOCKS, HD], F32, mix)
        wi_sb = sb("wi_sb", [P, BLOCKS, IDX_HEADS], F32, mix)
        probs = sb("probs", [P, 4, SEQ], F32, mix)
        keybias = sb("keybias", [P, BLOCKS, SEQ], F32, mix)
        top8 = sb("top8", [P, 8], F32, mix)
        row_sb = sb("row_sb", [P, 4, 4], F32, mix)
        qk_ss = sb("qk_ss", [P, 3, BLOCKS, 10], F32, mix)
        trig = sb("trig", [P, 30, SCHUNKS], F32, mix)
        pow_b = sb("pow_b", [P, 2, 16, SCHUNKS], F32, mix)
        pow_a = sb("pow_a", [P, 2, 16, SCHUNKS], F32, mix)
        table = sb("table", [P, 3, 2, SEQ], F32, mix)
        pool_t = sb("pool_t", [P, 2, SEQ], F32, mix)
        state = sb("state", [P, 2, SEQ], F32, mix)
        with ExitStack() as overlay:
            turn = sb("turn", [P, 2, 4, SEQ], F32, overlay)
        yb_hi = sb("yb_hi", [P, CT, SEQ], F32R, mix)
        yb_lo = sb("yb_lo", [P, CT, SEQ], F32R, mix)
        mix.close()
        gain_row = gate[:, 0, :]
        qk = h_tok[:, :, :].rearrange("p b (h d) -> p b h d", d=HD)
        mixed = h_tok
        scratch = probs

        ffn = ExitStack()
        sil = sb("sil", [P, HALF], F32, ffn)
        gain_ff = sb("gain_ff", [P, D], F32, ffn)
        zero_r = sb("zero_r", [P, P], F32R, ffn)
        upper = sb("upper", [P, P], F32, ffn)
        hid = sb("hid", [P, HALF], F32, ffn)
        hidT_hi = sb("hidT_hi", [P, HALF], F32R, ffn)
        hidT_lo = sb("hidT_lo", [P, HALF], F32R, ffn)
        h_hi = sb("h_hi", [P, BLOCKS, D], F32R, ffn)
        h_lo = sb("h_lo", [P, BLOCKS, D], F32R, ffn)
        xg_hi = sb("xg_hi", [P, KD, P], F32R, ffn)
        xg_lo = sb("xg_lo", [P, KD, P], F32R, ffn)
        y_hi = sb("y_hi", [P, D], F32R, ffn)
        y_lo = sb("y_lo", [P, D], F32R, ffn)
        router_sb = sb("router_sb", [P, KD, EXPERTS], F32, ffn)
        router_hi = sb("router_hi", [P, KD, EXPERTS], F32R, ffn)
        router_lo = sb("router_lo", [P, KD, EXPERTS], F32R, ffn)
        logits_T = sb("logits_T", [EXPERTS, SEQ], F32, ffn)
        slot_id = sb("slot_id", [P, 2, P], F32, ffn)
        pick = sb("pick", [P, BLOCKS, P], F32R, ffn)
        pickT = sb("pickT", [P, BLOCKS, P], F32R, ffn)
        rt = sb("rt", [P, 10, BLOCKS, EXPERTS], F32, ffn)
        rt8 = sb("rt8", [P, BLOCKS, 8], F32, ffn)
        rts = sb("rts", [P, 6, BLOCKS], F32, ffn)
        gate_of = sb("gate_of", [P, BLOCKS, EXPERTS], F32, ffn)
        slot_of = sb("slot_of", [P, BLOCKS, EXPERTS + 1], F32, ffn)
        most = sb("most", [P, 1], F32, ffn)
        most_i = sb("most_i", [1, 1], I32, ffn)
        ffn.close()

        raw_full = [sem(f"raw_full{i}") for i in range(RAW)]
        hi_done, lo_done, used = sem("hi_done"), sem("lo_done"), sem("used")
        dve_step, pool_step = sem("dve_step"), sem("pool_step")
        names = """x_loaded consts zero_made upper_made rope_loaded gain_loaded par_loaded0 par_loaded1
            ss_done var_done std_done h_done hT_ps
            hT_hi_done hT_lo_done x_added out_stored branch_block0 ob_quarters x_block0
            su_copied q_copied kv_copied u_copied v_made conv_done ya_hi_done ya_lo_done
            gate_done gated mixed_done mixT_ps mixT_hi_done mixT_lo_done
            sq_done qk_ss_done qk_std_done qk_inv_done idx_rope_done idxT_ps idxT_copied rope_done qkT_ps qkT_copied
            idx_ps scored logit_ps shifted exp_done row_inv_done prob_done pT_ps pT_copied
            o_ps o_copied yc_hi_done yc_lo_done
            dt_exp lrdt_done mag_exp den_done den_inv powers_done table_done table_stored0 table_stored1
            table_loaded0 table_loaded1 table_loaded2 table_loaded3 bu_ps turned
            scanned rotated y_ps skip_done gelu_done yg_hi_done yg_lo_done glu_sig yb_made yb_hi_done yb_lo_done
            sil_done hid_done hidT_ps hidT_hi_done hidT_lo_done
            router_loaded router_hi_done router_lo_done logitsT_ps logitsT_copied slots_loaded
            h_hi_done h_lo_done logits_ps exp_r picked rank_ps slots_done most_done top_r
            pick_done gather_ps xg_hi_done xg_lo_done pickT_ps pickT_done y_hi_done y_lo_done scatter_ps acc_done
            final_done""".split()

        S = {n: sem(n) for n in names}
        block = ctx.enter_context(nc.Block())

        streams = [mixer_stream(w_in, w_out_a, w_out_b, w_out_c, w_glu, w_o, layer) for layer in range(DEPTH)]

        def slot_view(buf, n, shape):
            k, w = shape
            return buf[:, n % (RAW if buf is raw else SPLIT), 0:k * w].rearrange("p (k n) -> p k n", k=k)

        def split_hi(act, n, turns=0, width=CHUNK):
            act.wait_ge(raw_full[n % RAW], 16 * (n // RAW + 1) + 16 * turns)
            if n >= SPLIT:
                act.wait_ge(used, n - SPLIT + 1 + 6 * turns)
            act.activation(w_hi[:, n % SPLIT, 0:width], raw[:, n % RAW, 0:width], ACT.Copy).then_inc(hi_done, 1)

        def split_lo(dve, n, seen=None, width=CHUNK):
            dve.wait_ge(hi_done, n + 1 if seen is None else seen)
            dve.tensor_tensor(w_lo[:, n % SPLIT, 0:width], raw[:, n % RAW, 0:width],
                              w_hi[:, n % SPLIT, 0:width].bitcast(F32), ALU.subtract).then_inc(lo_done, 1)

        def value(eng, v):
            return v if isinstance(v, int) else eng.snap(v)

        def table_factors(j):
            a = [pow_a[:, i, :, j:j + 1].broadcast_to([P, 16, 16]) for i in range(2)]
            b = [pow_b[:, i, :, j].unsqueeze(1).broadcast_to([P, 16, 16]) for i in range(2)]
            return a + b

        def trig_row(i, count=1):
            return trig[:, i, :] if count == 1 else trig[:, i:i + count, :]

        (LR, DT, LRDT, MAG, K, R, R2, SN, CS, M, M2, CQ, SQ, T1, T2, SIN, COS, NR, NI, DEN, INV, CRE, CIM,
         ANG) = range(24)
        W_ROWS, SQ_ROWS = (24, 26), 28

        def ops(eng, own):
            def tt(o, a, b, op):
                own.step(eng.tensor_tensor(o, a, b, op))

            def ts(o, a, c1, op1, c2=None, op2=None):
                own.step(eng.tensor_scalar(o, a, c1, c2, op1, op2) if op2 is not None else
                         eng.tensor_scalar(o, a, c1, None, op1))
            return tt, ts

        def s5_rates(eng, own, layer):
            tt, ts = ops(eng, own)
            li = par_sb[:, PAR_LIM:PAR_LIM + SCHUNKS]
            eng.wait_ge(S[f"par_loaded{layer}"], 16)
            ts(trig_row(LR), par_sb[:, PAR_LRE:PAR_LRE + SCHUNKS], -1e-4, ALU.min)
            tt(trig_row(T2), li, li, ALU.mult)
            own.join()
            tt(trig_row(T1), trig_row(LR), trig_row(LR), ALU.mult)
            own.join()
            eng.tensor_tensor(trig_row(DEN), trig_row(T1), trig_row(T2), ALU.add).then_inc(S["den_done"], 1)
            eng.wait_ge(S["dt_exp"], layer + 1)
            eng.tensor_tensor(trig_row(LRDT), trig_row(LR), trig_row(DT), ALU.mult).then_inc(S["lrdt_done"], 1)

        def s5_angles(eng, own, layer):
            tt, ts = ops(eng, own)
            k, r, r2, sn, cs, m, m2, cq, sq, t1, t2, sin, cos, ang = (
                trig_row(i) for i in (K, R, R2, SN, CS, M, M2, CQ, SQ, T1, T2, SIN, COS, ANG))
            li = par_sb[:, PAR_LIM:PAR_LIM + SCHUNKS]
            tt(ang, li, trig_row(DT), ALU.mult)
            own.join()
            ts(k, ang, 2.0 / float(np.pi), ALU.mult)
            own.join()
            ts(k, k, MAGIC, ALU.add)
            own.join()
            ts(k, k, -MAGIC, ALU.add)
            own.join()
            ts(t1, k, -PIO2[0], ALU.mult)
            ts(t2, k, -PIO2[1], ALU.mult)
            ts(sq, k, -PIO2[2], ALU.mult)
            ts(m, k, 0.25, ALU.mult)
            own.join()
            tt(r, ang, t1, ALU.add)
            ts(m, m, MAGIC, ALU.add)
            own.join()
            tt(r, r, t2, ALU.add)
            ts(m, m, -MAGIC, ALU.add, -4.0, ALU.mult)
            own.join()
            tt(r, r, sq, ALU.add)
            tt(m, m, k, ALU.add)
            own.join()
            tt(r2, r, r, ALU.mult)
            tt(m2, m, m, ALU.mult)
            own.join()
            ts(sn, r2, 1.0 / 362880, ALU.mult, -1.0 / 5040, ALU.add)
            ts(cs, r2, -1.0 / 3628800, ALU.mult, 1.0 / 40320, ALU.add)
            ts(cq, m2, 0.0, ALU.is_equal)
            ts(t1, m2, 4.0, ALU.is_equal)
            ts(sq, m2, 1.0, ALU.is_equal)
            own.join()
            tt(cq, cq, t1, ALU.subtract)
            tt(sq, sq, m, ALU.mult)
            for c_sin, c_cos in ((1.0 / 120, -1.0 / 720), (-1.0 / 6, 1.0 / 24), (1.0, -0.5)):
                tt(sn, sn, r2, ALU.mult)
                tt(cs, cs, r2, ALU.mult)
                own.join()
                ts(sn, sn, c_sin, ALU.add)
                ts(cs, cs, c_cos, ALU.add)
                own.join()
            tt(sn, sn, r, ALU.mult)
            tt(cs, cs, r2, ALU.mult)
            own.join()
            ts(cs, cs, 1.0, ALU.add)
            own.join()
            tt(t1, cs, cq, ALU.mult)
            tt(t2, sn, sq, ALU.mult)
            tt(m, sn, cq, ALU.mult)
            tt(m2, cs, sq, ALU.mult)
            own.join()
            tt(cos, t1, t2, ALU.subtract)
            tt(sin, m, m2, ALU.add)
            own.join()

        def s5_powers(eng, own, first=0, last=8):
            tt, ts = ops(eng, own)
            if first == 0:
                for dst in (pow_b, pow_a):
                    own.step(eng.memset(dst[:, 0, 0, :], 1.0))
                    own.step(eng.memset(dst[:, 1, 0, :], 0.0))
                own.join()
            for level in range(first, last):
                w_re, w_im = (trig_row(COS), trig_row(SIN)) if level == 0 else (
                    trig_row(W_ROWS[(level - 1) % 2]), trig_row(W_ROWS[(level - 1) % 2] + 1))
                dst, n = (pow_b, pow_a)[level // 4], 1 << (level % 4)
                a = dst[:, :, 0:n, :]
                by_re, by_im = (turn[:, i, :, :].rearrange("p a t -> p (a t)")[:, 0:2 * n * SCHUNKS]
                                .rearrange("p (c n j) -> p c n j", c=2, n=n) for i in range(2))
                wide = lambda w: w.unsqueeze(1).unsqueeze(1).broadcast_to([P, 2, n, SCHUNKS])
                sq_re, sq_im = trig_row(SQ_ROWS), trig_row(SQ_ROWS + 1)
                to = W_ROWS[level % 2]
                tt(by_re, a, wide(w_re), ALU.mult)
                tt(by_im, a, wide(w_im), ALU.mult)
                tt(sq_re, w_re, w_re, ALU.mult)
                tt(sq_im, w_im, w_im, ALU.mult)
                tt(trig_row(to + 1), w_re, w_im, ALU.mult)
                own.join()
                tt(dst[:, 0, n:2 * n, :], by_re[:, 0], by_im[:, 1], ALU.subtract)
                tt(trig_row(to), sq_re, sq_im, ALU.subtract)
                ts(trig_row(to + 1), trig_row(to + 1), 2.0, ALU.mult)
                last = eng.tensor_tensor(dst[:, 1, n:2 * n, :], by_re[:, 1], by_im[:, 0], ALU.add)
                if level < 7:
                    own.step(last)
                else:
                    last.then_inc(S["powers_done"], 1)
                own.join()

        def s5_fold(eng, own, layer):
            tt, ts = ops(eng, own)
            lr, mag, nr, ni, t1, t2, m, m2, cre, cim, inv = (
                trig_row(i) for i in (LR, MAG, NR, NI, T1, T2, M, M2, CRE, CIM, INV))
            li = par_sb[:, PAR_LIM:PAR_LIM + SCHUNKS]
            eng.wait_ge(S["mag_exp"], layer + 1)
            tt(nr, mag, trig_row(COS), ALU.mult)
            tt(ni, mag, trig_row(SIN), ALU.mult)
            own.join()
            ts(nr, nr, -1.0, ALU.add)
            own.join()
            tt(t1, nr, lr, ALU.mult)
            tt(t2, ni, li, ALU.mult)
            tt(m, ni, lr, ALU.mult)
            tt(m2, nr, li, ALU.mult)
            own.join()
            tt(cre, t1, t2, ALU.add)
            tt(cim, m, m2, ALU.subtract)
            own.join()
            eng.wait_ge(S["den_inv"], layer + 1)
            tt(cre, cre, inv, ALU.mult)
            tt(cim, cim, inv, ALU.mult)
            own.join()
            c_re, c_im = (par_sb[:, o:o + SCHUNKS * 32].rearrange("p (j c) -> p j c", c=32)
                          for o in (PAR_CRE, PAR_CIM))
            ta, tb, tc, td = (turn[:, i // 2, 2 * (i % 2):2 * (i % 2) + 2, :].rearrange("p a (j c) -> p (a j) c", c=32)
                              for i in range(4))
            kr, ki = (v.unsqueeze(2).broadcast_to([P, SCHUNKS, 32]) for v in (cre, cim))
            tt(ta, c_re, kr, ALU.mult)
            tt(tb, c_im, ki, ALU.mult)
            tt(tc, c_re, ki, ALU.mult)
            tt(td, c_im, kr, ALU.mult)
            own.join()
            tt(c_re, ta, tb, ALU.subtract)
            tt(c_im, td, tc, ALU.add)
            own.join()
            ts(c_im, c_im, -1.0, ALU.mult)
            own.join()

        squares = gate
        rowmax, rowsum, rowinv, smalls = (row_sb[:, i, :] for i in range(4))

        def banks(lo, count):
            return ps[:, lo:lo + count, :].rearrange("p a n -> p (a n)")

        def flat(t):
            return t.rearrange("p a b -> p (a b)")

        def probs_T(kt, q):
            return flat(probs[:, :, :])[:, (4 * kt + q) * P:(4 * kt + q + 1) * P]

        def table_at(layer, j):
            if layer == 0:
                return table[:, j % 3, :, :]
            if j % 4 < 2:
                return table[:, j % 4, :, :]
            return (pow_b if j % 4 == 2 else pow_a)[:, :, :, :].rearrange("p c k j -> p c (k j)")

        def mix_width(layer, c):
            k, w = streams[layer][c][1]
            return k * w

        @block.sync
        def _(sp):
            sp.dma_start(x_tok[:, :, :], x[0].rearrange("(b p) d -> p b d", p=P)).then_inc(S["x_loaded"], 16)

            def load(n, src, dst):
                if n >= RAW:
                    sp.wait_ge(lo_done, n - RAW + 1)
                sp.dma_start(dst, src).then_inc(raw_full[n % RAW], 16)

            def mixer(layer):
                for c, (src, shape) in enumerate(streams[layer]):
                    if layer == 0 and c == 2:
                        sp.dma_start(par_sb[:, :], par[0]).then_inc(S["par_loaded0"], 16)
                    load(MIX0[layer] + c, src, slot_view(raw, MIX0[layer] + c, shape))

            w1d = ffn_w1[0].rearrange("(k p) n -> p k n", p=P)
            w3d = ffn_w3[0].rearrange("(k p) n -> p k n", p=P)
            w2d = ffn_w2[0].rearrange("(k p) n -> p k n", p=P)

            def load_at(n, turns, src):
                free = value(sp, n - RAW + 1 + 6 * turns)
                sp.wait_ge(lo_done, free)
                shape = tuple(src.shape[1:])
                sp.dma_start(slot_view(raw, n, shape), src).then_inc(raw_full[n % RAW], 16)

            def dense():
                n = DENSE0
                load(n, w1d[:, :, 0:DENSE_W], slot_view(raw, n, (KD, DENSE_W)))
                load(n + 1, w3d[:, :, 0:DENSE_W], slot_view(raw, n + 1, (KD, DENSE_W)))
                with sp.Fori(0, (DENSE_STRIPES - 1) // 2) as t:
                    for h in range(2):
                        m = n + 2 + 3 * h
                        col = sp.snap((2 * t + 1 + h) * DENSE_W)
                        row = sp.snap((2 * t + h) * 2)
                        load_at(m, t, w1d[:, :, bass.ds(col, DENSE_W)])
                        load_at(m + 1, t, w3d[:, :, bass.ds(col, DENSE_W)])
                        load_at(m + 2, t, w2d[:, bass.ds(row, 2), :])
                last = n + DENSE_CHUNKS - 1
                load(last, w2d[:, 2 * (DENSE_STRIPES - 1):2 * DENSE_STRIPES, :], slot_view(raw, last, (2, D)))

            w1e = moe_w1[0].rearrange("e (k p) n -> p (e k) n", p=P)
            w3e = moe_w3[0].rearrange("e (k p) n -> p (e k) n", p=P)
            w2e = moe_w2[0].rearrange("e (k p) n -> p (e k) n", p=P)
            K2 = FF_EXPERT // P

            def experts(rnd):
                n = MOE0 + rnd * EXPERTS * MOE_CHUNKS

                def up(m, turns, w, e, t):
                    col = value(sp, t * HALF)
                    for half in range(2):
                        row = value(sp, KD * e + 4 * half)
                        load_at(m + half, turns, w[:, bass.ds(row, 4), bass.ds(col, HALF)])

                def down(m, turns, e, t):
                    for half in range(2):
                        row = value(sp, K2 * e + 4 * t + 2 * half)
                        load_at(m + half, turns, w2e[:, bass.ds(row, 2), :])

                def expert(e, last):
                    with sp.Fori(1, MOE_STRIPES) as t:
                        turns = MOE_STRIPES * e + t - 1
                        up(n + 4, turns, w1e, e, t)
                        up(n + 6, turns, w3e, e, t)
                        down(n + 8, turns, e, t - 1)
                    turns = MOE_STRIPES * e + MOE_STRIPES - 1
                    if last:
                        down(n + 4, turns, e, MOE_STRIPES - 1)
                        return
                    up(n + 4, turns, w1e, e + 1, 0)
                    down(n + 6, turns, e, MOE_STRIPES - 1)
                    up(n + 8, turns, w3e, e + 1, 0)

                up(n, 0, w1e, 0, 0)
                up(n + 2, 0, w3e, 0, 0)
                with sp.Fori(0, EXPERTS - 1) as e:
                    expert(e, False)
                expert(EXPERTS - 1, True)

            mixer(0)
            dense()
            mixer(1)
            experts(0)
            sp.wait_ge(S["most_done"], 1)
            most_tokens = sp.value_load(most_i[0:1, 0:1])
            with sp.If(most_tokens > SLOTS):
                experts(1)
            sp.wait_ge(S["final_done"], 1)
            sp.dma_start(out[0].rearrange("(b p) d -> p b d", p=P), x_tok[:, :, :]).then_inc(S["out_stored"], 16)
            sp.wait_ge(S["out_stored"], 16)

        @block.tensor
        def _(pe):
            def three(dst, x_hi, x_lo, n, tile, first, last):
                hi, lo = tile(w_hi), tile(w_lo)
                pe.matmul(dst, x_hi, hi, start=first, stop=False, skip_group_check=True)
                pe.matmul(dst, x_hi, lo, start=False, stop=False, skip_group_check=True)
                return pe.matmul(dst, x_lo, hi, start=False, stop=last, skip_group_check=True)

            def columns(n, bank, k0, nk, width, first, last, seen=None):
                pe.wait_ge(lo_done, n + 1 if seen is None else seen)
                for k in range(nk):
                    for b in range(BLOCKS):
                        tok = slice(b * P, b * P + P)
                        mm = three(ps[:, bank + b, 0:width], hT_hi[:, k0 + k, tok], hT_lo[:, k0 + k, tok], n,
                                   lambda w: slot_view(w, n, (nk, width))[:, k, :], first and k == 0,
                                   last and k == nk - 1)
                mm.then_inc(used, 1)

            def channels(n, bank, k0, x_hi, x_lo, first, last):
                pe.wait_ge(lo_done, n + 1)
                for k in range(4):
                    for c in range(CT):
                        dst = ps[:, bank + c // 2, (c % 2) * SEQ:(c % 2 + 1) * SEQ]
                        wh = slot_view(w_hi, n, (4, HALF))[:, k, c * P:c * P + P]
                        wl = slot_view(w_lo, n, (4, HALF))[:, k, c * P:c * P + P]
                        start = first and k == 0 and c % 2 == 0
                        pe.matmul(dst, wh, x_hi[:, k0 + k, :], start=start, stop=False, skip_group_check=True)
                        pe.matmul(dst, wl, x_hi[:, k0 + k, :], start=False, stop=False, skip_group_check=True)
                        mm = pe.matmul(dst, wh, x_lo[:, k0 + k, :], start=False, stop=last and k == 3,
                                       skip_group_check=True)
                mm.then_inc(used, 1)

            def rows(n, k0, x_hi, x_lo, first, last, bank=0, blocks=BLOCKS, seen=None, block0=None,
                     quarters=None, gates_read=None):
                pe.wait_ge(lo_done, n + 1 if seen is None else seen)
                order = [(k, b, h) for k in range(2) for b in range(blocks) for h in range(2)]
                if block0 is not None or quarters is not None or gates_read is not None:
                    order.sort(key=lambda kbh: kbh[1:])
                for k, b, h in order:
                    tok = slice(b * P, b * P + P)
                    if gates_read is not None and (k, b, h) == (0, 1, 0):
                        pe.wait_ge(S["gate_done"], gates_read)
                    mm = three(ps[:, bank + 2 * b + h, :], x_hi[:, k0 + k, tok], x_lo[:, k0 + k, tok], n,
                               lambda w: slot_view(w, n, (2, D))[:, k, h * HALF:(h + 1) * HALF],
                               first and k == 0, last and k == 1)
                    if block0 is not None and (k, b, h) == (1, 0, 1):
                        mm.then_inc(block0, 1)
                    if quarters is not None and k == 1 and (b, h) != (1, 1):
                        mm.then_inc(quarters, 1)
                mm.then_inc(used, 1)

            def turn_rows(src, bank, ready, seen, done, parts=1):
                for b in range(BLOCKS):
                    for k in range(KD):
                        if k % (KD // parts) == 0:
                            pe.wait_ge(ready, seen + parts * b + k // (KD // parts) + 1)
                        at = (k % 2) * SEQ + b * P
                        tr = pe.transpose(ps[:, bank + k // 2, at:at + P], src[:, b, k * P:k * P + P], ident[:, :])
                        if b == BLOCKS - 1 and k % 2:
                            tr.then_inc(done, 1)

            def norm_turn(i):
                turn_rows(h_tok, 0, S["h_done"], BLOCKS * i, S["hT_ps"])

            def bu(layer, j):
                if j == 0:
                    pe.wait_ge(S["su_copied"], layer + 1)
                    pe.wait_ge(S[f"par_loaded{layer}"], 16)
                else:
                    pe.wait_ge(S["turned"], 16 * layer + j)
                r = 32 * (j % 4)
                for part in range(2):
                    bt = par_sb[r:r + 32, PAR_B:PAR_B + CT * 2 * P].rearrange("p (c i n) -> p c i n", c=CT, i=2)
                    mm = pe.matmul(ps[:, 4, part * SEQ:(part + 1) * SEQ], bt[:, j // 4, part, :],
                                   su[r:r + 32, j // 4, :], start=part == 0, stop=part == 1, skip_group_check=True,
                                   tile_position=(r, 0))
                mm.then_inc(S["bu_ps"], 1)

            def y_of(layer, j):
                pe.wait_ge(S["rotated"], SCHUNKS * layer + j + 1)
                if j >= 4 and j % 4 == 0:
                    pe.wait_ge(S["skip_done"], CT * layer + j // 4)
                r, at = 32 * (j % 4), ((j // 4) % 2) * SEQ
                for part, col in ((0, PAR_CRE), (1, PAR_CIM)):
                    mm = pe.matmul(ps[r:r + 32, 5, at:at + SEQ], par_sb[:, col + 32 * j:col + 32 * j + 32],
                                   state[:, part, :], start=part == 0, stop=part == 1, skip_group_check=True,
                                   tile_position=(0, r))
                mm.then_inc(S["y_ps"], 1)

            def turn_heads(layer, pairs, done):
                for i, pair in enumerate(pairs):
                    for b in range(BLOCKS):
                        at = (i % 2) * SEQ + b * P
                        tr = pe.transpose(ps[:, 6 + i // 2, at:at + P], h_tok[:, b, pair * P:pair * P + P],
                                          ident[:, :])
                tr.then_inc(S[done], 1)

            def index_scores(layer, b):
                if b == 0:
                    pe.wait_ge(S["idxT_copied"], layer + 1)
                else:
                    pe.wait_ge(S["scored"], 2 * layer + 1)
                keys = (b + 1) * P
                for h in range(IDX_HEADS):
                    r = HD * (h % 2)
                    at = (h // 2) * keys
                    mm = pe.matmul(ps[:, 6 + h % 2, at:at + keys],
                                   qkT[r:r + HD, 5 + h // 2, b * P:b * P + P], qkT[r:r + HD, 7, 0:keys],
                                   start=at == 0, stop=True, skip_group_check=True, tile_position=(r, 0))
                mm.then_inc(S["idx_ps"], 1)

            def logits(layer, i):
                n = 4 * layer + i
                b, g = i // 2, i % 2
                if i == 0:
                    pe.wait_ge(S["qkT_copied"], 2 * layer + 2)
                else:
                    pe.wait_ge(S["o_copied"], n)
                keys = (b + 1) * P
                for h in range(4):
                    r = HD * (h % 2)
                    at = (h // 2) * keys
                    mm = pe.matmul(ps[:, 6 + h % 2, at:at + keys],
                                   qkT[r:r + HD, 2 * g + h // 2, b * P:b * P + P], qkT[r:r + HD, 4, 0:keys],
                                   start=at == 0, stop=True, skip_group_check=True, tile_position=(r, 0))
                mm.then_inc(S["logit_ps"], 1)

            def turn_probs(layer, i):
                n = 4 * layer + i
                pe.wait_ge(S["prob_done"], 4 * (n + 1))
                b = i // 2
                for kt in range(b + 1):
                    for h in range(4):
                        tr = pe.transpose(ps[:, 6 + kt, h * P:h * P + P], probs[:, h, kt * P:kt * P + P], ident[:, :])
                tr.then_inc(S["pT_ps"], 1)

            def values(layer, i):
                n = 4 * layer + i
                pe.wait_ge(S["pT_copied"], n + 1)
                b = i // 2
                for q in range(4):
                    r, pair = HD * (q // 2), q % 2
                    for kt in range(b + 1):
                        mm = pe.matmul(ps[r:r + HD, 6, pair * P:pair * P + P], v_sb[:, kt, :],
                                       probs_T(kt, q),
                                       start=kt == 0, stop=kt == b, skip_group_check=True, tile_position=(0, r))
                mm.then_inc(S["o_ps"], 1)

            def mixer(layer):
                c0 = MIX0[layer]
                norm_turn(2 * layer)

                def s5(c):
                    j = c - BU_FROM
                    if 0 <= j - 3 < SCHUNKS:
                        y_of(layer, j - 3)
                    if 0 <= j < SCHUNKS:
                        bu(layer, j)

                def stripe(c, bank, half, width=HALF):
                    columns(c0 + c + half, bank, 4 * half, 4, width, half == 0, half == 1)

                def held(c, bank, half):
                    channels(c0 + c + half, bank, 4 * half, hT_hi, hT_lo, half == 0, half == 1)

                pe.wait_ge(S["hT_lo_done"], 8 * layer + 2)
                stripe(C_KV, 0, 0, KV_W)
                pe.wait_ge(S["hT_lo_done"], 8 * layer + 4)
                stripe(C_KV, 0, 1, KV_W)
                stripe(C_Q, 2, 0)
                stripe(C_Q, 2, 1)
                pe.wait_ge(S["idx_rope_done"], BLOCKS * (layer + 1))
                turn_heads(layer, (5, 6, 7), "idxT_ps")
                index_scores(layer, 0)
                pe.wait_ge(S["kv_copied"], 7 * (layer + 1))
                pe.wait_ge(S["sq_done"], 3 * layer + 2)
                held(C_SU, 0, 0)
                index_scores(layer, 1)
                held(C_SU, 0, 1)
                pe.wait_ge(S["q_copied"], layer + 1)
                pe.wait_ge(S["sq_done"], 3 * layer + 3)
                held(C_AU, 2, 0)
                s5(C_AU)
                held(C_AU, 2, 1)
                pe.wait_ge(S["scored"], 2 * layer + 2)
                pe.wait_ge(S["rope_done"], BLOCKS * (layer + 1))
                turn_heads(layer, (0, 1, 2, 3), "qkT_ps")
                s5(C_AU + 1)
                pe.wait_ge(S["su_copied"], layer + 1)
                held(C_AC, 0, 0)
                pe.wait_ge(S["qkT_copied"], 2 * layer + 1)
                turn_heads(layer, (4,), "qkT_ps")
                s5(C_AC)
                held(C_AC, 0, 1)
                logits(layer, 0)
                s5(C_AC + 1)
                pe.wait_ge(S["u_copied"], layer + 1)
                held(C_AB, 2, 0)
                turn_probs(layer, 0)
                s5(C_AB)
                held(C_AB, 2, 1)
                values(layer, 0)
                logits(layer, 1)
                s5(C_AB + 1)
                pe.wait_ge(S["v_made"], layer + 1)
                stripe(C_GA, 0, 0)
                turn_probs(layer, 1)
                s5(C_GA)
                stripe(C_GA, 0, 1)
                values(layer, 1)
                logits(layer, 2)
                s5(C_GA + 1)
                pe.wait_ge(S["conv_done"], layer + 1)
                stripe(C_GA + 2, 2, 0)
                s5(C_GA + 2)
                stripe(C_GA + 2, 2, 1)
                turn_probs(layer, 2)
                s5(C_GA + 3)
                pe.wait_ge(S["gate_done"], 6 * layer + 1)
                pe.wait_ge(S["ya_lo_done"], layer + 1)
                rows(c0 + C_OA, 0, yac_hi, yac_lo, True, False, gates_read=6 * layer + 2)
                values(layer, 2)
                logits(layer, 3)
                s5(C_OA)
                rows(c0 + C_OA + 1, 2, yac_hi, yac_lo, False, True, block0=S["branch_block0"])
                s5(C_OA + 1)
                pe.wait_ge(S["gated"], 4 * layer + 1)
                stripe(C_GC, 0, 0)
                turn_probs(layer, 3)
                s5(C_GC)
                stripe(C_GC, 0, 1)
                values(layer, 3)
                s5(C_GC + 1)
                pe.wait_ge(S["gated"], 4 * layer + 2)
                stripe(C_GC + 2, 2, 0)
                s5(C_GC + 2)
                stripe(C_GC + 2, 2, 1)
                s5(C_GC + 3)
                pe.wait_ge(S["gate_done"], 6 * layer + 3)
                pe.wait_ge(S["yc_lo_done"], layer + 1)
                rows(c0 + C_OC, 0, yac_hi, yac_lo, True, False, gates_read=6 * layer + 4)
                s5(C_OC)
                rows(c0 + C_OC + 1, 2, yac_hi, yac_lo, False, True, block0=S["branch_block0"])
                s5(C_OC + 1)
                pe.wait_ge(S["gated"], 4 * layer + 3)
                stripe(C_GB, 0, 0)
                s5(C_GB)
                stripe(C_GB, 0, 1)
                pe.wait_ge(S["yg_lo_done"], layer + 1)
                channels(c0 + C_GLU, 4, 0, yb_hi, yb_lo, True, True)
                pe.wait_ge(S["gated"], 4 * (layer + 1))
                stripe(C_GB2, 2, 0)
                stripe(C_GB2, 2, 1)
                pe.wait_ge(S["gate_done"], 6 * layer + 5)
                pe.wait_ge(S["yb_lo_done"], layer + 1)
                rows(c0 + C_OB, 0, yb_hi, yb_lo, True, False, gates_read=6 * layer + 6)
                rows(c0 + C_OB + 1, 2, yb_hi, yb_lo, False, True, quarters=S["ob_quarters"])
                turn_rows(mixed, 4, S["mixed_done"], 5 * layer + 1, S["mixT_ps"], 2)
                for i in range(4):
                    pe.wait_ge(S["mixT_lo_done"], 4 * layer + i + 1)
                    rows(c0 + C_WO + i, 2 * i, hT_hi, hT_lo, i == 0, i == 3, block0=S["x_block0"] if i == 3 else None)

            def clear(bank, count):
                for b in range(bank, bank + count):
                    pe.matmul(ps[:, b, 0:P], zero_r[:, :], zero_r[:, :], start=True, stop=False,
                              skip_group_check=True)

            def dense():
                n0 = DENSE0

                def up(n, i, turns):
                    for which, bank, read in ((0, 0, S["sil_done"]), (1, 1, S["hid_done"])):
                        if i is not None:
                            pe.wait_ge(read, i)
                        pe.wait_ge(lo_done, n + which + 1 + 6 * turns)
                        for k in range(KD):
                            if i is None and which == 0 and k == KD // 2:
                                pe.wait_ge(S["hT_lo_done"], 8)
                            for b in range(BLOCKS):
                                tok = slice(b * P, b * P + P)
                                mm = three(ps[:, bank, b * DENSE_W:(b + 1) * DENSE_W], hT_hi[:, k, tok],
                                           hT_lo[:, k, tok], n,
                                           lambda w: slot_view(w, n + which, (KD, DENSE_W))[:, k, :],
                                           k == 0 and b == 0, k == KD - 1)
                        mm.then_inc(used, 1)

                def turn_hidden(i):
                    pe.wait_ge(S["hid_done"], i + 1)
                    for k in range(2):
                        for b in range(BLOCKS):
                            tr = pe.transpose(ps[:, 2, k * SEQ + b * P:k * SEQ + b * P + P],
                                              hid[:, b * DENSE_W + k * P:b * DENSE_W + k * P + P], ident[:, :])
                    tr.then_inc(S["hidT_ps"], 1)

                x_hi = hidT_hi[:, :].rearrange("p (k t) -> p k t", k=2)
                x_lo = hidT_lo[:, :].rearrange("p (k t) -> p k t", k=2)
                norm_turn(1)
                pe.wait_ge(S["zero_made"], 1)
                clear(4, 4)
                pe.wait_ge(S["hT_lo_done"], 6)
                up(n0, None, 0)
                turn_hidden(0)
                with pe.Fori(0, (DENSE_STRIPES - 1) // 2) as t:
                    for h in range(2):
                        m = n0 + 2 + 3 * h
                        i = 2 * t + 1 + h
                        up(m, i, t)
                        pe.wait_ge(S["hidT_lo_done"], i)
                        rows(m + 2, 0, x_hi, x_lo, False, False, bank=4, seen=m + 3 + 6 * t)
                        turn_hidden(i)
                pe.wait_ge(S["hidT_lo_done"], DENSE_STRIPES)
                rows(n0 + DENSE_CHUNKS - 1, 0, x_hi, x_lo, False, True, bank=4, block0=S["x_block0"])

            def route():
                norm_turn(3)
                pe.wait_ge(S["router_lo_done"], 1)
                for k in range(KD):
                    if k % 2 == 0:
                        pe.wait_ge(S["hT_lo_done"], 12 + k // 2 + 1)
                    dst = ps[0:EXPERTS, 4, 0:SEQ]
                    pe.matmul(dst, router_hi[:, k, :], hT_hi[:, k, :], start=k == 0, stop=False,
                              skip_group_check=True)
                    pe.matmul(dst, router_lo[:, k, :], hT_hi[:, k, :], start=False, stop=False,
                              skip_group_check=True)
                    mm = pe.matmul(dst, router_hi[:, k, :], hT_lo[:, k, :], start=False, stop=k == KD - 1,
                                   skip_group_check=True)
                mm.then_inc(S["logitsT_ps"], 1)
                pe.wait_ge(S["logitsT_copied"], 1)
                for b in range(BLOCKS):
                    tr = pe.transpose(ps[:, 6, b * EXPERTS:(b + 1) * EXPERTS], logits_T[:, b * P:(b + 1) * P],
                                      ident[0:EXPERTS, 0:EXPERTS])
                tr.then_inc(S["logits_ps"], 1)
                pe.wait_ge(S["picked"], 1)
                pe.wait_ge(S["upper_made"], 1)
                sel = rt[:, 7]
                pe.matmul(ps[:, 5, 0:8], upper[:, :], sel[:, 0, :], start=True, stop=True, skip_group_check=True)
                pe.matmul(ps[:, 5, 8:16], ones[:, :], sel[:, 0, :], start=False, stop=False, skip_group_check=True)
                pe.matmul(ps[:, 5, 8:16], upper[:, :], sel[:, 1, :], start=False, stop=True, skip_group_check=True)
                pe.matmul(ps[:, 5, 16:24], ones[:, :], sel[:, 0, :], start=False, stop=False, skip_group_check=True)
                pe.matmul(ps[:, 5, 16:24], ones[:, :], sel[:, 1, :], start=False, stop=True,
                          skip_group_check=True).then_inc(S["rank_ps"], 1)
                pe.wait_ge(S["slots_done"], 1)

            def experts(rnd):
                n0 = MOE0 + rnd * EXPERTS * MOE_CHUNKS
                e0 = rnd * EXPERTS
                i0 = DENSE_STRIPES + e0 * MOE_STRIPES
                xT_hi = hidT_hi[:, :].rearrange("p (k t) -> p k t", k=4)
                xT_lo = hidT_lo[:, :].rearrange("p (k t) -> p k t", k=4)

                def up(n, which, i, turns):
                    pe.wait_ge(S["hid_done"] if which else S["sil_done"], i)
                    for half in range(2):
                        m = n + half
                        pe.wait_ge(lo_done, m + 1 + 6 * turns)
                        for k in range(4):
                            kk = 4 * half + k
                            mm = three(ps[:, which, :], xg_hi[:, kk, :], xg_lo[:, kk, :], m,
                                       lambda w: slot_view(w, m, (4, HALF))[:, k, :], kk == 0, kk == KD - 1)
                        mm.then_inc(used, 1)

                def turn_hidden(i):
                    pe.wait_ge(S["hid_done"], i + 1)
                    for k in range(4):
                        tr = pe.transpose(ps[:, 4, k * P:k * P + P], hid[:, k * P:k * P + P], ident[:, :])
                    tr.then_inc(S["hidT_ps"], 1)

                def down(n, i, turns, first=False):
                    pe.wait_ge(S["hidT_lo_done"], i)
                    for half in range(2):
                        rows(n + half, 2 * half, xT_hi, xT_lo, first and half == 0, False, bank=2, blocks=1,
                             seen=n + half + 1 + 6 * turns)

                def gather(e):
                    pe.wait_ge(S["pick_done"], BLOCKS * (e0 + e + 1))
                    for src, bank in ((h_hi, 4), (h_lo, 6)):
                        for k in range(KD):
                            for b in range(BLOCKS):
                                mm = pe.matmul(ps[:, bank + k // 4, (k % 4) * P:(k % 4) * P + P],
                                               src[:, b, k * P:k * P + P], pick[:, b, :],
                                               start=k % 4 == 0 and b == 0, stop=b == 1, skip_group_check=True)
                        mm.then_inc(S["gather_ps"], 1)

                def turn_pick(e):
                    for b in range(BLOCKS):
                        tr = pe.transpose(ps[:, 5, b * P:b * P + P], pick[:, b, :].bitcast(F32), ident[:, :])
                    tr.then_inc(S["pickT_ps"], 1)

                def scatter(e):
                    pe.wait_ge(S["pickT_done"], e0 + e + 1)
                    for half in range(2):
                        pe.wait_ge(S["y_lo_done"], 2 * (e0 + e) + half + 1)
                        for b in range(BLOCKS):
                            dst = ps[:, 2 + half if b == 0 else 6 + half, :]
                            pe.matmul(dst, pickT[:, b, :], y_hi[:, half * HALF:(half + 1) * HALF], start=True,
                                      stop=False, skip_group_check=True)
                            mm = pe.matmul(dst, pickT[:, b, :], y_lo[:, half * HALF:(half + 1) * HALF], start=False,
                                           stop=True, skip_group_check=True)
                    mm.then_inc(S["scatter_ps"], 1)

                def expert(e, last):
                    i = i0 + MOE_STRIPES * e
                    turns = MOE_STRIPES * e
                    turn_hidden(i)
                    up(n0 + 4, 0, i + 1, turns)
                    up(n0 + 6, 1, i + 1, turns)
                    pe.wait_ge(S["acc_done"], 4 * (e0 + e) + 1)
                    down(n0 + 8, i + 1, turns, first=True)
                    turn_hidden(i + 1)
                    turn_pick(e)
                    with pe.Fori(2, MOE_STRIPES - 1) as t:
                        up(n0 + 4, 0, i + t, turns + t - 1)
                        up(n0 + 6, 1, i + t, turns + t - 1)
                        down(n0 + 8, i + t, turns + t - 1)
                        turn_hidden(i + t)
                    t = MOE_STRIPES - 1
                    up(n0 + 4, 0, i + t, turns + t - 1)
                    up(n0 + 6, 1, i + t, turns + t - 1)
                    if not last:
                        pe.wait_ge(S["hidT_lo_done"], i + t)
                        pe.wait_ge(S["pickT_done"], e0 + e + 1)
                        gather(e + 1)
                    down(n0 + 8, i + t, turns + t - 1)
                    if not last:
                        pe.wait_ge(S["xg_hi_done"], e0 + e + 2)
                    turn_hidden(i + t)
                    if last:
                        down(n0 + 4, i + t + 1, turns + t)
                    else:
                        pe.wait_ge(S["xg_lo_done"], e0 + e + 2)
                        up(n0 + 4, 0, i + t + 1, turns + t)
                        down(n0 + 6, i + t + 1, turns + t)
                        up(n0 + 8, 1, i + t + 1, turns + t)
                    scatter(e)

                if rnd == 0:
                    pe.wait_ge(S["h_lo_done"], BLOCKS)
                else:
                    pe.wait_ge(S["acc_done"], 4 * e0 + 1)
                gather(0)
                pe.wait_ge(S["xg_hi_done"], e0 + 1)
                pe.wait_ge(S["xg_lo_done"], e0 + 1)
                up(n0, 0, i0, 0)
                up(n0 + 2, 1, i0, 0)
                with pe.Fori(0, EXPERTS - 1) as e:
                    expert(e, False)
                expert(EXPERTS - 1, True)

            pe.wait_ge(S["consts"], 3)
            mixer(0)
            dense()
            mixer(1)
            route()
            experts(0)
            pe.wait_ge(S["most_done"], 1)
            most_tokens = pe.value_load(most_i[0:1, 0:1])
            with pe.If(most_tokens > SLOTS):
                experts(1)

        @block.scalar
        def _(act):
            act.dma_start(rope_sb[:, :, :, :], rope).then_inc(S["rope_loaded"], 16)

            def norm(i):
                for b in range(BLOCKS):
                    if i == 0:
                        act.wait_ge(S["x_loaded"], 16)
                    else:
                        act.wait_ge(S["x_added"], BLOCKS * (i - 1) + b + 1)
                    act.activation(h_tok[:, b, :], x_tok[:, b, :], ACT.Square,
                                   accum_out=norm_ss[:, 0, b:b + 1]).then_inc(S["ss_done"], 1)
                    act.wait_ge(S["var_done"], BLOCKS * i + b + 1)
                    act.activation(norm_ss[:, 2, b:b + 1], norm_ss[:, 1, b:b + 1], ACT.Sqrt)\
                       .then_inc(S["std_done"], 1)

            def turned_hi(i, ready, bank, done):
                for q in range(4):
                    act.wait_ge(ready, 4 * i + q + 1)
                    act.activation(flat(hT_hi[:, 2 * q:2 * q + 2, :]), ps[:, bank + q, :], ACT.Copy)\
                       .then_inc(done, 1)

            def sigmoid_gate(layer, c, k, half):
                act.wait_ge(used, MIX0[layer] + c + 2)
                if k >= 4:
                    act.wait_ge(S["mixed_done"], 5 * layer + 1)
                elif k >= 2:
                    act.wait_ge(S["gated"], 4 * layer + 2)
                act.activation(gate[:, :, half * HALF:(half + 1) * HALF], ps[:, 2 * half:2 * half + 2, :],
                               ACT.Sigmoid).then_inc(S["gate_done"], 1)

            def softmax_exp(layer, i):
                n, keys = 4 * layer + i, (i // 2 + 1) * P
                act.wait_ge(S["shifted"], n + 1)
                for h in range(4):
                    ins = act.activation(probs[:, h, 0:keys], probs[:, h, 0:keys], ACT.Exp,
                                         bias=rowmax[:, h:h + 1], accum_out=rowsum[:, h:h + 1])
                    ins.then_inc(S["exp_done"], 1)

            def normalise(layer, i):
                n, keys = 4 * layer + i, (i // 2 + 1) * P
                act.wait_ge(S["row_inv_done"], n + 1)
                for h in range(4):
                    act.activation(probs[:, h, 0:keys], probs[:, h, 0:keys], ACT.Copy, scale=rowinv[:, h:h + 1])\
                       .then_inc(S["prob_done"], 1)

            def copy_pT(layer, i):
                n, tiles = 4 * layer + i, i // 2 + 1
                act.wait_ge(S["pT_ps"], n + 1)
                act.activation(flat(probs[:, :, :])[:, 0:tiles * 4 * P], banks(6, tiles), ACT.Copy)\
                   .then_inc(S["pT_copied"], 1)

            def copy_o(layer, i):
                n, b, g = 4 * layer + i, i // 2, i % 2
                act.wait_ge(S["o_ps"], n + 1)
                act.activation(qkT[:, 2 * g:2 * g + 2, b * P:(b + 1) * P],
                               ps[:, 6, 0:2 * P].rearrange("p (a n) -> p a n", a=2), ACT.Copy)\
                   .then_inc(S["o_copied"], 1)

            def yc_hi(layer):
                act.wait_ge(S["o_copied"], 4 * (layer + 1))
                act.wait_ge(used, MIX0[layer] + C_OA + 2)
                act.activation(flat(yac_hi[:, :, :]), flat(qkT[:, 0:4, :]), ACT.Copy).then_inc(S["yc_hi_done"], 1)

            def step_sizes(layer):
                act.wait_ge(S[f"par_loaded{layer}"], 16)
                act.activation(trig_row(DT), par_sb[:, PAR_LDT:PAR_LDT + SCHUNKS], ACT.Exp).then_inc(S["dt_exp"], 1)

            def decays(layer):
                act.wait_ge(S["lrdt_done"], layer + 1)
                act.activation(trig_row(MAG), trig_row(LRDT), ACT.Exp).then_inc(S["mag_exp"], 1)

            def mixer(layer):
                c0 = MIX0[layer]
                sp = lambda c: split_hi(act, c0 + c, width=mix_width(layer, c))
                if layer == 0:
                    norm(0)
                    sp(0)
                else:
                    sp(0)
                    sp(1)
                    norm(2)
                    sp(2)
                turned_hi(2 * layer, S["hT_ps"], 0, S["hT_hi_done"])
                if layer == 0:
                    step_sizes(0)
                    sp(1)
                    sp(2)
                    decays(0)
                sp(3)
                act.wait_ge(used, c0 + C_KV + 2)
                act.wait_ge(S["hT_lo_done"], 4 * (2 * layer + 1))
                kv = ps[:, 0:2, :]
                for to, at, width in ((10, 2, IDX_HEADS), (14, 6, 1), (15, 6, 1), (8, 0, 1), (9, 0, 1)):
                    act.activation(h_tok[:, :, to * HD:(to + width) * HD], kv[:, :, at * HD:(at + width) * HD],
                                   ACT.Copy).then_inc(S["kv_copied"], 1)
                act.activation(v_sb[:, :, :], kv[:, :, HD:2 * HD], ACT.Copy).then_inc(S["kv_copied"], 1)
                act.activation(wi_sb[:, :, :], kv[:, :, 7 * HD:7 * HD + IDX_HEADS], ACT.Copy,
                               scale=IDX_HEADS ** -0.5).then_inc(S["kv_copied"], 1)
                for head in (8, 9):
                    act.activation(squares[:, :, head * HD:(head + 1) * HD], kv[:, :, 0:HD], ACT.Square)\
                       .then_inc(S["sq_done"], 1)
                sp(4)
                sp(5)
                act.wait_ge(S["idxT_ps"], layer + 1)
                act.activation(flat(qkT[:, 5:8, :]), banks(6, 2)[:, 0:3 * SEQ], ACT.Copy).then_inc(S["idxT_copied"], 1)
                act.wait_ge(used, c0 + C_Q + 2)
                act.activation(squares[:, :, 0:HALF], ps[:, 2:4, :], ACT.Square).then_inc(S["sq_done"], 1)
                act.activation(h_tok[:, :, 0:HALF], ps[:, 2:4, :], ACT.Copy).then_inc(S["q_copied"], 1)
                sp(6)
                act.wait_ge(S["qk_ss_done"], layer + 1)
                act.activation(qk_ss[:, 1, :, :], qk_ss[:, 0, :, :], ACT.Sqrt).then_inc(S["qk_std_done"], 1)
                sp(7)
                act.wait_ge(used, c0 + C_SU + 2)
                act.activation(flat(su[:, :, :]), banks(0, 2), ACT.Copy).then_inc(S["su_copied"], 1)
                sp(8)
                sp(9)
                act.wait_ge(used, c0 + C_AU + 2)
                act.activation(flat(u_t[:, :, :]), banks(2, 2), ACT.Copy).then_inc(S["u_copied"], 1)
                act.wait_ge(S["qkT_ps"], 2 * layer + 1)
                act.activation(flat(qkT[:, 0:4, :]), banks(6, 2), ACT.Copy).then_inc(S["qkT_copied"], 1)
                sp(10)
                act.wait_ge(S["qkT_ps"], 2 * layer + 2)
                act.activation(qkT[:, 4, :], ps[:, 6, 0:SEQ], ACT.Copy).then_inc(S["qkT_copied"], 1)
                sp(11)
                softmax_exp(layer, 0)
                normalise(layer, 0)
                sp(12)
                copy_pT(layer, 0)
                sp(13)
                copy_o(layer, 0)
                softmax_exp(layer, 1)
                normalise(layer, 1)
                sp(14)
                copy_pT(layer, 1)
                sp(15)
                act.wait_ge(S["conv_done"], layer + 1)
                act.activation(flat(yac_hi[:, :, :]), flat(u_t[:, :, :]), ACT.Copy).then_inc(S["ya_hi_done"], 1)
                copy_o(layer, 1)
                sigmoid_gate(layer, C_GA, 0, 0)
                softmax_exp(layer, 2)
                normalise(layer, 2)
                sp(16)
                sp(17)
                copy_pT(layer, 2)
                sigmoid_gate(layer, C_GA + 2, 1, 1)
                sp(18)
                copy_o(layer, 2)
                softmax_exp(layer, 3)
                sp(19)
                normalise(layer, 3)
                sp(20)
                copy_pT(layer, 3)
                sp(21)
                sigmoid_gate(layer, C_GC, 2, 0)
                copy_o(layer, 3)
                yc_hi(layer)
                sp(22)
                sp(23)
                sigmoid_gate(layer, C_GC + 2, 3, 1)
                sp(24)
                sp(25)
                sp(26)
                act.wait_ge(S["skip_done"], CT * (layer + 1))
                act.activation(flat(su[:, :, :]), flat(su[:, :, :]), ACT.Gelu_apprx_tanh).then_inc(S["gelu_done"], 1)
                act.wait_ge(S["gelu_done"], layer + 1)
                act.wait_ge(S["rotated"], SCHUNKS * (layer + 1))
                act.activation(flat(yb_hi[:, :, :]), flat(su[:, :, :]), ACT.Copy).then_inc(S["yg_hi_done"], 1)
                sp(27)
                sigmoid_gate(layer, C_GB, 4, 0)
                sp(28)
                act.wait_ge(used, c0 + C_GLU + 1)
                act.activation(flat(u_t[:, :, :]), banks(4, 2), ACT.Sigmoid).then_inc(S["glu_sig"], 1)
                sp(29)
                act.wait_ge(S["yb_made"], layer + 1)
                act.activation(flat(yb_hi[:, :, :]), flat(su[:, :, :]), ACT.Copy).then_inc(S["yb_hi_done"], 1)
                sp(30)
                sigmoid_gate(layer, C_GB2, 5, 1)
                sp(31)
                sp(32)
                sp(33)
                turned_hi(layer, S["mixT_ps"], 4, S["mixT_hi_done"])
                sp(34)

            def silu(i, after, width=HALF):
                act.wait_ge(used, after)
                act.wait_ge(S["hid_done"], i)
                act.activation(sil[:, 0:width], ps[:, 0, 0:width], ACT.Silu).then_inc(S["sil_done"], 1)

            def hidden_hi(i, bank):
                act.wait_ge(S["hidT_ps"], i + 1)
                act.activation(hidT_hi[:, :], ps[:, bank, :], ACT.Copy).then_inc(S["hidT_hi_done"], 1)

            def dense():
                n = DENSE0
                split_hi(act, n)
                split_hi(act, n + 1)
                norm(1)
                split_hi(act, n + 2)
                turned_hi(1, S["hT_ps"], 0, S["hT_hi_done"])
                split_hi(act, n + 3)
                silu(0, n + 1)
                split_hi(act, n + 4)
                step_sizes(1)
                hidden_hi(0, 2)
                decays(1)
                with act.Fori(0, (DENSE_STRIPES - 3) // 2) as t:
                    for h in range(2):
                        m = n + 5 + 3 * h
                        split_hi(act, m, t)
                        silu(2 * t + h + 1, n + 3 + 3 * h + 6 * t)
                        split_hi(act, m + 1, t)
                        split_hi(act, m + 2, t)
                        hidden_hi(2 * t + h + 1, 2)
                last = n + 5 + 6 * ((DENSE_STRIPES - 3) // 2)
                i = DENSE_STRIPES - 2
                split_hi(act, last)
                silu(i, last - 2 + 0)
                split_hi(act, last + 1)
                split_hi(act, last + 2)
                hidden_hi(i, 2)
                split_hi(act, last + 3)
                silu(i + 1, last + 1)
                hidden_hi(i + 1, 2)

            def route():
                split_hi(act, MOE0)
                split_hi(act, MOE0 + 1)
                act.wait_ge(S["router_loaded"], 16)
                act.activation(flat(router_hi[:, :, :]), flat(router_sb[:, :, :]), ACT.Copy)\
                   .then_inc(S["router_hi_done"], 1)
                norm(3)
                turned_hi(3, S["hT_ps"], 0, S["hT_hi_done"])
                for b in range(BLOCKS):
                    act.activation(h_hi[:, b, :], h_tok[:, b, :], ACT.Copy).then_inc(S["h_hi_done"], 1)
                act.wait_ge(S["top_r"], 1)
                act.activation(flat(rt[:, 2]), flat(rt[:, 1]), ACT.Exp).then_inc(S["exp_r"], 1)

            def experts(rnd):
                n0 = MOE0 + rnd * EXPERTS * MOE_CHUNKS
                e0 = rnd * EXPERTS
                i0 = DENSE_STRIPES + e0 * MOE_STRIPES

                def xg(e):
                    act.wait_ge(S["gather_ps"], 2 * (e0 + e) + 1)
                    act.activation(flat(xg_hi[:, :, :]), banks(4, 2), ACT.Copy).then_inc(S["xg_hi_done"], 1)

                def stripe(i, t, turns):
                    split_hi(act, n0 + 6, turns)
                    hidden_hi(i + t - 1, 4)
                    split_hi(act, n0 + 7, turns)
                    silu(i + t, n0 + 6 + 6 * turns)
                    split_hi(act, n0 + 8, turns)
                    split_hi(act, n0 + 9, turns)

                def expert(e, last):
                    i = i0 + MOE_STRIPES * e
                    turns = MOE_STRIPES * e
                    stripe(i, 1, turns)
                    split_hi(act, n0 + 10, turns)
                    split_hi(act, n0 + 11, turns)
                    act.wait_ge(S["pickT_ps"], e0 + e + 1)
                    act.activation(flat(pickT[:, :, :]), ps[:, 5, 0:2 * P], ACT.Copy).then_inc(S["pickT_done"], 1)
                    with act.Fori(2, MOE_STRIPES - 1) as t:
                        stripe(i, t, turns + t - 1)
                        split_hi(act, n0 + 10, turns + t - 1)
                        split_hi(act, n0 + 11, turns + t - 1)
                    t = MOE_STRIPES - 1
                    stripe(i, t, turns + t - 1)
                    split_hi(act, n0 + 10, turns + t - 1)
                    if not last:
                        xg(e + 1)
                    split_hi(act, n0 + 11, turns + t - 1)
                    if not last:
                        split_hi(act, n0 + 6, turns + t)
                    hidden_hi(i + t, 4)
                    if not last:
                        split_hi(act, n0 + 7, turns + t)
                        silu(i + t + 1, n0 + 6 + 6 * (turns + t))
                        split_hi(act, n0 + 8, turns + t)
                        split_hi(act, n0 + 9, turns + t)
                    act.wait_ge(used, n0 + (6 if last else 8) + 6 * (turns + t))
                    for half in range(2):
                        act.activation(y_hi[:, half * HALF:(half + 1) * HALF], ps[:, 2 + half, :], ACT.Copy)\
                           .then_inc(S["y_hi_done"], 1)
                    if not last:
                        split_hi(act, n0 + 10, turns + t)
                        split_hi(act, n0 + 11, turns + t)

                if rnd > 0:
                    split_hi(act, n0)
                    split_hi(act, n0 + 1)
                split_hi(act, n0 + 2)
                xg(0)
                split_hi(act, n0 + 3)
                silu(i0, n0 + 2)
                split_hi(act, n0 + 4)
                split_hi(act, n0 + 5)
                with act.Fori(0, EXPERTS - 1) as e:
                    expert(e, False)
                expert(EXPERTS - 1, True)

            mixer(0)
            dense()
            mixer(1)
            route()
            experts(0)
            act.wait_ge(S["most_done"], 1)
            most_tokens = act.value_load(most_i[0:1, 0:1])
            with act.If(most_tokens > SLOTS):
                experts(1)

        @block.vector
        def _(dve):
            own = Chain(dve, dve_step)

            def norm(i, gains, after=None, bank=0):
                def add(b):
                    if after is None:
                        return
                    if b == 0:
                        dve.wait_ge(S["x_block0"], i)
                    else:
                        dve.wait_ge(used, after)
                    dve.tensor_tensor(x_tok[:, b, :], x_tok[:, b, :], banks(bank + 2 * b, 2), ALU.add)\
                       .then_inc(S["x_added"], 1)

                def variance(b):
                    dve.wait_ge(S["ss_done"], BLOCKS * i + b + 1)
                    dve.tensor_scalar(norm_ss[:, 1, b:b + 1], norm_ss[:, 0, b:b + 1], 1.0 / D, EPS, ALU.mult,
                                      ALU.add).then_inc(S["var_done"], 1)

                def scale(b):
                    dve.wait_ge(S["std_done"], BLOCKS * i + b + 1)
                    own.then(dve.reciprocal(norm_ss[:, 3, b:b + 1], norm_ss[:, 2, b:b + 1]))
                    if b == 0:
                        dve.wait_ge(S["gain_loaded"], 16 * (i + 1))
                    dve.scalar_tensor_tensor(h_tok[:, b, :], x_tok[:, b, :], norm_ss[:, 3, b:b + 1], gains,
                                             ALU.mult, ALU.mult).then_inc(S["h_done"], 1)

                add(0)
                variance(0)
                add(1)
                scale(0)
                variance(1)
                scale(1)

            def turned_lo(i, ready, bank, done):
                for q in range(4):
                    dve.wait_ge(ready, 4 * i + q + 1)
                    dve.tensor_tensor(flat(hT_lo[:, 2 * q:2 * q + 2, :]), ps[:, bank + q, :],
                                      flat(hT_hi[:, 2 * q:2 * q + 2, :]).bitcast(F32), ALU.subtract).then_inc(done, 1)

            def rotate_in(layer, j):
                n = SCHUNKS * layer + j
                if layer == 0:
                    dve.wait_ge(S["table_done"], 2 * (j + 1))
                else:
                    dve.wait_ge(S[f"table_loaded{j % 4}"], 16 * (j // 4 + 1))
                if n >= 2:
                    dve.wait_ge(S["rotated"], n - 1)
                dve.wait_ge(S["bu_ps"], n + 1)
                t = turn[:, j % 2]
                cos, sin = table_at(layer, j)[:, 0, :], table_at(layer, j)[:, 1, :]
                re, im = ps[:, 4, 0:SEQ], ps[:, 4, SEQ:2 * SEQ]
                own.step(dve.tensor_tensor(t[:, 0, :], re, cos, ALU.mult))
                own.step(dve.tensor_tensor(t[:, 1, :], im, sin, ALU.mult))
                own.step(dve.tensor_tensor(t[:, 2, :], im, cos, ALU.mult))
                dve.tensor_tensor(t[:, 3, :], re, sin, ALU.mult).then_inc(S["turned"], 1)
                own.join()
                own.step(dve.tensor_tensor(t[:, 0, :], t[:, 0, :], t[:, 1, :], ALU.add))
                dve.wait_ge(S["turned"], n + 1)
                own.step(dve.tensor_tensor(t[:, 2, :], t[:, 2, :], t[:, 3, :], ALU.subtract))
                own.join()
                mag = trig[:, 3, j:j + 1].broadcast_to([P, SEQ])
                dve.tensor_tensor_scan(t[:, 1, :], mag, t[:, 0, :], 0.0, ALU.mult, ALU.add).then_inc(S["scanned"], 1)
                dve.tensor_tensor_scan(t[:, 3, :], mag, t[:, 2, :], 0.0, ALU.mult, ALU.add).then_inc(S["scanned"], 1)

            def add_skip(layer, c):
                dve.wait_ge(S["y_ps"], SCHUNKS * layer + 4 * c + 4)
                at = (c % 2) * SEQ
                dve.scalar_tensor_tensor(su[:, c, :], su[:, c, :], par_sb[:, PAR_D + c:PAR_D + c + 1],
                                         ps[:, 5, at:at + SEQ], ALU.mult, ALU.add).then_inc(S["skip_done"], 1)

            def conv(layer):
                u2 = u_t
                for tap in range(3):
                    for c in range(CT):
                        w = par_sb[:, PAR_CW + tap * CT + c:PAR_CW + tap * CT + c + 1]
                        v = v_t[:, c, tap:tap + SEQ]
                        if tap == 0:
                            own.step(dve.tensor_scalar(u2[:, c, :], v, w, None, ALU.mult))
                        else:
                            own.step(dve.scalar_tensor_tensor(u2[:, c, :], v, w, u2[:, c, :], ALU.mult, ALU.add))
                    own.join()
                dve.wait_ge(used, MIX0[layer] + C_AB + 2)
                dve.tensor_tensor(flat(u_t[:, :, :]), flat(u_t[:, :, :]), banks(2, 2), ALU.mult)\
                   .then_inc(S["conv_done"], 1)

            def score(layer, b):
                dve.wait_ge(S["idx_ps"], 2 * layer + b + 1)
                keys = (b + 1) * P
                sc, tmp = keybias[:, b, 0:keys], scratch[:, 1, 0:keys]
                for h in range(IDX_HEADS):
                    at = (h // 2) * keys
                    src = ps[:, 6 + h % 2, at:at + keys]
                    ins = dve.tensor_scalar(sc if h == 0 else scratch[:, h, 0:keys], src, 0.0,
                                            wi_sb[:, b, h:h + 1], ALU.max, ALU.mult)
                    if h < IDX_HEADS - 1:
                        own.step(ins)
                    else:
                        ins.then_inc(S["scored"], 1)
                own.join()
                dve.wait_ge(S["scored"], 2 * layer + b + 1)
                own.step(dve.tensor_tensor(sc, sc, tmp, ALU.add))
                own.then(dve.tensor_tensor(scratch[:, 2, 0:keys], scratch[:, 2, 0:keys], scratch[:, 3, 0:keys],
                                           ALU.add))
                own.then(dve.tensor_tensor(sc, sc, scratch[:, 2, 0:keys], ALU.add))
                diag = sc[:, b * P:keys]
                own.then(dve.tensor_tensor(diag, diag, causal[:, :], ALU.add))

            def choice_rows(b):
                if b == 0:
                    return (probs[:, r, 0:P] for r in range(1, 4))
                return (gate[:, r // 2, HALF + SEQ * (r % 2):HALF + SEQ * (r % 2 + 1)] for r in range(1, 4))

            def best(layer, b, first, last):
                keys = (b + 1) * P
                sc = keybias[:, b, 0:keys]
                work, _, _ = choice_rows(b)
                if b == 1 and first == 0:
                    dve.wait_ge(S["rope_done"], BLOCKS * (layer + 1))
                for r in range(first, last):
                    src = sc if r == 0 else work
                    own.then(dve.max(top8[:, :], src))
                    if r < TOPK // 8 - 1:
                        own.then(dve.match_replace(work, top8[:, :], src, DEAD))

            def choose(b):
                keys = (b + 1) * P
                sc = keybias[:, b, 0:keys]
                work, gt, eq = choice_rows(b)
                kth = top8[:, 7:8]
                own.step(dve.tensor_scalar(gt, sc, kth, None, ALU.is_gt))
                own.then(dve.tensor_scalar(eq, sc, kth, None, ALU.is_equal))
                own.step(dve.tensor_reduce(smalls[:, 0:1], gt, AX_X, ALU.add))
                own.then(dve.tensor_tensor_scan(work, ones_row(keys), eq, 0.0, ALU.mult, ALU.add))
                own.then(dve.tensor_scalar(smalls[:, 1:2], smalls[:, 0:1], -1.0, float(TOPK), ALU.mult, ALU.add))
                own.then(dve.scalar_tensor_tensor(work, work, smalls[:, 1:2], eq, ALU.is_le, ALU.mult))
                own.then(dve.tensor_tensor(work, work, gt, ALU.add))
                own.then(dve.tensor_scalar(sc, work, -NEG, NEG, ALU.mult, ALU.add))
                diag = keybias[:, b, b * P:keys]
                own.then(dve.tensor_tensor(diag, diag, causal[:, :], ALU.add))

            def ones_row(width):
                return ones[:, 0:1].broadcast_to([P, width])

            def shift(layer, i):
                n, b = 4 * layer + i, i // 2
                keys = (b + 1) * P
                dve.wait_ge(S["logit_ps"], n + 1)
                dst = probs[:, :, 0:keys]
                bias = keybias[:, b:b + 1, 0:keys].broadcast_to([P, 2, keys])
                for odd in range(2):
                    src = ps[:, 6 + odd, 0:2 * keys].rearrange("p (h k) -> p h k", h=2)
                    own.step(dve.scalar_tensor_tensor(dst[:, 2 * odd:2 * odd + 2, :], src, HD ** -0.5, bias,
                                                      ALU.mult, ALU.add))
                own.join()
                own.then(dve.tensor_reduce(rowinv[:, :], dst, AX_X, ALU.max))
                dve.tensor_scalar(rowmax[:, :], rowinv[:, :], -1.0, None, ALU.mult).then_inc(S["shifted"], 1)

            def invert_sums(layer, i):
                n = 4 * layer + i
                dve.wait_ge(S["exp_done"], 4 * (n + 1))
                dve.reciprocal(rowinv[:, :], rowsum[:, :]).then_inc(S["row_inv_done"], 1)

            def merge_gate(layer, branch, c):
                dve.wait_ge(S["gate_done"], 6 * layer + 2 * (branch + 1))
                for b in range(BLOCKS):
                    if b == 0:
                        dve.wait_ge(S["branch_block0"], 2 * layer + branch + 1)
                    else:
                        dve.wait_ge(used, MIX0[layer] + c + 2)
                    dst = (gate if branch else mixed)[:, b, :]
                    dve.tensor_tensor(dst, gate[:, b, :], banks(2 * b, 2), ALU.mult).then_inc(S["gated"], 1)

            def merge_add(layer):
                dve.wait_ge(S["gated"], 4 * (layer + 1))
                dve.tensor_tensor(flat(mixed[:, :, :]), flat(mixed[:, :, :]), flat(gate[:, :, :]), ALU.add)\
                   .then_inc(S["mixed_done"], 1)

            def merge_last(layer):
                dve.wait_ge(S["gate_done"], 6 * (layer + 1))
                dve.wait_ge(S["mixed_done"], 5 * layer + 1)
                for q in range(4):
                    if q < 3:
                        dve.wait_ge(S["ob_quarters"], 3 * layer + q + 1)
                    else:
                        dve.wait_ge(used, MIX0[layer] + C_OB + 2)
                    part = (slice(None), q // 2, slice((q % 2) * HALF, (q % 2 + 1) * HALF))
                    own.then(dve.tensor_tensor(gate[part], gate[part], ps[:, q, :], ALU.mult))
                    dve.tensor_tensor(mixed[part], mixed[part], gate[part], ALU.add).then_inc(S["mixed_done"], 1)

            def sub_hi(dst, whole, hi, done):
                dve.tensor_tensor(dst, whole, hi.bitcast(F32), ALU.subtract).then_inc(done, 1)

            def invert_den(layer):
                dve.wait_ge(S["den_done"], layer + 1)
                dve.reciprocal(trig_row(INV), trig_row(DEN)).then_inc(S["den_inv"], 1)

            def mixer(layer):
                c0 = MIX0[layer]
                chunk = lambda c: split_lo(dve, c0 + c, width=mix_width(layer, c))
                turn_j = lambda j: rotate_in(layer, j)
                if layer == 0:
                    norm(0, gain_row)
                    chunk(0)
                    turned_lo(0, S["hT_hi_done"], 0, S["hT_lo_done"])
                    chunk(1)
                    s5_rates(dve, own, 0)
                    invert_den(0)
                    chunk(2)
                    s5_angles(dve, own, 0)
                    chunk(3)
                    s5_powers(dve, own, 0, 4)
                    chunk(4)
                    s5_powers(dve, own, 4, 8)
                    dve.wait_ge(S["powers_done"], 1)
                    chunk(5)
                else:
                    chunk(0)
                    chunk(1)
                    norm(2, gain_row, DENSE0 + DENSE_CHUNKS, 4)
                    turned_lo(2, S["hT_hi_done"], 0, S["hT_lo_done"])
                    for c in range(2, 6):
                        chunk(c)
                score(layer, 0)
                dve.wait_ge(S["sq_done"], 3 * (layer + 1))
                own.then(dve.tensor_reduce(qk_ss[:, 2, :, :], gate_sq, AX_X, ALU.add))
                dve.tensor_scalar(qk_ss[:, 0, :, :], qk_ss[:, 2, :, :], 1.0 / HD, EPS, ALU.mult, ALU.add)\
                   .then_inc(S["qk_ss_done"], 1)
                chunk(6)
                dve.wait_ge(S["qk_std_done"], layer + 1)
                dve.reciprocal(qk_ss[:, 2, :, :], qk_ss[:, 1, :, :]).then_inc(S["qk_inv_done"], 1)
                score(layer, 1)
                if layer == 0:
                    s5_fold(dve, own, 0)
                chunk(7)
                best(layer, 0, 0, 4)
                chunk(8)
                turn_j(0)
                best(layer, 0, 4, 8)
                choose(0)
                chunk(9)
                turn_j(1)
                chunk(10)
                turn_j(2)
                shift(layer, 0)
                own.then(dve.memset(v_t[:, :, 0:2], 0.0))
                dve.wait_ge(used, c0 + C_AC + 2)
                dve.wait_ge(S["u_copied"], layer + 1)
                dve.tensor_tensor(v_t[:, :, 2:SEQ + 2], u_t[:, :, :],
                                  banks(0, 2).rearrange("p (c n) -> p c n", c=CT), ALU.mult).then_inc(S["v_made"], 1)
                invert_sums(layer, 0)
                chunk(11)
                turn_j(3)
                best(layer, 1, 0, 4)
                chunk(12)
                turn_j(4)
                shift(layer, 1)
                best(layer, 1, 4, 8)
                invert_sums(layer, 1)
                chunk(13)
                turn_j(5)
                dve.wait_ge(S["v_made"], layer + 1)
                conv(layer)
                chunk(14)
                turn_j(6)
                add_skip(layer, 0)
                choose(1)
                chunk(15)
                turn_j(7)
                shift(layer, 2)
                dve.wait_ge(S["ya_hi_done"], layer + 1)
                sub_hi(flat(yac_lo[:, :, :]), flat(u_t[:, :, :]), flat(yac_hi[:, :, :]), S["ya_lo_done"])
                invert_sums(layer, 2)
                chunk(16)
                turn_j(8)
                chunk(17)
                turn_j(9)
                chunk(18)
                shift(layer, 3)
                turn_j(10)
                invert_sums(layer, 3)
                add_skip(layer, 1)
                chunk(19)
                merge_gate(layer, 0, C_OA)
                turn_j(11)
                chunk(20)
                turn_j(12)
                chunk(21)
                turn_j(13)
                chunk(22)
                add_skip(layer, 2)
                dve.wait_ge(S["yc_hi_done"], layer + 1)
                sub_hi(flat(yac_lo[:, :, :]), flat(qkT[:, 0:4, :]), flat(yac_hi[:, :, :]), S["yc_lo_done"])
                turn_j(14)
                chunk(23)
                turn_j(15)
                chunk(24)
                merge_gate(layer, 1, C_OC)
                chunk(25)
                merge_add(layer)
                chunk(26)
                add_skip(layer, 3)
                dve.wait_ge(S["yg_hi_done"], layer + 1)
                sub_hi(flat(yb_lo[:, :, :]), flat(su[:, :, :]), flat(yb_hi[:, :, :]), S["yg_lo_done"])
                chunk(27)
                chunk(28)
                dve.wait_ge(S["glu_sig"], layer + 1)
                dve.tensor_tensor(flat(su[:, :, :]), flat(su[:, :, :]), flat(u_t[:, :, :]), ALU.mult)\
                   .then_inc(S["yb_made"], 1)
                chunk(29)
                dve.wait_ge(S["yb_hi_done"], layer + 1)
                sub_hi(flat(yb_lo[:, :, :]), flat(su[:, :, :]), flat(yb_hi[:, :, :]), S["yb_lo_done"])
                chunk(30)
                chunk(31)
                chunk(32)
                merge_last(layer)
                turned_lo(layer, S["mixT_hi_done"], 4, S["mixT_lo_done"])
                chunk(33)
                chunk(34)

            def times_up(sil_seen, w3_used, turned, width=HALF):
                dve.wait_ge(S["sil_done"], sil_seen)
                dve.wait_ge(used, w3_used)
                if turned is not None:
                    dve.wait_ge(S["hidT_ps"], turned)
                dve.tensor_tensor(hid[:, 0:width], sil[:, 0:width], ps[:, 1, 0:width], ALU.mult)\
                   .then_inc(S["hid_done"], 1)

            def hidden_lo(seen, bank):
                dve.wait_ge(S["hidT_hi_done"], seen)
                dve.tensor_tensor(hidT_lo[:, :], ps[:, bank, :], hidT_hi[:, :].bitcast(F32), ALU.subtract)\
                   .then_inc(S["hidT_lo_done"], 1)

            def dense():
                n = DENSE0
                split_lo(dve, n)
                split_lo(dve, n + 1)
                norm(1, gain_ff[:, :], DENSE0)
                turned_lo(1, S["hT_hi_done"], 0, S["hT_lo_done"])
                split_lo(dve, n + 2)
                split_lo(dve, n + 3)
                times_up(1, n + 2, None)
                split_lo(dve, n + 4)
                split_lo(dve, n + 5)
                hidden_lo(1, 2)
                split_lo(dve, n + 6)
                invert_den(1)
                with dve.Fori(0, (DENSE_STRIPES - 3) // 2) as t:
                    hi_at = [dve.snap(n + 7 + k + 1 + 6 * t) for k in range(6)]
                    w3_at = [dve.snap(n + 4 + 3 * h + 6 * t) for h in range(2)]
                    i_at = [dve.snap(2 * t + k) for k in range(1, 4)]
                    for h in range(2):
                        m = n + 7 + 3 * h
                        times_up(i_at[h + 1], w3_at[h], i_at[h])
                        split_lo(dve, m, hi_at[3 * h])
                        split_lo(dve, m + 1, hi_at[3 * h + 1])
                        hidden_lo(i_at[h + 1], 2)
                        split_lo(dve, m + 2, hi_at[3 * h + 2])
                m = n + 7 + 6 * ((DENSE_STRIPES - 3) // 2)
                i = DENSE_STRIPES - 2
                times_up(i + 1, m - 3, i)
                split_lo(dve, m)
                split_lo(dve, m + 1)
                hidden_lo(i + 1, 2)
                times_up(i + 2, m, i + 1)
                hidden_lo(i + 2, 2)

            def route():
                split_lo(dve, MOE0)
                split_lo(dve, MOE0 + 1)
                dve.wait_ge(S["router_hi_done"], 1)
                sub_hi(flat(router_lo[:, :, :]), flat(router_sb[:, :, :]), flat(router_hi[:, :, :]),
                       S["router_lo_done"])
                norm(3, gain_ff[:, :], MOE0)
                turned_lo(3, S["hT_hi_done"], 0, S["hT_lo_done"])
                for b in range(BLOCKS):
                    dve.wait_ge(S["h_hi_done"], b + 1)
                    dve.tensor_tensor(h_lo[:, b, :], h_tok[:, b, :], h_hi[:, b, :].bitcast(F32), ALU.subtract)\
                       .then_inc(S["h_lo_done"], 1)
                dve.wait_ge(S["logitsT_ps"], 1)
                dve.tensor_copy(logits_T[:, :], ps[0:EXPERTS, 4, 0:SEQ]).then_inc(S["logitsT_copied"], 1)
                dve.wait_ge(S["logits_ps"], 1)
                lg, shifted_l, ex, gt, eq, rank, keep, sel, tmp = (rt[:, k] for k in range(9))
                own.then(dve.tensor_copy(flat(lg), ps[:, 6, 0:BLOCKS * EXPERTS]))
                for b in range(BLOCKS):
                    own.step(dve.max(rt8[:, b, :], lg[:, b, :]))
                own.join()
                for b in range(BLOCKS):
                    own.step(dve.tensor_scalar(gt[:, b, :], lg[:, b, :], rt8[:, b, 1:2], None, ALU.is_gt))
                    own.step(dve.tensor_scalar(eq[:, b, :], lg[:, b, :], rt8[:, b, 1:2], None, ALU.is_equal))
                    own.step(dve.tensor_scalar(shifted_l[:, b, :], lg[:, b, :], rt8[:, b, 0:1], None, ALU.subtract))
                own.join()
                dve.tensor_reduce(rts[:, 0, :], gt, AX_X, ALU.add).then_inc(S["top_r"], 1)
                for b in range(BLOCKS):
                    own.step(dve.tensor_tensor_scan(rank[:, b, :], ones_row(EXPERTS), eq[:, b, :], 0.0, ALU.mult,
                                                    ALU.add))
                dve.wait_ge(S["top_r"], 1)
                own.then(dve.tensor_scalar(rts[:, 1, :], rts[:, 0, :], -1.0, 2.0, ALU.mult, ALU.add))
                for b in range(BLOCKS):
                    own.step(dve.scalar_tensor_tensor(keep[:, b, :], rank[:, b, :], rts[:, 1, b:b + 1], eq[:, b, :],
                                                      ALU.is_le, ALU.mult))
                own.join()
                dve.tensor_tensor(flat(sel), flat(keep), flat(gt), ALU.add).then_inc(S["picked"], 1)
                dve.wait_ge(S["picked"], 1)
                dve.wait_ge(S["exp_r"], 1)
                own.then(dve.tensor_tensor(flat(tmp), flat(ex), flat(sel), ALU.mult))
                own.then(dve.tensor_reduce(rts[:, 2, :], tmp, AX_X, ALU.add))
                own.then(dve.reciprocal(rts[:, 3, :], rts[:, 2, :]))
                for b in range(BLOCKS):
                    own.step(dve.tensor_scalar(gate_of[:, b, :], tmp[:, b, :], rts[:, 3, b:b + 1], None, ALU.mult))
                dve.wait_ge(S["rank_ps"], 1)
                own.step(dve.tensor_reduce(most[:, :], ps[:, 5, 16:24], AX_X, ALU.max))
                dve.memset(slot_of[:, :, :], -1.0).then_inc(S["acc_done"], 1)
                dve.wait_ge(S["acc_done"], 1)
                own.then(dve.tensor_tensor(flat(rank), ps[:, 5, 0:16], flat(sel), ALU.mult))
                dve.tensor_scalar(slot_of[:, :, 0:EXPERTS], rank, -1.0, None, ALU.add).then_inc(S["slots_done"], 1)
                dve.wait_ge(S["slots_done"], 1)
                dve.tensor_copy(most_i[:, :], most[0:1, :]).then_inc(S["most_done"], 1)

            def pick_slots(e, rnd):
                for b in range(BLOCKS):
                    dve.tensor_scalar(pick[:, b, :], slot_id[:, rnd, :], slot_of[:, b, bass.ds(e, 1)], None,
                                      ALU.is_equal).then_inc(S["pick_done"], 1)

            def experts(rnd):
                n0 = MOE0 + rnd * EXPERTS * MOE_CHUNKS
                e0 = rnd * EXPERTS
                i0 = DENSE_STRIPES + e0 * MOE_STRIPES

                def lo(n, turns):
                    split_lo(dve, n, value(dve, n + 1 + 6 * turns))

                def xg(e):
                    seen = value(dve, 2 * (e0 + e + 1))
                    dve.wait_ge(S["gather_ps"], seen)
                    dve.tensor_copy(flat(xg_lo[:, :, :]), banks(6, 2)).then_inc(S["xg_lo_done"], 1)

                def stripe(i, t, turns):
                    prev, this = value(dve, i + t), value(dve, i + t + 1)
                    w3_at = value(dve, n0 + 8 + 6 * turns)
                    lo(n0 + 6, turns)
                    hidden_lo(prev, 4)
                    lo(n0 + 7, turns)
                    lo(n0 + 8, turns)
                    lo(n0 + 9, turns)
                    times_up(this, w3_at, prev)

                def y(e, y_used):
                    dve.wait_ge(used, y_used)
                    for half in range(2):
                        seen = value(dve, 2 * (e0 + e) + half + 1)
                        part = slice(half * HALF, (half + 1) * HALF)
                        dve.wait_ge(S["y_hi_done"], seen)
                        dve.tensor_tensor(y_lo[:, part], ps[:, 2 + half, :], y_hi[:, part].bitcast(F32),
                                          ALU.subtract).then_inc(S["y_lo_done"], 1)

                def add_to_x(e):
                    e_at, a_at = value(dve, e0 + e + 1), value(dve, 4 * (e0 + e) + 1)
                    dve.wait_ge(S["scatter_ps"], e_at)
                    dve.wait_ge(S["acc_done"], a_at)
                    for b in range(BLOCKS):
                        for half in range(2):
                            dst = x_tok[:, b, half * HALF:(half + 1) * HALF]
                            dve.scalar_tensor_tensor(dst, ps[:, 2 + half if b == 0 else 6 + half, :],
                                                     gate_of[:, b, bass.ds(e, 1)], dst, ALU.mult, ALU.add)\
                               .then_inc(S["acc_done"], 1)

                def expert(e, last):
                    i = i0 + MOE_STRIPES * e
                    turns = MOE_STRIPES * e
                    stripe(i, 1, turns)
                    lo(n0 + 10, turns)
                    if not last:
                        e_at = value(dve, e0 + e + 1)
                        dve.wait_ge(S["pickT_ps"], e_at)
                        pick_slots(value(dve, e + 1), rnd)
                    lo(n0 + 11, turns)
                    with dve.Fori(2, MOE_STRIPES - 1) as t:
                        stripe(i, t, turns + t - 1)
                        lo(n0 + 10, turns + t - 1)
                        lo(n0 + 11, turns + t - 1)
                    t = MOE_STRIPES - 1
                    stripe(i, t, turns + t - 1)
                    lo(n0 + 10, turns + t - 1)
                    if not last:
                        xg(e + 1)
                    if last:
                        hidden_lo(i + t + 1, 4)
                    lo(n0 + 11, turns + t - 1)
                    if last:
                        y(e, n0 + 6 + 6 * (turns + t))
                        add_to_x(e)
                        return
                    turned, y_used = value(dve, i + t + 1), value(dve, n0 + 8 + 6 * (turns + t))
                    next_i, w3_at = value(dve, i + t + 2), value(dve, n0 + 10 + 6 * (turns + t))
                    lo(n0 + 6, turns + t)
                    hidden_lo(turned, 4)
                    lo(n0 + 7, turns + t)
                    lo(n0 + 8, turns + t)
                    lo(n0 + 9, turns + t)
                    y(e, y_used)
                    lo(n0 + 10, turns + t)
                    times_up(next_i, w3_at, turned)
                    lo(n0 + 11, turns + t)
                    add_to_x(e)

                dve.wait_ge(S["slots_loaded"], 16)
                pick_slots(0, rnd)
                if rnd > 0:
                    lo(n0, 0)
                    lo(n0 + 1, 0)
                lo(n0 + 2, 0)
                xg(0)
                lo(n0 + 3, 0)
                lo(n0 + 4, 0)
                times_up(i0 + 1, n0 + 4, i0)
                lo(n0 + 5, 0)
                with dve.Fori(0, EXPERTS - 1) as e:
                    expert(e, False)
                expert(EXPERTS - 1, True)

            gate_sq = flat(gate[:, :, :]).rearrange("p (b h d) -> p b h d", b=BLOCKS, d=HD)[:, :, 0:10, :]
            mixer(0)
            dense()
            mixer(1)
            route()
            experts(0)
            dve.wait_ge(S["most_done"], 1)
            most_tokens = dve.value_load(most_i[0:1, 0:1])
            with dve.If(most_tokens > SLOTS):
                experts(1)
                dve.wait_ge(S["acc_done"], 4 * 2 * EXPERTS + 1)
            dve.wait_ge(S["acc_done"], 4 * EXPERTS + 1)
            dve.tensor_copy(most[:, :], ones[:, 0:1]).then_inc(S["final_done"], 1)

        @block.gpsimd
        def _(pool):
            own = Chain(pool, pool_step)

            def constants():
                for t in (ident, causal):
                    own.step(pool.memset(t[:, :], 0.0))
                pool.memset(ones[:, :], 1.0).then_inc(S["consts"], 1)
                own.join()
                pool.affine_select(out=ident[:, :], in_=ident[:, :], compare_op=ALU.not_equal, fill=1.0, base=0,
                                   pattern=[[-1, P]], channel_multiplier=1).then_inc(S["consts"], 1)
                pool.affine_select(out=causal[:, :], in_=causal[:, :], compare_op=ALU.is_ge, fill=NEG, base=0,
                                   pattern=[[-1, P]], channel_multiplier=1).then_inc(S["consts"], 1)

            def make_upper():
                own.then(pool.memset(upper[:, :], 1.0))
                pool.affine_select(out=upper[:, :], in_=upper[:, :], compare_op=ALU.is_ge, fill=0.0, base=0,
                                   pattern=[[1, P]], channel_multiplier=-1).then_inc(S["upper_made"], 1)

            def load_gain(i, dst):
                pool.dma_start(dst, gains[i].partition_broadcast(P)).then_inc(S["gain_loaded"], 16)

            def make_table(layer, j):
                n = SCHUNKS * layer + j + 1
                slot = j % 2 if layer else j % 3
                if layer == 0 and j >= 3:
                    pool.wait_ge(S["turned"], j - 2)
                if layer == 1 and j >= 2:
                    pool.wait_ge(S[f"table_stored{j % 2}"], 16 * (j // 2))
                a_r, a_i, b_r, b_i = table_factors(j)
                cos, sin = (table[:, slot, i, :].rearrange("p (a b) -> p a b", a=16) for i in range(2))
                s1, s2 = (pool_t[:, i, :].rearrange("p (a b) -> p a b", a=16) for i in range(2))
                own.step(pool.tensor_tensor(s1, a_r, b_r, ALU.mult))
                own.then(pool.tensor_tensor(s2, a_i, b_i, ALU.mult))
                pool.tensor_tensor(cos, s1, s2, ALU.subtract).then_inc(S["table_done"], 1)
                pool.wait_ge(S["table_done"], 2 * n - 1)
                own.step(pool.tensor_tensor(s1, a_r, b_i, ALU.mult))
                own.then(pool.tensor_tensor(s2, a_i, b_r, ALU.mult))
                pool.tensor_tensor(sin, s1, s2, ALU.add).then_inc(S["table_done"], 1)
                pool.wait_ge(S["table_done"], 2 * n)

            def store_table(j):
                make_table(1, j)
                pool.dma_start(table_store[j], flat_table(j)).then_inc(S[f"table_stored{j % 2}"], 16)

            def load_table(j):
                pool.wait_ge(S[f"table_stored{j % 2}"], 16 * (SCHUNKS // 2))
                if j >= 4:
                    pool.wait_ge(S["turned"], SCHUNKS + j - 3)
                pool.dma_start(table_at(1, j), table_store[j].rearrange("p (c t) -> p c t", c=2))\
                    .then_inc(S[f"table_loaded{j % 4}"], 16)

            def flat_table(j):
                return table[:, j % 2, :, :].rearrange("p a t -> p (a t)")

            def rotate_out(layer, j):
                n = SCHUNKS * layer + j
                pool.wait_ge(S["scanned"], 2 * (n + 1))
                if layer == 1:
                    pool.wait_ge(S[f"table_loaded{j % 4}"], 16 * (j // 4 + 1))
                if n >= 1:
                    pool.wait_ge(S["y_ps"], n)
                g_re, g_im = turn[:, j % 2, 1, :], turn[:, j % 2, 3, :]
                cos, sin = table_at(layer, j)[:, 0, :], table_at(layer, j)[:, 1, :]
                own.step(pool.tensor_tensor(pool_t[:, 0, :], g_re, cos, ALU.mult))
                own.then(pool.tensor_tensor(pool_t[:, 1, :], g_im, sin, ALU.mult))
                own.then(pool.tensor_tensor(state[:, 0, :], pool_t[:, 0, :], pool_t[:, 1, :], ALU.subtract))
                own.step(pool.tensor_tensor(pool_t[:, 0, :], g_re, sin, ALU.mult))
                own.then(pool.tensor_tensor(pool_t[:, 1, :], g_im, cos, ALU.mult))
                pool.tensor_tensor(state[:, 1, :], pool_t[:, 0, :], pool_t[:, 1, :], ALU.add).then_inc(S["rotated"], 1)
                pool.wait_ge(S["rotated"], n + 1)

            def rotary(lo, heads, done):
                cols = slice(lo * HD, (lo + heads) * HD)
                for b in range(BLOCKS):
                    xv = h_tok[:, b, cols].rearrange("p (h i d) -> p h i d", i=2, d=32)
                    tv = gate[:, b, cols].rearrange("p (h i d) -> p h i d", i=2, d=32)
                    for i in range(2):
                        sin = rope_sb[:, b, 1 + i, :].unsqueeze(1).broadcast_to([P, heads, 32])
                        own.step(pool.tensor_tensor(tv[:, :, i, :], xv[:, :, 1 - i, :], sin, ALU.mult))
                    own.join()
                    cos = rope_sb[:, b, 0:1, :].broadcast_to([P, 2 * heads, 32])
                    x3 = h_tok[:, b, cols].rearrange("p (h d) -> p h d", d=32)
                    own.then(pool.tensor_tensor(x3, x3, cos, ALU.mult))
                    pool.tensor_tensor(h_tok[:, b, cols], h_tok[:, b, cols], gate[:, b, cols], ALU.add)\
                        .then_inc(S[done], 1)

            def index_rope(layer):
                pool.wait_ge(S["kv_copied"], 7 * layer + 3)
                if layer == 0:
                    pool.wait_ge(S["rope_loaded"], 16)
                rotary(10, 6, "idx_rope_done")

            def norm_and_rope(layer):
                pool.wait_ge(S["qk_inv_done"], layer + 1)
                pool.wait_ge(S["q_copied"], layer + 1)
                pool.wait_ge(S["kv_copied"], 7 * layer + 5)
                heads = qk[:, :, 0:10, :]
                own.then(pool.tensor_tensor(heads, heads, qk_ss[:, 2, :, :].unsqueeze(3)
                                            .broadcast_to([P, BLOCKS, 10, HD]), ALU.mult))
                gain = par_sb[:, PAR_GAIN:PAR_GAIN + 10 * HD].unsqueeze(1).broadcast_to([P, BLOCKS, 10 * HD])
                part = h_tok[:, :, 0:10 * HD]
                own.then(pool.tensor_tensor(part, part, gain, ALU.mult))
                rotary(0, 10, "rope_done")

            def mixer(layer):
                index_rope(layer)
                if layer == 0:
                    pool.wait_ge(S["powers_done"], 1)
                    make_table(0, 0)
                norm_and_rope(layer)
                if layer == 0:
                    make_table(0, 1)
                for j in range(SCHUNKS):
                    if layer == 0 and j + 2 < SCHUNKS:
                        make_table(0, j + 2)
                    rotate_out(layer, j)
                    if layer == 1 and j + 4 < SCHUNKS:
                        load_table(j + 4)

            load_gain(0, gain_row)
            constants()
            mixer(0)
            pool.wait_ge(S["mixed_done"], 5)
            load_gain(1, gain_ff[:, :])
            pool.memset(zero_r[:, :].bitcast(F32), 0.0).then_inc(S["zero_made"], 1)
            pool.wait_ge(S["x_added"], 2)
            pool.dma_start(par_sb[:, :], par[1]).then_inc(S["par_loaded1"], 16)
            s5_rates(pool, own, 1)
            s5_angles(pool, own, 1)
            s5_powers(pool, own)
            pool.wait_ge(S["powers_done"], 2)
            s5_fold(pool, own, 1)
            for j in range(SCHUNKS):
                store_table(j)
            for j in range(4):
                load_table(j)
            pool.wait_ge(S["x_added"], 4)
            load_gain(2, gain_row)
            mixer(1)
            pool.wait_ge(S["mixed_done"], 10)
            load_gain(3, gain_ff[:, :])
            make_upper()
            pool.dma_start(router_sb[:, :, :], router_w[0].rearrange("(k p) e -> p k e", p=P))\
                .then_inc(S["router_loaded"], 16)
            pool.dma_start(slot_id[:, :, :], slot_ids.rearrange("p (r s) -> p r s", r=2)).then_inc(S["slots_loaded"], 16)


def rope_rows():
    pos = np.arange(SEQ, dtype=np.float32)
    inv = np.float32(10000.0) ** (-np.arange(HD // 2, dtype=np.float32) / np.float32(HD // 2))
    ang = (pos[:, None] * inv[None, :].astype(np.float32)).astype(np.float32)
    t = np.stack([np.cos(ang), -np.sin(ang), np.sin(ang)], 1).astype(np.float32)
    return np.ascontiguousarray(t.reshape(BLOCKS, P, 3, HD // 2).transpose(1, 0, 2, 3))


def small_parameters(i):
    groups = SSM // GROUP
    out = np.zeros((DEPTH, P, PAR_W), np.float32)
    states = lambda a: a.reshape(DEPTH, SCHUNKS, P).transpose(0, 2, 1)
    out[:, :, PAR_LRE:PAR_LRE + SCHUNKS] = states(i["ssm_lam_re"])
    out[:, :, PAR_LIM:PAR_LIM + SCHUNKS] = states(i["ssm_lam_im"])
    out[:, :, PAR_LDT:PAR_LDT + SCHUNKS] = states(np.repeat(i["ssm_log_dt"][:, :, None], STATE, 2))
    out[:, :, PAR_CW:PAR_CW + 3 * CT] = i["conv_w"].reshape(DEPTH, 3 * CT, P).transpose(0, 2, 1)
    out[:, :, PAR_D:PAR_D + CT] = i["ssm_d"].reshape(DEPTH, CT, P).transpose(0, 2, 1)
    gain = np.concatenate([np.tile(i["q_norm_g"], (1, HEADS)), np.tile(i["k_norm_g"], (1, 2))], 1)
    out[:, :, PAR_GAIN:PAR_GAIN + 10 * HD] = gain[:, None, :]
    c_re = out[:, :, PAR_CRE:PAR_CRE + SCHUNKS * 32].reshape(DEPTH, P, SCHUNKS, 32)
    c_im = np.zeros_like(c_re)
    c_re = np.zeros_like(c_re)
    b = np.zeros((DEPTH, P, CT, 2, P), np.float32)
    for g in range(groups):
        j, odd = g // 2, g % 2
        rows = slice(STATE * odd, STATE * odd + STATE)
        cols = slice(GROUP * odd, GROUP * odd + GROUP)
        c_re[:, rows, j, cols] = i["ssm_c_re"][:, g].transpose(0, 2, 1)
        c_im[:, rows, j, cols] = i["ssm_c_im"][:, g].transpose(0, 2, 1)
        at = slice(32 * (j % 4) + GROUP * odd, 32 * (j % 4) + GROUP * odd + GROUP)
        b[:, at, j // 4, 0, rows] = i["ssm_b_re"][:, g].transpose(0, 2, 1)
        b[:, at, j // 4, 1, rows] = i["ssm_b_im"][:, g].transpose(0, 2, 1)
    out[:, :, PAR_CRE:PAR_CRE + SCHUNKS * 32] = c_re.reshape(DEPTH, P, -1)
    out[:, :, PAR_CIM:PAR_CIM + SCHUNKS * 32] = c_im.reshape(DEPTH, P, -1)
    out[:, :, PAR_B:PAR_W] = b.reshape(DEPTH, P, -1)
    return out


def kernel(**inputs):
    import concourse.bacc as bacc
    from concourse.bass_utils import run_bass_kernel_spmd

    i = {name: np.asarray(a) for name, a in inputs.items()}
    slots = np.broadcast_to(np.arange(2 * P, dtype=np.float32), (P, 2 * P))
    arrays = {
        "x": i["x"], "gains": np.stack([i["ln1_g"], i["ln2_g"]], 1).reshape(2 * DEPTH, D), "w_in": i["w_in"],
        "par": small_parameters(i), "w_glu": i["ssm_w_glu"], "w_out_a": i["w_out_a"], "w_out_b": i["w_out_b"],
        "w_out_c": i["w_out_c"], "w_o": i["w_o"], "rope": rope_rows(), "slot_ids": slots, "ffn_w1": i["ffn_w1"],
        "ffn_w3": i["ffn_w3"], "ffn_w2": i["ffn_w2"], "router_w": i["router_w"], "moe_w1": i["moe_w1"],
        "moe_w3": i["moe_w3"], "moe_w2": i["moe_w2"],
    }
    arrays = {name: np.ascontiguousarray(a) for name, a in arrays.items()}
    nc = bacc.Bacc("TRN2", target_bir_lowering=False, num_devices=1)
    args = {name: nc.dram_tensor(name, a.shape, F32, kind="ExternalInput").ap() for name, a in arrays.items()}
    out = nc.dram_tensor("out", (1, SEQ, D), F32, kind="ExternalOutput").ap()
    table_store = nc.dram_tensor("table_store", (SCHUNKS, P, 2 * SEQ), F32, kind="Internal").ap()
    trunk(nc, **args, table_store=table_store, out=out)
    result = run_bass_kernel_spmd(nc, [arrays], core_ids=[0])
    return result.results[0]["out"]
```
